# Optimizing a Trainium2 kernel written in Bass

```python
import jax, jax.numpy as jnp
from jax import lax
import numpy as np

D_MODEL = 1024
BATCH = 1
SEQ = 512
DEPTH = 2

N_GROUPS = 4
MIX_WIDTH = D_MODEL
GROUP_WIDTH = MIX_WIDTH // N_GROUPS
HEAD_DIM = 64
GROUP_HEADS = GROUP_WIDTH // HEAD_DIM
Q_BLOCK = 128
MLA_Q_LORA = 192
MLA_KV_LORA = 128
MLA_NOPE_DIM = 64
MLA_ROPE_DIM = 32
MLA_V_DIM = HEAD_DIM
ROPE_THETA = 10000.0
IDX_HEADS = 4
IDX_DIM = 32
DSA_TOPK = 256
NSA_KV_DIM = HEAD_DIM
CMP_LEN = 32
CMP_STRIDE = 16
SEL_LEN = 64
SEL_TOPN = 16
WINDOW = 512

EPS = 1e-6
NEG_INF = -1e30

kernel_name = "hymba_mla_fox_dsa_nsa_adaln"

SEGMENTS = [
    ("mla_q_lat", MLA_Q_LORA), ("mla_kv_lat", MLA_KV_LORA), ("mla_k_rope", MLA_ROPE_DIM),
    ("fox_q", GROUP_WIDTH), ("fox_k", GROUP_WIDTH), ("fox_v", GROUP_WIDTH), ("fox_f", GROUP_HEADS),
    ("dsa_q", GROUP_WIDTH), ("dsa_k", GROUP_WIDTH), ("dsa_v", GROUP_WIDTH),
    ("idx_q", IDX_HEADS * IDX_DIM), ("idx_k", IDX_DIM), ("idx_w", IDX_HEADS),
    ("nsa_q", GROUP_WIDTH), ("nsa_k_cmp", NSA_KV_DIM), ("nsa_v_cmp", NSA_KV_DIM),
    ("nsa_k_sel", NSA_KV_DIM), ("nsa_v_sel", NSA_KV_DIM), ("nsa_k_win", NSA_KV_DIM),
    ("nsa_v_win", NSA_KV_DIM), ("nsa_gate", GROUP_HEADS * 3),
    ("gate_z", MIX_WIDTH),
]
PROJ_WIDTH = sum(w for _, w in SEGMENTS)

def split_columns(proj):
    out, off = {}, 0
    for name, w in SEGMENTS:
        out[name] = proj[..., off:off + w]
        off += w
    return out

def rms_norm(x, g):
    xf = x.astype(jnp.float32)
    y = xf * lax.rsqrt(jnp.mean(xf * xf, axis=-1, keepdims=True) + EPS)
    return (y * g.astype(jnp.float32)).astype(x.dtype)

def alibi_slopes(n):
    return jnp.asarray(2.0 ** (-8.0 * (np.arange(n) + 1) / n), dtype=jnp.float32)

def masked_softmax(s, mask):
    p = jax.nn.softmax(jnp.where(mask, s, NEG_INF), axis=-1)
    return jnp.where(jnp.any(mask, axis=-1, keepdims=True), p, 0.0)

def merge_blocks(o):
    nb, b, qb, w = o.shape
    return jnp.moveaxis(o, 0, 1).reshape(b, nb * qb, w)

def to_heads(t, n_heads):
    b, s, w = t.shape
    return t.reshape(b, s, n_heads, w // n_heads)

def apply_rope(x, pos):
    half = x.shape[-1] // 2
    inv = ROPE_THETA ** (-jnp.arange(half, dtype=jnp.float32) / half)
    ang = pos.astype(jnp.float32)[:, None] * inv[None, :]
    cos, sin = jnp.cos(ang)[None, :, None, :], jnp.sin(ang)[None, :, None, :]
    xf = x.astype(jnp.float32)
    x1, x2 = xf[..., :half], xf[..., half:]
    return jnp.concatenate([x1 * cos - x2 * sin, x1 * sin + x2 * cos], axis=-1).astype(x.dtype)

def causal_block_attention(q, k, v, scale, bias_fn):
    B, S, H, _ = q.shape
    key_pos = jnp.arange(S)

    def block(i):
        q0 = i * Q_BLOCK
        qb = lax.dynamic_slice_in_dim(q, q0, Q_BLOCK, axis=1)
        t = q0 + jnp.arange(Q_BLOCK)
        s = jnp.einsum('bqhd,bkhd->bhqk', qb, k).astype(jnp.float32) * scale
        if bias_fn is not None:
            s = s + bias_fn(q0)
        p = masked_softmax(s, t[:, None] >= key_pos[None, :])
        o = jnp.einsum('bhqk,bkhd->bqhd', p.astype(v.dtype), v)
        return o.reshape(B, Q_BLOCK, -1)

    return merge_blocks(lax.map(block, jnp.arange(S // Q_BLOCK)))

def mla_mixer(q_lat, kv_lat, k_rope, q_norm, w_uq, kv_norm, w_ukv, pos):
    B, S, _ = q_lat.shape
    q = (rms_norm(q_lat, q_norm) @ w_uq).reshape(B, S, GROUP_HEADS, MLA_NOPE_DIM + MLA_ROPE_DIM)
    kv = (rms_norm(kv_lat, kv_norm) @ w_ukv).reshape(B, S, GROUP_HEADS, MLA_NOPE_DIM + MLA_V_DIM)
    q_nope, q_pe = q[..., :MLA_NOPE_DIM], apply_rope(q[..., MLA_NOPE_DIM:], pos)
    k_nope, v = kv[..., :MLA_NOPE_DIM], kv[..., MLA_NOPE_DIM:]
    k_pe = jnp.broadcast_to(apply_rope(k_rope[:, :, None, :], pos), (B, S, GROUP_HEADS, MLA_ROPE_DIM))
    qf = jnp.concatenate([q_nope, q_pe], axis=-1)
    kf = jnp.concatenate([k_nope, k_pe], axis=-1)
    return causal_block_attention(qf, kf, v, (MLA_NOPE_DIM + MLA_ROPE_DIM) ** -0.5, None)

def fox_mixer(q, k, v, f_logit, b_f):
    log_f = jax.nn.log_sigmoid(f_logit.astype(jnp.float32) + b_f.astype(jnp.float32))
    F = jnp.moveaxis(jnp.cumsum(log_f, axis=1), 2, 1)

    def bias(q0):
        Ft = lax.dynamic_slice_in_dim(F, q0, Q_BLOCK, axis=2)
        return Ft[..., None] - F[:, :, None, :]

    return causal_block_attention(to_heads(q, GROUP_HEADS), to_heads(k, GROUP_HEADS),
                                  to_heads(v, GROUP_HEADS), HEAD_DIM ** -0.5, bias)

def dsa_mixer(q, k, v, q_idx, k_idx, w_idx, slopes):
    B, S, _ = q.shape
    q, k, v = to_heads(q, GROUP_HEADS), to_heads(k, GROUP_HEADS), to_heads(v, GROUP_HEADS)
    q_idx = to_heads(q_idx, IDX_HEADS)
    w_idx = w_idx * (IDX_HEADS ** -0.5)
    topk = min(DSA_TOPK, S // 4)
    key_pos = jnp.arange(S)
    gather = jax.vmap(lambda arr, idx: arr[idx])

    def block(i):
        q0 = i * Q_BLOCK
        t = q0 + jnp.arange(Q_BLOCK)
        qb = lax.dynamic_slice_in_dim(q, q0, Q_BLOCK, axis=1)
        qi = lax.dynamic_slice_in_dim(q_idx, q0, Q_BLOCK, axis=1)
        wi = lax.dynamic_slice_in_dim(w_idx, q0, Q_BLOCK, axis=1)
        idx_score = jnp.einsum('bqh,bqhk->bqk', wi,
                               jax.nn.relu(jnp.einsum('bqhd,bkd->bqhk', qi, k_idx))).astype(jnp.float32)
        idx_score = jnp.where(t[:, None] >= key_pos[None, :], idx_score, NEG_INF)
        _, sel = lax.top_k(idx_score, topk)
        k_sel = gather(k, sel)
        v_sel = gather(v, sel)
        dist = (t[None, :, None] - sel).astype(jnp.float32)[:, None]
        s = jnp.einsum('bqhd,bqkhd->bhqk', qb, k_sel).astype(jnp.float32) * HEAD_DIM ** -0.5
        s = s - slopes[:, None, None] * dist
        p = masked_softmax(s, dist >= 0)
        o = jnp.einsum('bhqk,bqkhd->bqhd', p.astype(v.dtype), v_sel)
        return o.reshape(B, Q_BLOCK, -1)

    return merge_blocks(lax.map(block, jnp.arange(S // Q_BLOCK)))

def nsa_mixer(q, k_cmp, v_cmp, k_sel, v_sel, k_win, v_win, gate_logit, cmp_pos, cmp_w1, cmp_w2, slopes):
    B, S, _ = q.shape
    q = to_heads(q, GROUP_HEADS)
    gates = jax.nn.sigmoid(gate_logit.reshape(B, S, GROUP_HEADS, 3))
    scale = NSA_KV_DIM ** -0.5
    n_cmp = (S - CMP_LEN) // CMP_STRIDE + 1
    cmp_start = jnp.arange(n_cmp) * CMP_STRIDE
    cmp_end = cmp_start + CMP_LEN - 1
    tok = cmp_start[:, None] + jnp.arange(CMP_LEN)[None, :]

    def compress(t_in, pos_emb, w1, w2):
        blk = (t_in[:, tok] + pos_emb).reshape(B, n_cmp, CMP_LEN * NSA_KV_DIM)
        return jax.nn.silu(blk @ w1) @ w2

    kc = compress(k_cmp, cmp_pos[0], cmp_w1[0], cmp_w2[0])
    vc = compress(v_cmp, cmp_pos[1], cmp_w1[1], cmp_w2[1])
    n_sel = S // SEL_LEN
    sel_start = jnp.arange(n_sel) * SEL_LEN
    cmp_to_sel = ((cmp_start[:, None] < sel_start[None, :] + SEL_LEN)
                  & (cmp_end[:, None] >= sel_start[None, :])).astype(jnp.float32)
    top_n = min(SEL_TOPN, n_sel)
    ks_blk = k_sel.reshape(B, n_sel, SEL_LEN, NSA_KV_DIM)
    vs_blk = v_sel.reshape(B, n_sel, SEL_LEN, NSA_KV_DIM)
    kw_pad = jnp.pad(k_win, ((0, 0), (WINDOW, 0), (0, 0)))
    vw_pad = jnp.pad(v_win, ((0, 0), (WINDOW, 0), (0, 0)))
    gather = jax.vmap(lambda arr, idx: arr[idx])
    blk_id = jnp.arange(n_sel)

    def block(i):
        q0 = i * Q_BLOCK
        t = q0 + jnp.arange(Q_BLOCK)
        qb = lax.dynamic_slice_in_dim(q, q0, Q_BLOCK, axis=1)
        s_c = jnp.einsum('bqhd,bnd->bhqn', qb, kc).astype(jnp.float32) * scale
        s_c = s_c - slopes[:, None, None] * (t[:, None] - cmp_end[None, :]).astype(jnp.float32)
        p_c = masked_softmax(s_c, cmp_end[None, :] <= t[:, None])
        o_c = jnp.einsum('bhqn,bnd->bqhd', p_c.astype(vc.dtype), vc)
        imp = jnp.einsum('bhqn,nj->bqj', p_c, cmp_to_sel)
        cur = t // SEL_LEN
        forced = (blk_id[None, :] == cur[:, None]) | (blk_id[None, :] == 0)
        imp = jnp.where(forced, jnp.inf, jnp.where(blk_id[None, :] <= cur[:, None], imp, -jnp.inf))
        _, sel = lax.top_k(imp, top_n)
        ks = gather(ks_blk, sel).reshape(B, Q_BLOCK, top_n * SEL_LEN, NSA_KV_DIM)
        vs = gather(vs_blk, sel).reshape(B, Q_BLOCK, top_n * SEL_LEN, NSA_KV_DIM)
        pos_s = (sel[..., None] * SEL_LEN + jnp.arange(SEL_LEN)).reshape(B, Q_BLOCK, -1)
        dist_s = (t[None, :, None] - pos_s).astype(jnp.float32)[:, None]
        s_s = jnp.einsum('bqhd,bqkd->bhqk', qb, ks).astype(jnp.float32) * scale
        s_s = s_s - slopes[:, None, None] * dist_s
        p_s = masked_softmax(s_s, dist_s >= 0)
        o_s = jnp.einsum('bhqk,bqkd->bqhd', p_s.astype(vs.dtype), vs)
        kw = lax.dynamic_slice_in_dim(kw_pad, q0, WINDOW + Q_BLOCK, axis=1)
        vw = lax.dynamic_slice_in_dim(vw_pad, q0, WINDOW + Q_BLOCK, axis=1)
        pos_w = q0 - WINDOW + jnp.arange(WINDOW + Q_BLOCK)
        dist_w = t[:, None] - pos_w[None, :]
        s_w = jnp.einsum('bqhd,bkd->bhqk', qb, kw).astype(jnp.float32) * scale
        s_w = s_w - slopes[:, None, None] * dist_w.astype(jnp.float32)
        p_w = masked_softmax(s_w, (dist_w >= 0) & (dist_w < WINDOW) & (pos_w[None, :] >= 0))
        o_w = jnp.einsum('bhqk,bkd->bqhd', p_w.astype(vw.dtype), vw)
        g = lax.dynamic_slice_in_dim(gates, q0, Q_BLOCK, axis=1)
        o = g[..., 0:1] * o_c + g[..., 1:2] * o_s + g[..., 2:3] * o_w
        return o.reshape(B, Q_BLOCK, -1)

    return merge_blocks(lax.map(block, jnp.arange(S // Q_BLOCK)))

def hybrid_layer(x, c, rms_g, w_ada, b_ada, w_in, mla_q_norm, mla_w_uq, mla_kv_norm, mla_w_ukv,
                 fox_b_f, nsa_cmp_pos, nsa_cmp_w1, nsa_cmp_w2, out_norm_g, w_out, slopes):
    B, S, _ = x.shape
    pos = jnp.arange(S)
    mod = jax.nn.silu(c) @ w_ada + b_ada
    shift, scale, gate = jnp.split(mod[:, None, :], 3, axis=-1)
    h = rms_norm(x, rms_g) * (1.0 + scale) + shift
    p = split_columns(h @ w_in)
    o_a = mla_mixer(p["mla_q_lat"], p["mla_kv_lat"], p["mla_k_rope"],
                    mla_q_norm, mla_w_uq, mla_kv_norm, mla_w_ukv, pos)
    o_b = fox_mixer(p["fox_q"], p["fox_k"], p["fox_v"], p["fox_f"], fox_b_f)
    o_c = dsa_mixer(p["dsa_q"], p["dsa_k"], p["dsa_v"], p["idx_q"], p["idx_k"], p["idx_w"], slopes)
    o_d = nsa_mixer(p["nsa_q"], p["nsa_k_cmp"], p["nsa_v_cmp"], p["nsa_k_sel"], p["nsa_v_sel"],
                    p["nsa_k_win"], p["nsa_v_win"], p["nsa_gate"],
                    nsa_cmp_pos, nsa_cmp_w1, nsa_cmp_w2, slopes)
    o = jnp.concatenate([o_a, o_b, o_c, o_d], axis=-1).reshape(B, S, N_GROUPS, GROUP_WIDTH)
    o = rms_norm(o, out_norm_g.reshape(N_GROUPS, GROUP_WIDTH)).reshape(B, S, MIX_WIDTH)
    o = o * jax.nn.silu(p["gate_z"])
    return x + gate * (o @ w_out)

def setup_inputs(seed: int = 0) -> dict:
    key = jax.random.key(seed)
    ks = jax.random.split(key, 20)
    f32 = jnp.float32
    nrm = lambda k, shape, s: jax.random.normal(k, shape, f32) * s
    D = D_MODEL
    return {
        "x": nrm(ks[0], (BATCH, SEQ, D), 1.0),
        "c": nrm(ks[1], (BATCH, D), 1.0),
        "rms_g": 1.0 + nrm(ks[2], (DEPTH, D), 0.05),
        "w_ada": nrm(ks[3], (DEPTH, D, 3 * D), 0.5 * D ** -0.5),
        "b_ada": nrm(ks[4], (DEPTH, 3 * D), 0.01),
        "w_in": nrm(ks[5], (DEPTH, D, PROJ_WIDTH), D ** -0.5),
        "mla_q_norm": 1.0 + nrm(ks[6], (DEPTH, MLA_Q_LORA), 0.05),
        "mla_w_uq": nrm(ks[7], (DEPTH, MLA_Q_LORA, GROUP_HEADS * (MLA_NOPE_DIM + MLA_ROPE_DIM)), MLA_Q_LORA ** -0.5),
        "mla_kv_norm": 1.0 + nrm(ks[8], (DEPTH, MLA_KV_LORA), 0.05),
        "mla_w_ukv": nrm(ks[9], (DEPTH, MLA_KV_LORA, GROUP_HEADS * (MLA_NOPE_DIM + MLA_V_DIM)), MLA_KV_LORA ** -0.5),
        "fox_b_f": 3.0 + nrm(ks[10], (DEPTH, GROUP_HEADS), 0.5),
        "nsa_cmp_pos": nrm(ks[11], (DEPTH, 2, CMP_LEN, NSA_KV_DIM), 0.1),
        "nsa_cmp_w1": nrm(ks[12], (DEPTH, 2, CMP_LEN * NSA_KV_DIM, NSA_KV_DIM), (CMP_LEN * NSA_KV_DIM) ** -0.5),
        "nsa_cmp_w2": nrm(ks[13], (DEPTH, 2, NSA_KV_DIM, NSA_KV_DIM), NSA_KV_DIM ** -0.5),
        "out_norm_g": 1.0 + nrm(ks[14], (DEPTH, MIX_WIDTH), 0.05),
        "w_out": nrm(ks[15], (DEPTH, MIX_WIDTH, D), MIX_WIDTH ** -0.5),
        "final_g": 1.0 + nrm(ks[16], (D,), 0.05),
    }

def reference(x, c, rms_g, w_ada, b_ada, w_in, mla_q_norm, mla_w_uq, mla_kv_norm, mla_w_ukv,
              fox_b_f, nsa_cmp_pos, nsa_cmp_w1, nsa_cmp_w2, out_norm_g, w_out, final_g):
    slopes = alibi_slopes(GROUP_HEADS)
    for l in range(DEPTH):
        x = hybrid_layer(x, c, rms_g[l], w_ada[l], b_ada[l], w_in[l], mla_q_norm[l], mla_w_uq[l],
                         mla_kv_norm[l], mla_w_ukv[l], fox_b_f[l], nsa_cmp_pos[l], nsa_cmp_w1[l],
                         nsa_cmp_w2[l], out_norm_g[l], w_out[l], slopes)
    return rms_norm(x, final_g)


_drawn_inputs = setup_inputs


def setup_inputs(seed=0):
    import zlib

    import numpy as np

    out = dict(_drawn_inputs(seed))
    spreads = {}
    factors = {'b_ada': 2.789,
     'mla_q_norm': 8.0,
     'mla_kv_norm': 5.253,
     'fox_b_f': 11.797,
     'nsa_cmp_pos': 4.664,
     'out_norm_g': 3.214}
    for name, (base, spread) in spreads.items():
        noise = np.random.default_rng([zlib.crc32(name.encode()), seed]).standard_normal(out[name].shape)
        drawn = base * np.exp(spread * noise) if base else spread * noise
        out[name] = __import__('jax').numpy.asarray(drawn.astype(out[name].dtype))
    for name, factor in factors.items():
        out[name] = (out[name] * factor).astype(out[name].dtype)
    return out
```

```python
from contextlib import ExitStack

import numpy as np
import concourse.bass as bass
from concourse import mybir

F32 = mybir.dt.float32
BF16 = mybir.dt.bfloat16
ALU = mybir.AluOpType
ACT = mybir.ActivationFunctionType
AX_X = mybir.AxisListType.X

P = 128
D, SEQ, DEPTH = 1024, 512, 2
KD = D // P
NB = SEQ // P
H, HD = 4, 64
GW = H * HD
Q_LORA, KV_LORA, ROPE = 192, 128, 32
QK_W = HD + ROPE
TOPK = min(256, SEQ // 4)
CMP_LEN, CMP_STRIDE = 32, 16
N_CMP = (SEQ - CMP_LEN) // CMP_STRIDE + 1
NCP = 32
CMP_J = CMP_LEN // 2
EPS = 1e-6
MASKED = -1e30
TAKEN = -3e38
LOWEST = -2e38

RING = 3
SLOT = KD * 256
N_ADA, N_OUT = 12, 4
A1_W = Q_LORA + 32 + 4 + 4 + 12
A2_W = KV_LORA + ROPE
IN_W = [A1_W, A2_W] + [256] * 3
IN2_W = [256] * 10
U_A1, U_A2, U_IQ, U_FQ, U_FK, U_MLA, U_CMP = range(N_ADA, N_ADA + 7)
U_DQ, U_DK, U_NQ, U_SW, U_FV, U_DV, U_GZ = range(U_CMP + 1, U_CMP + 8)
U_OUT = U_GZ + 4
NU = U_OUT + N_OUT
MLA_W = 2 * H * QK_W + 2 * GW
CMPW_W = 2 * CMP_J * HD
UNIT_W = ([SLOT] * N_ADA + [KD * w for w in IN_W] + [MLA_W, CMPW_W]
          + [KD * w for w in IN2_W] + [SLOT] * N_OUT)
UNIT_AT = [sum(UNIT_W[:u]) for u in range(NU + 1)]
assert len(UNIT_W) == NU and NU % RING == 0

C_QL, C_IK, C_IW, C_FF, C_NG, C_KVL, C_KR = 0, 192, 224, 228, 232, 244, 372
TM_W = A1_W + A2_W

PR = {}
_at = 0
for _n, _w in (("rms_g", KD), ("b_ada", 3 * KD), ("out_g", KD), ("q_g", 2), ("kv_g", 1), ("b_f", H),
               ("pos", 2 * CMP_J), ("w2k", 2 * HD), ("w2v", HD)):
    PR[_n] = (_at, _at + _w)
    _at += _w
PR_W = _at

CO = {}
_at = 0
for _n, _w in (("ident", P), ("alibi", H * SEQ), ("mask", SEQ), ("cmpb", NB * H * NCP), ("cos", NB * 16),
               ("sin", NB * 16), ("mean", P), ("selrow", H * P), ("ones", SEQ), ("late", 1), ("eps", 1)):
    CO[_n] = (_at, _at + _w)
    _at += _w
CO_W = _at

MIXERS = ["mla", "fox", "sel", "win", "dsa"]
UNITS = [(m, i, h) for m in MIXERS for i in range(NB) for h in range(H)]
NUN = len(UNITS)
OUT_COL = {"mla": 0, "fox": GW, "dsa": 2 * GW, "sel": 3 * GW, "win": 3 * GW}
CMP_T_AT, CMP_V0_AT, CMP_V1_AT = 8, 12, 16


def program(nc, x_t, c_t, w_all, par, const, fin_g, y_t):
    with ExitStack() as ctx:
        def sb(name, shape, dt=F32):
            return ctx.enter_context(nc.sbuf_tensor(name, shape, dt))

        def sem(name):
            return ctx.enter_context(nc.semaphore(name))

        xT = sb("xT", [P, KD, SEQ])
        hT = sb("hT", [P, KD, SEQ])
        ring = sb("ring", [P, RING, SLOT])
        o_sb = sb("o_sb", [P, NB, D])
        sz = sb("sz", [P, NB, D])
        tm = sb("tm", [P, NB, TM_W])
        fq, fk = sb("fq", [P, 2, SEQ]), sb("fk", [P, 2, SEQ])
        dq, dk = sb("dq", [P, 2, SEQ]), sb("dk", [P, 2, SEQ])
        nq = sb("nq", [P, 2, SEQ])
        iq = sb("iq", [P, SEQ])
        cmp2 = sb("cmp2", [P, 2, SEQ])
        blk = sb("blk", [P, 2, CMP_J, N_CMP])
        ks2, kw2 = sb("ks2", [P, SEQ]), sb("kw2", [P, SEQ])
        mq, mk = sb("mq", [P, H, SEQ]), sb("mk", [P, H, SEQ])
        v_tm = sb("v_tm", [P, NB, GW])
        fv, dv = sb("fv", [P, NB, GW]), sb("dv", [P, NB, GW])
        nv = sb("nv", [P, NB, 2 * HD])
        fb = sb("fb", [P, H, SEQ])
        cst = sb("cst", [P, CO_W])
        prm = sb("prm", [P, PR_W])
        fing = sb("fing", [P, KD])
        cT, sc = sb("cT", [P, KD]), sb("sc", [P, KD])
        mod, gs = sb("mod", [P, 3 * KD]), sb("gs", [P, KD])
        rb = sb("rb", [P, SEQ])
        identb, maskb = sb("identb", [P, P], BF16), sb("maskb", [P, P], BF16)
        work = [None] + [sb(f"work{i}", [P, P * (i + 1)]) for i in range(1, NB)]
        selm = [None] + [sb(f"selm{i}", [P, P * (i + 1)], BF16) for i in range(1, NB)]
        top8 = sb("top8", [P, NB, 8])
        lss, llr = sb("lss", [P, 2, NB]), sb("llr", [P, 2, NB])
        junk = sb("junk", [P, GW])
        fy, fa, fe, fl, fls = (sb(n, [P, NB, H]) for n in ("fy", "fa", "fe", "fl", "fls"))
        fcum = sb("fcum", [H, SEQ])
        ge, gd, gsig = (sb(n, [P, NB, H, 3]) for n in ("ge", "gd", "gsig"))
        hidk, hidv = sb("hidk", [HD, NCP]), sb("hidv", [HD, H, NCP])
        kc2, vcd = sb("kc2", [P, NCP]), sb("vcd", [P, H, HD])
        pc = sb("pc", [P, NB, H, NCP])
        pct = sb("pct", [P, NB, P])
        cmx, cden, crec, cfac = (sb(n, [P, NB, H]) for n in ("cmx", "cden", "crec", "cfac"))
        nmx, rsum = sb("nmx", [P, NUN]), sb("rsum", [P, NUN])
        rinv, rfac = sb("rinv", [P, NUN]), sb("rfac", [P, NUN])
        otmp = sb("otmp", [P, GW])
        gss, gln, grs = (sb(n, [P, NB, H]) for n in ("gss", "gln", "grs"))
        ps = ctx.enter_context(nc.psum_tensor("ps", [P, 8, 512], F32))

        flat_h = hT[:, :, :].rearrange("p k t -> p (k t)")
        sm = [flat_h[:, 512 * n:512 * n + 512] for n in range(3)]
        pr_ = [flat_h[:, 512 * (3 + n):512 * (3 + n) + 512] for n in range(3)]
        pt = [flat_h[:, 512 * (6 + n):512 * (6 + n) + 512] for n in range(2)]
        flat_o = o_sb[:, :, :].rearrange("p i d -> p (i d)")
        q_tm = flat_o[:, 0:NB * H * QK_W].rearrange("p (i h e) -> p i h e", i=NB, h=H)
        k_tm = flat_o[:, NB * H * QK_W:2 * NB * H * QK_W].rearrange("p (i h e) -> p i h e", i=NB, h=H)
        rt = [flat_o[:, 3072 + 256 * n:3072 + 256 * n + 256].rearrange("p (i h e) -> p i h e", i=NB, h=H)
              for n in range(4)]
        flat_s = sz[:, :, :].rearrange("p i d -> p (i d)")
        qn = flat_s[:, 0:768].rearrange("p (i c) -> p i c", i=NB)
        kn = flat_s[:, 768:1280].rearrange("p (i c) -> p i c", i=NB)
        qlT = [flat_s[:, 1280:1792], flat_s[:, 1792:2304]]
        klT = flat_s[:, 2304:2816]
        ikd = flat_s[:, 2816:3328].rearrange("p (i g c) -> p i g c", i=NB, g=H)
        ikT = flat_s[:, 3328:3840]
        rl = fb
        lnv = work[NB - 1]

        def con(name):
            return cst[:, CO[name][0]:CO[name][1]]

        def par_(name):
            return prm[:, PR[name][0]:PR[name][1]]

        ident = con("ident")
        alibi = con("alibi").rearrange("p (h t) -> p h t", h=H)
        cosv = con("cos").rearrange("p (i e) -> p i e", i=NB).unsqueeze(2)
        sinv = con("sin").rearrange("p (i e) -> p i e", i=NB).unsqueeze(2)
        selrow = con("selrow").rearrange("p (h c) -> p h c", h=H)
        late, eps = con("late"), con("eps")

        w_loaded = [sem(f"w_loaded{n}") for n in range(RING)]
        w_used = sem("w_used")
        par_loaded = sem("par_loaded")
        first_loaded = sem("first_loaded")
        setup_act, setup_dve = sem("setup_act"), sem("setup_dve")
        fin_act, fin_pe, fin_dve, y_stored = sem("fin_act"), sem("fin_pe"), sem("fin_dve"), sem("y_stored")
        go = sem("go")

        layer_sems = []

        def lsem(name):
            layer_sems.append(sem(name))
            return layer_sems[-1]

        arrived = lsem("arrived")
        s_sq, s_ssum, s_rb = lsem("s_sq"), lsem("s_ssum"), lsem("s_rb")
        s_mod, s_h0, s_h = lsem("s_mod"), lsem("s_h0"), lsem("s_h")
        s_proj, s_evac = lsem("s_proj"), lsem("s_evac")
        s_ikd, s_ikp, s_ikT = lsem("s_ikd"), lsem("s_ikp"), lsem("s_ikT")
        s_idx, s_relu, s_isc = lsem("s_idx"), lsem("s_relu"), lsem("s_isc")
        s_top, s_selm = lsem("s_top"), lsem("s_selm")
        s_lss, s_llr, s_lat, s_latp, s_latT = (lsem(n) for n in ("s_lss", "s_llr", "s_lat", "s_latp", "s_latT"))
        s_uq, s_uqe, s_ukv, s_ukve = lsem("s_uq"), lsem("s_uqe"), lsem("s_ukv"), lsem("s_ukve")
        s_rope = lsem("s_rope")
        s_mqp, s_mq, s_mkp, s_mk = lsem("s_mqp"), lsem("s_mq"), lsem("s_mkp"), lsem("s_mk")
        s_fa, s_fl, s_fls, s_flp, s_fcum = (lsem(n) for n in ("s_fa", "s_fl", "s_fls", "s_flp", "s_fcum"))
        s_fbp, s_fb = lsem("s_fbp"), lsem("s_fb")
        s_gd, s_ge, s_gsig = lsem("s_gd"), lsem("s_ge"), lsem("s_gsig")
        s_blk, s_hidp, s_hid, s_kcp, s_kc = (lsem(n) for n in ("s_blk", "s_hidp", "s_hid", "s_kcp", "s_kc"))
        s_cs, s_csub, s_cexp, s_pc = lsem("s_cs"), lsem("s_csub"), lsem("s_cexp"), lsem("s_pc")
        s_pctp, s_pct, s_cpv, s_co = lsem("s_pctp"), lsem("s_pct"), lsem("s_cpv"), lsem("s_co")
        s_sc, s_ttr, s_exp, s_tr = lsem("s_sc"), lsem("s_ttr"), lsem("s_exp"), lsem("s_tr")
        s_pta, s_ptd, s_pv, s_norm = lsem("s_pta"), lsem("s_ptd"), lsem("s_pv"), lsem("s_norm")
        s_gss, s_grs, s_y, s_yp, s_oT = (lsem(n) for n in ("s_gss", "s_grs", "s_y", "s_yp", "s_oT"))
        s_out, s_x = lsem("s_out"), lsem("s_x")
        d_link, a_link, g_link = lsem("d_link"), lsem("a_link"), lsem("g_link")

        def linker(eng, s):
            count = [0]

            def link(ins):
                count[0] += 1
                ins.then_inc(s, 1)
                eng.wait_ge(s, count[0])
            return link

        def weights(u, n):
            return ring[:, u % RING, 0:n]

        def wait_weights(pe, layer, u):
            pe.wait_ge(w_loaded[u % RING], layer * (16 * (NU // RING)) + 16 * (u // RING + 1))

        steps = []
        for u in (U_A1, U_A2):
            steps += [(u, i) for i in range(NB)]
        for u in (U_IQ, U_FQ, U_FK, U_DQ, U_DK, U_NQ):
            steps += [(u, 0), (u, 1)]
        steps += [(U_SW, 0)] + [(U_SW, 1 + i) for i in range(NB)]
        for u in (U_FV, U_DV, U_GZ, U_GZ + 1, U_GZ + 2, U_GZ + 3):
            steps += [(u, i) for i in range(NB)]
        step_no = {s: n for n, s in enumerate(steps)}
        last_step = {u: n for n, (u, _) in enumerate(steps)}

        def unit_steps(u):
            return [("proj", s) for s in steps if s[0] == u]

        SCHED = (unit_steps(U_A1) + [("latr", 0)] + unit_steps(U_A2) + [("latr", 1)] + unit_steps(U_IQ) + [("ik", 0)]
                 + [("proj", (U_FQ, 0)), ("idx", 1), ("proj", (U_FQ, 1)), ("foxT", 0), ("proj", (U_FK, 0)),
                    ("idx", 2), ("proj", (U_FK, 1)), ("idx", 3), ("lat", 0), ("uq", 0), ("ukv", 0)]
                 + [("hid", 0)] + unit_steps(U_DQ) + [("kc", 0)] + unit_steps(U_DK) + [("mq", 0)]
                 + unit_steps(U_NQ) + [("mk", 0)] + unit_steps(U_SW) + [("fb", 0)] + unit_steps(U_FV)
                 + [("cs", 0)] + unit_steps(U_DV) + unit_steps(U_GZ) + unit_steps(U_GZ + 1)
                 + unit_steps(U_GZ + 2) + unit_steps(U_GZ + 3))
        SCHED.remove(("latr", 0))

        block = ctx.enter_context(nc.Block())

        @block.sync
        def _(sp):
            sp.dma_start(cT[:], c_t).then_inc(first_loaded, 16)
            sp.dma_start(xT[:], x_t).then_inc(first_loaded, 16)
            sp.dma_start(prm[:], par[0]).then_inc(par_loaded, 16)

            def load(layer, u):
                n = UNIT_W[u]
                sp.dma_start(ring[:, u % RING, 0:n], w_all[layer, :, UNIT_AT[u]:UNIT_AT[u] + n]).then_inc(
                    w_loaded[u % RING], 16)

            for layer in range(DEPTH):
                for u in range(NU):
                    if layer or u >= RING:
                        sp.wait_ge(w_used, layer * NU + u - RING + 1)
                    load(layer, u)
                    if layer == 0 and u == RING - 1:
                        sp.dma_start(cst[:], const).then_inc(first_loaded, 16)
                        sp.dma_start(fing[:], fin_g).then_inc(first_loaded, 16)
                if layer + 1 < DEPTH:
                    sp.wait_ge(go, layer + 1)
                    sp.dma_start(prm[:], par[layer + 1]).then_inc(par_loaded, 16)
            for k in range(KD):
                sp.wait_ge(fin_dve, k + 1)
                sp.dma_start(y_t[:, k, :], xT[:, k, :]).then_inc(y_stored, 16)
            sp.wait_ge(y_stored, 16 * KD)

        @block.tensor
        def _(pe):
            mm, tp = nc.tensor.matmul, nc.tensor.transpose

            def proj(layer, s):
                u, i = s
                n = step_no[s]
                if last_step[u] - n == sum(1 for t in steps if t[0] == u) - 1:
                    wait_weights(pe, layer, u)
                if n == 0:
                    pe.wait_ge(s_h, KD)
                if n >= 4:
                    pe.wait_ge(s_evac, n - 3)
                bank = ps[:, n % 4, :]
                width = UNIT_W[u] // KD
                w = weights(u, KD * width).rearrange("p (k c) -> p k c", k=KD)
                for k in range(KD):
                    if u in (U_IQ, U_FQ, U_FK, U_DQ, U_DK, U_NQ) or s == (U_SW, 0):
                        last = mm(bank, w[:, k, P * i:P * i + P], hT[:, k, :], start=k == 0, stop=k == KD - 1)
                    else:
                        j = i - 1 if u == U_SW else i
                        wk = w[:, k, P:] if u == U_SW else w[:, k, :]
                        last = mm(bank[:, 0:wk.shape[-1]], hT[:, k, P * j:P * j + P], wk,
                                  start=k == 0, stop=k == KD - 1)
                if n == last_step[u]:
                    last.then_inc(w_used, 1)
                else:
                    last.then_inc(s_proj, 1)

            def ik(layer):
                pe.wait_ge(s_ikd, 1)
                for i in range(NB):
                    last = tp(ps[:, 4, P * i:P * i + P], ikd[:, i].rearrange("p g c -> p (g c)"), ident)
                last.then_inc(s_ikp, 1)

            def idx(layer, i):
                if i == 1:
                    pe.wait_ge(s_ikT, 1)
                    pe.wait_ge(s_evac, step_no[U_IQ, 0] + 1)
                elif i == 2:
                    pe.wait_ge(s_fcum, 1)
                else:
                    pe.wait_ge(s_relu, i - 1)
                for h in range(H):
                    r = slice(32 * h, 32 * h + 32)
                    last = mm(ps[:, 4 + h, 0:P * (i + 1)], iq[r, P * i:P * i + P], ikT[r, 0:P * (i + 1)],
                              start=True, stop=True)
                last.then_inc(s_idx, 1)

            def foxT(layer):
                pe.wait_ge(s_fls, 1)
                pe.wait_ge(s_relu, 1)
                for i in range(NB):
                    last = tp(ps[0:H, 4, P * i:P * i + P], fls[:, i, :], ident)
                last.then_inc(s_flp, 1)

            def lat(layer):
                pe.wait_ge(s_lat, 1)
                pe.wait_ge(s_relu, 3)
                for i in range(NB):
                    tp(ps[:, 4, P * i:P * i + P], qn[:, i, 0:P], ident)
                    tp(ps[0:Q_LORA - P, 5, P * i:P * i + P], qn[:, i, P:Q_LORA], ident)
                    last = tp(ps[:, 6, P * i:P * i + P], kn[:, i, :], ident)
                last.then_inc(s_latp, 1)

            def uq(layer):
                wait_weights(pe, layer, U_MLA)
                pe.wait_ge(s_latT, 3)
                w = weights(U_MLA, MLA_W)
                for i in range(NB):
                    mm(ps[:, 4 + i, 0:H * QK_W], qlT[0][:, P * i:P * i + P], w[:, 0:H * QK_W], start=True, stop=False)
                    last = mm(ps[:, 4 + i, 0:H * QK_W], qlT[1][0:64, P * i:P * i + P], w[0:64, H * QK_W:2 * H * QK_W],
                              start=False, stop=True)
                    last.then_inc(s_uq, 1)

            def ukv(layer):
                w = weights(U_MLA, MLA_W)
                for i in range(NB):
                    pe.wait_ge(s_uqe, i + 1)
                    last = mm(ps[:, 4 + i, :], klT[:, P * i:P * i + P], w[:, 2 * H * QK_W:MLA_W], start=True, stop=True)
                    if i < NB - 1:
                        last.then_inc(s_ukv, 1)
                last.then_inc(w_used, 1)

            def hid(layer):
                wait_weights(pe, layer, U_CMP)
                pe.wait_ge(s_blk, 2)
                pe.wait_ge(s_ukve, 1)
                w = weights(U_CMP, CMPW_W).rearrange("p (s j c) -> p s j c", s=2, j=CMP_J)
                for s in range(2):
                    for j in range(CMP_J):
                        last = mm(ps[0:HD, 4, 64 * s:64 * s + N_CMP], w[:, s, j, :], blk[:, s, j, :],
                                  start=j == 0, stop=j == CMP_J - 1)
                last.then_inc(w_used, 1)

            def kc(layer):
                pe.wait_ge(s_hid, 2)
                pe.wait_ge(s_ukve, 3)
                mm(ps[:, 5, 0:N_CMP], par_("w2k")[0:HD, :], hidk[:, 0:N_CMP], start=True, stop=True)
                mm(ps[:, 6, 0:HD], hidv[:, :, :].rearrange("p g n -> p (g n)"), par_("w2v")[0:HD, :],
                   start=True, stop=True).then_inc(s_kcp, 1)

            def mqT(layer):
                pe.wait_ge(s_rope, 1)
                pe.wait_ge(s_kc, 2)
                pe.wait_ge(s_ukve, NB)
                for h in range(H):
                    for i in range(NB):
                        last = tp(ps[0:QK_W, 4 + h, P * i:P * i + P], q_tm[:, i, h, :], ident)
                    last.then_inc(s_mqp, 1)

            def mkT(layer):
                pe.wait_ge(s_rope, 2)
                for h in range(H):
                    pe.wait_ge(s_mq, h + 1)
                    for i in range(NB):
                        last = tp(ps[0:QK_W, 4 + h, P * i:P * i + P], k_tm[:, i, h, :], ident)
                    last.then_inc(s_mkp, 1)

            def fbT(layer):
                for h in range(H):
                    pe.wait_ge(s_mk, h + 1)
                    mm(ps[:, 4 + h, :], selrow[0:H, h, :], fcum[:, :], start=True, stop=True).then_inc(s_fbp, 1)

            def cs(layer):
                pe.wait_ge(s_fb, 2)
                pe.wait_ge(s_evac, last_step[U_NQ] + 1)
                for i in range(NB):
                    for h in range(H):
                        r = slice(64 * (h % 2), 64 * (h % 2) + 64)
                        c = (i * 2 + h // 2) * NCP
                        last = mm(ps[:, 4 + h % 2, c:c + N_CMP], nq[r, h // 2, P * i:P * i + P], kc2[r, 0:N_CMP],
                                  start=True, stop=True)
                last.then_inc(s_cs, 1)

            stages = {"ik": ik, "foxT": foxT, "lat": lat, "uq": uq, "ukv": ukv, "hid": hid, "kc": kc,
                      "mq": mqT, "mk": mkT, "fb": fbT, "cs": cs}

            def scores(u):
                m, i, h = UNITS[u]
                n, w = u % 3, P * (i + 1)
                q = slice(P * i, P * i + P)
                r = slice(64 * (h % 2), 64 * (h % 2) + 64)
                lhs, rhs = {"mla": (mq[0:QK_W, h, q], mk[0:QK_W, h, 0:w]),
                            "fox": (fq[r, h // 2, q], fk[r, h // 2, 0:w]),
                            "dsa": (dq[r, h // 2, q], dk[r, h // 2, 0:w]),
                            "sel": (nq[r, h // 2, q], ks2[r, 0:w]),
                            "win": (nq[r, h // 2, q], kw2[r, 0:w])}[m]
                if u >= 3:
                    pe.wait_ge(s_ttr, u - 2)
                if m == "dsa" and i > 0:
                    pe.wait_ge(s_selm, i)
                masked = m == "fox" or (m == "dsa" and i > 0)
                last = mm(ps[:, n, 0:w], lhs, rhs, start=True, stop=not masked)
                if m == "fox":
                    last = mm(ps[:, n, w - P:w], identb[:, :], maskb[:, :], start=False, stop=True)
                elif masked:
                    last = mm(ps[:, n, 0:w], identb[:, :], selm[i][:, :], start=False, stop=True)
                last.then_inc(s_sc, 1)

            def turn(u):
                _, i, _ = UNITS[u]
                pe.wait_ge(s_exp, u + 1)
                if u >= 2:
                    pe.wait_ge(s_pta if u % 2 == 0 else s_ptd, u // 2)
                for j in range(i + 1):
                    last = tp(ps[:, 3 + u % 2, P * j:P * j + P], pr_[u % 3][:, P * j:P * j + P], ident)
                last.then_inc(s_tr, 1)

            def values(u):
                m, i, h = UNITS[u]
                g = u // H
                pe.wait_ge(s_pta if u % 2 == 0 else s_ptd, u // 2 + 1)
                if h == 0 and g >= 2:
                    pe.wait_ge(s_norm, g - 1)
                for j in range(i + 1):
                    v = {"mla": v_tm[:, j, HD * h:HD * h + HD], "fox": fv[:, j, HD * h:HD * h + HD],
                         "dsa": dv[:, j, HD * h:HD * h + HD], "sel": nv[:, j, 0:HD], "win": nv[:, j, HD:2 * HD]}[m]
                    last = mm(ps[:, 5 + g % 2, HD * h:HD * h + HD], pt[u % 2][:, P * j:P * j + P], v,
                              start=j == 0, stop=j == i)
                last.then_inc(s_pv, 1)

            def cmp_turn():
                pe.wait_ge(s_pc, 1)
                for i in range(NB):
                    last = tp(ps[:, 7, P * i:P * i + P], pc[:, i].rearrange("p h n -> p (h n)"), ident)
                last.then_inc(s_pctp, 1)

            def cmp_values(half):
                pe.wait_ge(s_pct, 1) if half == 0 else pe.wait_ge(s_co, 1)
                for i in (2 * half, 2 * half + 1):
                    c = (i % 2) * GW
                    last = mm(ps[:, 7, c:c + GW], pct[:, i, :], vcd[:, :, :].rearrange("p h e -> p (h e)"),
                              start=True, stop=True)
                last.then_inc(s_cpv, 1)

            def mean_square(src, s):
                for k in range(KD):
                    last = mm(ps[:, 6, :], con("mean"), src[:, k, :], start=k == 0, stop=k == KD - 1)
                last.then_inc(s, 1)

            sq = flat_o.rearrange("p (k t) -> p k t", k=KD)
            pe.wait_ge(first_loaded, 64)
            pe.wait_ge(setup_dve, 4)
            pe.wait_ge(setup_act, 1)
            with pe.Fori(0, DEPTH) as layer:
                pe.wait_ge(s_sq, 1)
                mean_square(sq, s_ssum)
                for u in range(N_ADA):
                    wait_weights(pe, layer, u)
                    w = weights(u, SLOT).rearrange("p (k c) -> p k c", k=KD)
                    for m in range(2):
                        for k in range(KD):
                            last = mm(ps[:, 7, 2 * u + m:2 * u + m + 1], w[:, k, P * m:P * m + P], sc[:, k:k + 1],
                                      start=k == 0, stop=k == KD - 1)
                    last.then_inc(w_used, 1)
                for kind, a in SCHED:
                    if kind == "proj":
                        proj(layer, a)
                    elif kind == "idx":
                        idx(layer, a)
                    elif kind in stages:
                        stages[kind](layer)
                pe.wait_ge(s_evac, len(steps))
                pe.wait_ge(s_fb, H)
                for t in range(NUN + 3):
                    if t < NUN:
                        scores(t)
                    if 2 <= t < NUN + 2:
                        turn(t - 2)
                    if t >= 3:
                        values(t - 3)
                    if t == CMP_T_AT:
                        cmp_turn()
                    if t == CMP_V0_AT:
                        cmp_values(0)
                    if t == CMP_V1_AT:
                        cmp_values(1)
                pe.wait_ge(s_norm, NUN // H)
                for k in range(KD):
                    pe.wait_ge(s_y, 2 * NB)
                    if k >= 4:
                        pe.wait_ge(s_oT, k - 3)
                    for i in range(NB):
                        last = tp(ps[:, k % 4, P * i:P * i + P], o_sb[:, i, P * k:P * k + P], ident)
                    last.then_inc(s_yp, 1)
                pe.wait_ge(s_oT, KD)
                for k in range(KD):
                    u = U_OUT + k // 2
                    if k % 2 == 0:
                        wait_weights(pe, layer, u)
                    if k >= 4:
                        pe.wait_ge(s_x, k - 3)
                    w = weights(u, SLOT).rearrange("p (k c) -> p k c", k=KD)
                    for kk in range(KD):
                        last = mm(ps[:, k % 4, :], w[:, kk, P * (k % 2):P * (k % 2) + P], hT[:, kk, :],
                                  start=kk == 0, stop=kk == KD - 1)
                    last.then_inc(w_used if k % 2 else s_out, 1)
                pe.wait_ge(s_x, KD)
                pe.sem_inc(arrived, 1)
                pe.wait_ge(go, layer + 1)
            pe.wait_ge(fin_act, 1)
            mean_square(sq, fin_pe)

        @block.scalar
        def _(act):
            a = nc.scalar.activation
            count = [0]

            def copied(ins):
                ins.then_inc(s_evac, 1)

            def wait_step(layer, s):
                u, _ = s
                n = step_no[s]
                if n == last_step[u]:
                    act.wait_ge(w_used, layer * NU + u + 1)
                else:
                    act.wait_ge(s_proj, n + 1 - sum(1 for v in last_step if last_step[v] < n))

            def proj(layer, s):
                u, i = s
                wait_step(layer, s)
                bank = ps[:, step_no[s] % 4, :]
                cp = nc.scalar.copy
                lo, hi = slice(0, 64), slice(64, P)
                if u == U_A1:
                    copied(cp(tm[:, i, 0:A1_W], bank[:, 0:A1_W]))
                elif u == U_A2:
                    copied(cp(tm[:, i, A1_W:TM_W], bank[:, 0:A2_W]))
                elif s == (U_IQ, 0):
                    copied(cp(iq[:, :], bank))
                elif s == (U_IQ, 1):
                    cp(cmp2[lo, 0, :], bank[lo, :])
                    cp(cmp2[hi, 0, 0:SEQ - 1], bank[lo, 1:SEQ])
                    cp(cmp2[lo, 1, :], bank[hi, :])
                    copied(cp(cmp2[hi, 1, 0:SEQ - 1], bank[hi, 1:SEQ]))
                elif u in (U_FQ, U_FK, U_DQ, U_DK, U_NQ):
                    dst = {U_FQ: fq, U_FK: fk, U_DQ: dq, U_DK: dk, U_NQ: nq}[u]
                    copied(cp(dst[:, i, :], bank))
                elif s == (U_SW, 0):
                    cp(ks2[lo, :], bank[lo, :])
                    cp(ks2[hi, :], bank[lo, :])
                    cp(kw2[lo, :], bank[hi, :])
                    copied(cp(kw2[hi, :], bank[hi, :]))
                elif u == U_SW:
                    copied(cp(nv[:, i - 1, :], bank[:, 0:2 * HD]))
                elif u == U_FV:
                    copied(cp(fv[:, i, :], bank[:, 0:GW]))
                elif u == U_DV:
                    copied(cp(dv[:, i, :], bank[:, 0:GW]))
                else:
                    c = 256 * (u - U_GZ)
                    copied(a(sz[:, i, c:c + 256], bank[:, 0:256], ACT.Silu))

            def latr(link):
                act.wait_ge(s_lss, 1)
                link(a(llr[:, 0, :], lss[:, 0, :], ACT.Ln, bias=eps, scale=1.0 / Q_LORA))
                link(a(llr[:, 1, :], lss[:, 1, :], ACT.Ln, bias=eps, scale=1.0 / KV_LORA))
                a(lss[:, :, :], llr[:, :, :], ACT.Exp, scale=-0.5).then_inc(s_llr, 1)
                act.wait_ge(s_fa, 1)
                link(a(fe[:, :, :], fa[:, :, :], ACT.Exp, scale=-1.0))
                a(fl[:, :, :], fe[:, :, :], ACT.Ln, bias=1.0).then_inc(s_fl, 1)
                act.wait_ge(s_gd, 1)
                a(ge[:, :, :, :], gd[:, :, :, :], ACT.Exp).then_inc(s_ge, 1)

            def stage(layer, kind, arg, link):
                cp = nc.scalar.copy
                if kind == "latr":
                    latr(link)
                elif kind == "ik":
                    act.wait_ge(s_ikp, 1)
                    cp(ikT, ps[:, 4, :]).then_inc(s_ikT, 1)
                elif kind == "idx":
                    act.wait_ge(s_idx, arg)
                    if arg > 1:
                        act.wait_ge(s_isc, H * (arg - 1))
                    w = P * (arg + 1)
                    a(rl[:, :, 0:w], ps[:, 4:8, 0:w], ACT.Relu, scale=0.5).then_inc(s_relu, 1)
                elif kind == "lat":
                    act.wait_ge(s_latp, 1)
                    g = par_("q_g")
                    a(qlT[0], ps[:, 4, :], ACT.Copy, scale=g[:, 0:1]).then_inc(s_latT, 1)
                    a(qlT[1][0:64, :], ps[0:64, 5, :], ACT.Copy, scale=g[0:64, 1:2]).then_inc(s_latT, 1)
                    a(klT, ps[:, 6, :], ACT.Copy, scale=par_("kv_g")).then_inc(s_latT, 1)
                elif kind == "uq":
                    for i in range(NB):
                        act.wait_ge(s_uq, i + 1)
                        cp(q_tm[:, i].rearrange("p h e -> p (h e)"), ps[:, 4 + i, 0:H * QK_W]).then_inc(s_uqe, 1)
                elif kind == "ukv":
                    for i in range(NB):
                        if i < NB - 1:
                            act.wait_ge(s_ukv, i + 1)
                        else:
                            act.wait_ge(w_used, layer * NU + U_MLA + 1)
                        kv = ps[:, 4 + i, :].rearrange("p (h e) -> p h e", h=H)
                        cp(k_tm[:, i, :, 0:HD], kv[:, :, 0:HD])
                        cp(v_tm[:, i].rearrange("p (h e) -> p h e", h=H), kv[:, :, HD:2 * HD]).then_inc(s_ukve, 1)
                elif kind == "hid":
                    act.wait_ge(w_used, layer * NU + U_CMP + 1)
                    a(hidk[:, 0:N_CMP], ps[0:HD, 4, 0:N_CMP], ACT.Silu).then_inc(s_hid, 1)
                    a(hidv[:, :, 0:N_CMP], ps[0:HD, 4, 64:64 + N_CMP].unsqueeze(1).broadcast_to([HD, H, N_CMP]),
                      ACT.Silu).then_inc(s_hid, 1)
                elif kind == "kc":
                    act.wait_ge(s_kcp, 1)
                    cp(kc2[:, 0:N_CMP], ps[:, 5, 0:N_CMP]).then_inc(s_kc, 1)
                    for h in range(H):
                        r = slice(NCP * h, NCP * h + NCP)
                        last = cp(vcd[r, h, :], ps[r, 6, 0:HD])
                    last.then_inc(s_kc, 1)
                elif kind in ("mq", "mk"):
                    dst, made, done = (mq, s_mqp, s_mq) if kind == "mq" else (mk, s_mkp, s_mk)
                    for h in range(H):
                        act.wait_ge(made, h + 1)
                        cp(dst[0:QK_W, h, :], ps[0:QK_W, 4 + h, :]).then_inc(done, 1)
                elif kind == "fb":
                    act.wait_ge(s_isc, H * (NB - 1))
                    for h in range(H):
                        act.wait_ge(s_fbp, h + 1)
                        cp(fb[:, h, :], ps[:, 4 + h, :]).then_inc(s_fb, 1)

            def rms(link, done):
                link(a(lnv[:, :], ps[:, 6, :], ACT.Ln, bias=eps))
                a(rb[:, :], lnv[:, :], ACT.Exp, scale=-0.5).then_inc(done, 1)

            act.wait_ge(first_loaded, 64)
            act.wait_ge(setup_dve, 4)
            a(sc[:, :], cT[:, :], ACT.Silu).then_inc(setup_act, 1)
            with act.Fori(0, DEPTH) as layer:
                link = linker(act, a_link)
                a(flat_o, xT[:, :, :].rearrange("p k t -> p (k t)"), ACT.Square).then_inc(s_sq, 1)
                act.wait_ge(s_ssum, 1)
                rms(link, s_rb)
                for k in range(KD):
                    act.wait_ge(s_h0, k + 1)
                    a(hT[:, k, :], hT[:, k, :], ACT.Identity, bias=mod[:, k:k + 1]).then_inc(s_h, 1)
                for kind, arg in SCHED:
                    if kind == "proj":
                        proj(layer, arg)
                    else:
                        stage(layer, kind, arg, link)
                act.wait_ge(s_csub, 1)
                a(pc[:, :, :, 0:N_CMP], pc[:, :, :, 0:N_CMP], ACT.Exp).then_inc(s_cexp, 1)
                for t in range(NUN + 2):
                    if t < NUN:
                        _, i, _ = UNITS[t]
                        w = P * (i + 1)
                        act.wait_ge(s_ttr, t + 1)
                        if t >= 3:
                            act.wait_ge(s_tr, t - 2)
                        a(pr_[t % 3][:, 0:w], sm[t % 3][:, 0:w], ACT.Exp, bias=nmx[:, t:t + 1], scale=-1.0,
                          accum_out=rsum[:, t:t + 1]).then_inc(s_exp, 1)
                    u = t - 2
                    if u >= 0 and u % 2 == 0:
                        w = P * (UNITS[u][1] + 1)
                        act.wait_ge(s_tr, u + 1)
                        if u >= 2:
                            act.wait_ge(s_pv, u - 1)
                        nc.scalar.copy(pt[0][:, 0:w], ps[:, 3, 0:w]).then_inc(s_pta, 1)
                    if t == CMP_T_AT:
                        act.wait_ge(s_pctp, 1)
                        nc.scalar.copy(pct[:, :, :].rearrange("p i q -> p (i q)"), ps[:, 7, :]).then_inc(s_pct, 1)
                act.wait_ge(s_norm, NUN // H)
                for i in range(NB):
                    for m in range(4):
                        link(a(junk[:, :], o_sb[:, i, GW * m:GW * m + GW], ACT.Square, accum_out=gss[:, i, m:m + 1]))
                link(a(gln[:, :, :], gss[:, :, :], ACT.Ln, bias=eps, scale=1.0 / GW))
                a(grs[:, :, :], gln[:, :, :], ACT.Exp, scale=-0.5).then_inc(s_grs, 1)
                for k in range(KD):
                    act.wait_ge(s_yp, k + 1)
                    a(hT[:, k, :], ps[:, k % 4, :], ACT.Copy, scale=par_("out_g")[:, k:k + 1]).then_inc(s_oT, 1)
                act.wait_ge(s_x, KD)
                act.sem_inc(arrived, 1)
                act.wait_ge(go, layer + 1)
            a(flat_o, xT[:, :, :].rearrange("p k t -> p (k t)"), ACT.Square).then_inc(fin_act, 1)
            act.wait_ge(fin_pe, 1)
            a(lnv[:, :], ps[:, 6, :], ACT.Ln, bias=eps).then_inc(fin_act, 1)
            act.wait_ge(fin_act, 2)
            a(rb[:, :], lnv[:, :], ACT.Exp, scale=-0.5).then_inc(fin_act, 1)

        @block.vector
        def _(dve):
            v = nc.vector

            def wait_tm(n):
                dve.wait_ge(s_evac, n)

            def softmax_units():
                for t in range(NUN + 4):
                    if t < NUN:
                        m, i, h = UNITS[t]
                        w = P * (i + 1)
                        bias = {"mla": con("mask")[:, SEQ - w:SEQ], "fox": fb[:, h, 0:w]}.get(
                            m, alibi[:, h, SEQ - w:SEQ])
                        dve.wait_ge(s_sc, t + 1)
                        if t >= 3:
                            dve.wait_ge(s_exp, t - 2)
                        scale = QK_W ** -0.5 if m == "mla" else HD ** -0.5
                        v.tensor_tensor_reduce(sm[t % 3][:, 0:w], ps[:, t % 3, 0:w], bias, -scale, 3e38,
                                               ALU.add, ALU.min, nmx[:, t:t + 1]).then_inc(s_ttr, 1)
                    u = t - 2
                    if 0 <= u < NUN and u % 2 == 1:
                        w = P * (UNITS[u][1] + 1)
                        dve.wait_ge(s_tr, u + 1)
                        if u >= 2:
                            dve.wait_ge(s_pv, u - 1)
                        v.tensor_copy(pt[1][:, 0:w], ps[:, 4, 0:w]).then_inc(s_ptd, 1)
                    if t >= 7 and (t - 3) % H == 0:
                        norm((t - 3) // H - 1)
                    if t == CMP_V0_AT:
                        cmp_out(0)
                    if t == CMP_V1_AT:
                        cmp_out(1)

            def norm(g):
                m, i, _ = UNITS[H * g]
                c = slice(H * g, H * g + H)
                dve.wait_ge(s_pv, H * (g + 1))
                link(v.reciprocal(rinv[:, c], rsum[:, c]))
                fac = rinv[:, c]
                if m in ("sel", "win"):
                    link(v.tensor_tensor(rfac[:, c], rinv[:, c], gsig[:, i, :, 1 if m == "sel" else 2], ALU.mult))
                    fac = rfac[:, c]
                o = ps[:, 5 + g % 2, 0:GW].rearrange("p (h e) -> p h e", h=H)
                dst = o_sb[:, i, OUT_COL[m]:OUT_COL[m] + GW]
                fac = fac.unsqueeze(2).broadcast_to([P, H, HD])
                if m in ("sel", "win"):
                    link(v.tensor_tensor(otmp[:, :].rearrange("p (h e) -> p h e", h=H), o, fac, ALU.mult))
                    v.tensor_tensor(dst, dst, otmp[:, :], ALU.add).then_inc(s_norm, 1)
                else:
                    v.tensor_tensor(dst.rearrange("p (h e) -> p h e", h=H), o, fac, ALU.mult).then_inc(s_norm, 1)

            def cmp_out(half):
                dve.wait_ge(s_cpv, half + 1)
                for i in (2 * half, 2 * half + 1):
                    o = ps[:, 7, (i % 2) * GW:(i % 2) * GW + GW].rearrange("p (h e) -> p h e", h=H)
                    dst = o_sb[:, i, 3 * GW:4 * GW].rearrange("p (h e) -> p h e", h=H)
                    last = v.tensor_tensor(dst, o, cfac[:, i].unsqueeze(2).broadcast_to([P, H, HD]), ALU.mult)
                last.then_inc(s_co, 1)

            dve.wait_ge(first_loaded, 64)
            v.memset(hidv[:, :, :], 0.0).then_inc(setup_dve, 1)
            v.memset(pc[:, :, :, :], 0.0).then_inc(setup_dve, 1)
            v.memset(vcd[:, :, :], 0.0).then_inc(setup_dve, 1)
            v.tensor_copy(identb[:, :], ident)
            v.tensor_copy(maskb[:, :], con("mask")[:, SEQ - P:SEQ]).then_inc(setup_dve, 1)
            with dve.Fori(0, DEPTH) as layer:
                link = linker(dve, d_link)
                dve.wait_ge(par_loaded, layer * 16 + 16)
                dve.wait_ge(w_used, layer * NU + N_ADA)
                link(v.tensor_tensor(mod[:, :], ps[:, 7, 0:3 * KD], par_("b_ada"), ALU.add))
                link(v.scalar_tensor_tensor(out=gs[:, :], in0=mod[:, KD:2 * KD], scalar=1.0, in1=par_("rms_g"),
                                            op0=ALU.add, op1=ALU.mult))
                dve.wait_ge(s_rb, 1)
                for k in range(KD):
                    v.scalar_tensor_tensor(out=hT[:, k, :], in0=xT[:, k, :], scalar=gs[:, k:k + 1], in1=rb[:, :],
                                           op0=ALU.mult, op1=ALU.mult).then_inc(s_h0, 1)
                wait_tm(step_no[U_A1, NB - 1] + 1)
                v.tensor_copy(ikd, tm[:, :, C_IK:C_IK + 32].unsqueeze(2).broadcast_to([P, NB, H, 32])).then_inc(s_ikd, 1)
                bf = par_("b_f").unsqueeze(1).broadcast_to([P, NB, H])
                link(v.tensor_tensor(fy[:, :, :], tm[:, :, C_FF:C_FF + H], bf, ALU.add))
                v.scalar_tensor_tensor(out=fa[:, :, :], in0=fy[:, :, :], scalar=-1.0, in1=fy[:, :, :],
                                       op0=ALU.mult, op1=ALU.max).then_inc(s_fa, 1)
                v.tensor_scalar(gd[:, :, :, :].rearrange("p i h b -> p i (h b)"), tm[:, :, C_NG:C_NG + 3 * H],
                                -1.0, 80.0, ALU.mult, ALU.min).then_inc(s_gd, 1)
                for i in range(NB):
                    link(v.tensor_tensor_reduce(junk[:, 0:Q_LORA], tm[:, i, 0:Q_LORA], tm[:, i, 0:Q_LORA], 1.0, 0.0,
                                                ALU.mult, ALU.add, lss[:, 0, i:i + 1]))
                wait_tm(step_no[U_A2, NB - 1] + 1)
                for i in range(NB):
                    kvl = tm[:, i, C_KVL:C_KVL + KV_LORA]
                    link(v.tensor_tensor_reduce(junk[:, 0:KV_LORA], kvl, kvl, 1.0, 0.0, ALU.mult, ALU.add,
                                                lss[:, 1, i:i + 1]))
                dve.sem_inc(s_lss, 1)
                dve.wait_ge(s_fl, 1)
                v.scalar_tensor_tensor(out=fls[:, :, :], in0=fy[:, :, :], scalar=0.0, in1=fl[:, :, :],
                                       op0=ALU.min, op1=ALU.subtract).then_inc(s_fls, 1)
                v.tensor_tensor(qn, tm[:, :, 0:Q_LORA], lss[:, 0, :].unsqueeze(2).broadcast_to([P, NB, Q_LORA]), ALU.mult)
                v.tensor_tensor(kn, tm[:, :, C_KVL:C_KVL + KV_LORA],
                                lss[:, 1, :].unsqueeze(2).broadcast_to([P, NB, KV_LORA]), ALU.mult).then_inc(s_lat, 1)
                dve.wait_ge(s_ge, 1)
                link(v.tensor_scalar(gd[:, :, :, :], ge[:, :, :, :], 1.0, None, ALU.add))
                v.reciprocal(gsig[:, :, :, :], gd[:, :, :, :]).then_inc(s_gsig, 1)
                wait_tm(step_no[U_IQ, 1] + 1)
                pos = par_("pos").rearrange("p (s j) -> p s j", s=2)
                for s in range(2):
                    src = bass.AP(tensor=cmp2[:, s, :].tensor, offset=cmp2[:, s, :].offset,
                                  ap=[cmp2[:, s, :].ap[0], [2, CMP_J], [CMP_STRIDE, N_CMP]])
                    v.tensor_tensor(blk[:, s], src, pos[:, s, :].unsqueeze(2).broadcast_to([P, CMP_J, N_CMP]),
                                    ALU.add).then_inc(s_blk, 1)

                def index_scores(i):
                    w = P * (i + 1)
                    dve.wait_ge(s_relu, i)
                    for h in range(H):
                        before = con("mask")[:, SEQ - w:SEQ] if h == 0 else work[i][:, :]
                        v.scalar_tensor_tensor(out=work[i][:, :], in0=rl[:, h, 0:w],
                                               scalar=tm[:, i, C_IW + h:C_IW + h + 1], in1=before,
                                               op0=ALU.mult, op1=ALU.add).then_inc(s_isc, 1)
                        dve.wait_ge(s_isc, H * (i - 1) + h + 1)

                index_scores(1)
                dve.wait_ge(s_flp, 1)
                v.tensor_tensor_scan(fcum[:, :], con("ones")[0:H, :], ps[0:H, 4, :], 0.0, ALU.mult,
                                     ALU.add).then_inc(s_fcum, 1)
                index_scores(2)
                index_scores(3)
                n = NB - 1
                for r in range(TOPK // 8):
                    for i in range(1, NB):
                        if r:
                            dve.wait_ge(s_top, 2 * n * (r - 1) + n + i)
                        v.max(top8[:, i, :], work[i][:, :]).then_inc(s_top, 1)
                    for i in range(1, NB):
                        dve.wait_ge(s_top, 2 * n * r + i)
                        v.match_replace(work[i][:, :], top8[:, i, :], work[i][:, :], TAKEN).then_inc(s_top, 1)
                dve.wait_ge(s_top, 2 * n * (TOPK // 8))
                for i in range(1, NB):
                    v.tensor_scalar(selm[i][:, :], work[i][:, :], LOWEST, MASKED, ALU.is_gt, ALU.mult).then_inc(s_selm, 1)
                dve.wait_ge(s_cs, 1)
                cb = con("cmpb").rearrange("p (i h n) -> p i h n", i=NB, h=H)[:, :, :, 0:N_CMP]
                pcv = pc[:, :, :, 0:N_CMP]
                for b in range(2):
                    css = ps[:, 4 + b, 0:NB * 2 * NCP].rearrange("p (i h n) -> p i h n", i=NB, h=2)[:, :, :, 0:N_CMP]
                    link(v.tensor_tensor(pcv[:, :, b::2, :], css, cb[:, :, b::2, :], ALU.add))
                link(v.tensor_reduce(cmx[:, :, :], pcv, AX_X, ALU.max))
                link(v.tensor_tensor(pcv, pcv, cmx[:, :, :].unsqueeze(3).broadcast_to([P, NB, H, N_CMP]), ALU.subtract))
                v.tensor_scalar(pcv, pcv, HD ** -0.5, None, ALU.mult).then_inc(s_csub, 1)
                dve.wait_ge(s_cexp, 1)
                link(v.tensor_reduce(cden[:, :, :], pcv, AX_X, ALU.add))
                link(v.reciprocal(crec[:, :, :], cden[:, :, :]))
                link(v.tensor_scalar(crec[:, 0, :], crec[:, 0, :], late, None, ALU.mult))
                v.tensor_tensor(cfac[:, :, :], crec[:, :, :], gsig[:, :, :, 0], ALU.mult).then_inc(s_pc, 1)
                dve.wait_ge(s_pc, 1)
                softmax_units()
                dve.wait_ge(s_grs, 1)
                for i in range(NB):
                    for half in range(2):
                        for m in (2 * half, 2 * half + 1):
                            o = o_sb[:, i, GW * m:GW * m + GW]
                            last = v.scalar_tensor_tensor(out=o, in0=o, scalar=grs[:, i, m:m + 1],
                                                          in1=sz[:, i, GW * m:GW * m + GW], op0=ALU.mult, op1=ALU.mult)
                        last.then_inc(s_y, 1)
                for k in range(KD):
                    if k % 2 == 0:
                        dve.wait_ge(s_out, k // 2 + 1)
                    else:
                        dve.wait_ge(w_used, layer * NU + U_OUT + k // 2 + 1)
                    v.scalar_tensor_tensor(out=xT[:, k, :], in0=ps[:, k % 4, :], scalar=mod[:, 2 * KD + k:2 * KD + k + 1],
                                           in1=xT[:, k, :], op0=ALU.mult, op1=ALU.add).then_inc(s_x, 1)
                dve.wait_ge(s_x, KD)
                dve.sem_inc(arrived, 1)
                dve.wait_ge(go, layer + 1)
            dve.wait_ge(fin_act, 3)
            for k in range(KD):
                v.scalar_tensor_tensor(out=xT[:, k, :], in0=xT[:, k, :], scalar=fing[:, k:k + 1], in1=rb[:, :],
                                       op0=ALU.mult, op1=ALU.mult).then_inc(fin_dve, 1)

        @block.gpsimd
        def _(pool):
            g = nc.gpsimd
            with pool.Fori(0, DEPTH) as layer:
                link = linker(pool, g_link)
                pool.wait_ge(s_uqe, NB)
                cb = cosv.broadcast_to([P, NB, H, 16])
                sb_ = sinv.broadcast_to([P, NB, H, 16])
                x1, x2 = q_tm[:, :, :, HD:HD + 16], q_tm[:, :, :, HD + 16:HD + 32]
                g.tensor_tensor(rt[0], x1, cb, ALU.mult)
                g.tensor_tensor(rt[1], x2, sb_, ALU.mult)
                g.tensor_tensor(rt[2], x1, sb_, ALU.mult)
                link(g.tensor_tensor(rt[3], x2, cb, ALU.mult))
                g.tensor_tensor(x1, rt[0], rt[1], ALU.subtract)
                g.tensor_tensor(x2, rt[2], rt[3], ALU.add).then_inc(s_rope, 1)
                pool.wait_ge(s_rope, 1)
                k1 = tm[:, :, C_KR:C_KR + 16].unsqueeze(2).broadcast_to([P, NB, H, 16])
                k2 = tm[:, :, C_KR + 16:C_KR + 32].unsqueeze(2).broadcast_to([P, NB, H, 16])
                g.tensor_tensor(rt[0], k1, cb, ALU.mult)
                g.tensor_tensor(rt[1], k2, sb_, ALU.mult)
                g.tensor_tensor(rt[2], k1, sb_, ALU.mult)
                link(g.tensor_tensor(rt[3], k2, cb, ALU.mult))
                g.tensor_tensor(k_tm[:, :, :, HD:HD + 16], rt[0], rt[1], ALU.subtract)
                g.tensor_tensor(k_tm[:, :, :, HD + 16:HD + 32], rt[2], rt[3], ALU.add).then_inc(s_rope, 1)
                pool.wait_ge(s_rope, 2)
                pool.wait_ge(arrived, 3)
                for s in layer_sems:
                    pool.sem_clear(s)
                pool.sem_inc(go, 1)


def _constants():
    f = np.float32
    out = np.zeros((P, CO_W), f)

    def put(name, a):
        a = np.asarray(a, f)
        out[:a.shape[0], CO[name][0]:CO[name][1]] = a.reshape(a.shape[0], -1)

    p = np.arange(P)
    slopes = (2.0 ** (-8.0 * (np.arange(H) + 1) / H)).astype(f)
    c = np.arange(SEQ) - (SEQ - P)
    mask = np.where(c[None, :] <= p[:, None], 0.0, MASKED)
    put("ident", np.eye(P))
    put("mask", mask)
    put("alibi", slopes[None, :, None] * (HD ** 0.5 * c)[None, None, :] + mask[:, None, :])
    t = np.arange(SEQ).reshape(NB, P).T
    end = np.arange(NCP) * CMP_STRIDE + CMP_LEN - 1
    cmpb = slopes[None, None, :, None] * (HD ** 0.5 * end) + np.zeros((P, NB, 1, 1))
    put("cmpb", np.where(end <= t[:, :, None, None], cmpb, MASKED))
    inv = f(10000.0) ** (-np.arange(16, dtype=f) / f(16))
    ang = t[:, :, None].astype(f) * inv.astype(f)
    put("cos", np.cos(ang))
    put("sin", np.sin(ang))
    put("mean", np.full((P, P), 1.0 / D))
    put("selrow", (np.eye(H) * -(HD ** 0.5))[:, :, None] * np.ones(P))
    put("ones", np.ones((H, SEQ)))
    put("late", (p >= CMP_LEN - 1)[:, None])
    put("eps", np.full((P, 1), EPS))
    return out


def _rows(w):
    return w.reshape(w.shape[0], -1, P, w.shape[-1]).transpose(0, 2, 1, 3)


def _units(w, width):
    n = w.shape[-1]
    return [w[..., c:c + width].reshape(w.shape[0], P, -1) for c in range(0, n, width)]


def kernel(x, c, rms_g, w_ada, b_ada, w_in, mla_q_norm, mla_w_uq, mla_kv_norm, mla_w_ukv, fox_b_f,
           nsa_cmp_pos, nsa_cmp_w1, nsa_cmp_w2, out_norm_g, w_out, final_g):
    import concourse.bacc as bacc
    from concourse.bass_utils import run_bass_kernel_spmd

    (x, c, rms_g, w_ada, b_ada, w_in, mla_q_norm, mla_w_uq, mla_kv_norm, mla_w_ukv, fox_b_f, nsa_cmp_pos,
     nsa_cmp_w1, nsa_cmp_w2, out_norm_g, w_out, final_g) = (
        np.asarray(a) for a in (x, c, rms_g, w_ada, b_ada, w_in, mla_q_norm, mla_w_uq, mla_kv_norm, mla_w_ukv,
                                fox_b_f, nsa_cmp_pos, nsa_cmp_w1, nsa_cmp_w2, out_norm_g, w_out, final_g))
    widths = [("q_lat", 192), ("kv_lat", 128), ("k_rope", 32), ("fox_q", 256), ("fox_k", 256), ("fox_v", 256),
              ("fox_f", 4), ("dsa_q", 256), ("dsa_k", 256), ("dsa_v", 256), ("idx_q", 128), ("idx_k", 32),
              ("idx_w", 4), ("nsa_q", 256), ("k_cmp", 64), ("v_cmp", 64), ("k_sel", 64), ("v_sel", 64),
              ("k_win", 64), ("v_win", 64), ("nsa_gate", 12), ("gate_z", 1024)]
    rows, seg, at = _rows(w_in), {}, 0
    for name, w in widths:
        seg[name] = rows[..., at:at + w]
        at += w

    def unit(*names):
        return np.concatenate([seg[n] for n in names], axis=-1).reshape(DEPTH, P, -1)

    w_uq = np.zeros((DEPTH, 2 * P, H * QK_W), np.float32)
    w_uq[:, :Q_LORA] = mla_w_uq
    mla = np.concatenate([_rows(w_uq).reshape(DEPTH, P, -1), mla_w_ukv], axis=-1)
    cmpw = nsa_cmp_w1.reshape(DEPTH, 2, CMP_J, P, HD).transpose(0, 3, 1, 2, 4).reshape(DEPTH, P, -1)
    w_all = np.concatenate(
        _units(_rows(w_ada), 256)
        + [unit("q_lat", "idx_k", "idx_w", "fox_f", "nsa_gate"), unit("kv_lat", "k_rope"),
           unit("idx_q", "k_cmp", "v_cmp"), unit("fox_q"), unit("fox_k"), mla, cmpw, unit("dsa_q"), unit("dsa_k"),
           unit("nsa_q"), unit("k_sel", "k_win", "v_sel", "v_win"), unit("fox_v"), unit("dsa_v")]
        + _units(seg["gate_z"], 256) + _units(_rows(w_out), 256), axis=-1)

    par = np.zeros((DEPTH, P, PR_W), np.float32)

    def put(name, a):
        par[:, :a.shape[1], PR[name][0]:PR[name][1]] = a

    def cols(a):
        return a.reshape(DEPTH, -1, P).transpose(0, 2, 1)

    put("rms_g", cols(rms_g))
    put("b_ada", cols(b_ada))
    put("out_g", cols(out_norm_g))
    qg = np.zeros((DEPTH, 2 * P), np.float32)
    qg[:, :Q_LORA] = mla_q_norm
    put("q_g", cols(qg))
    put("kv_g", mla_kv_norm[:, :, None])
    put("b_f", np.broadcast_to(fox_b_f[:, None, :], (DEPTH, P, H)))
    put("pos", nsa_cmp_pos.reshape(DEPTH, 2, CMP_J, P).transpose(0, 3, 1, 2).reshape(DEPTH, P, -1))
    put("w2k", np.concatenate([nsa_cmp_w2[:, 0]] * 2, axis=-1))
    put("w2v", nsa_cmp_w2[:, 1])

    arrays = {
        "x_t": x[0].T.reshape(KD, P, SEQ).transpose(1, 0, 2),
        "c_t": c.reshape(KD, P).T,
        "w_all": w_all, "par": par, "const": _constants(),
        "fin_g": final_g.reshape(KD, P).T,
    }
    arrays = {k: np.ascontiguousarray(v) for k, v in arrays.items()}
    nc = bacc.Bacc("TRN2", target_bir_lowering=False, num_devices=1)
    aps = [nc.dram_tensor(k, v.shape, mybir.dt.from_np(v.dtype), kind="ExternalInput").ap() for k, v in arrays.items()]
    y_t = nc.dram_tensor("y_t", (P, KD, SEQ), F32, kind="ExternalOutput").ap()
    program(nc, *aps, y_t)
    r = run_bass_kernel_spmd(nc, [arrays], core_ids=[0])
    y = np.asarray(r.results[0]["y_t"])
    return np.ascontiguousarray(y.transpose(1, 0, 2).reshape(D, SEQ).T)[None]
```

```python
from contextlib import ExitStack

import numpy as np
import concourse.bass as bass
from concourse import mybir

F32 = mybir.dt.float32
BF16 = mybir.dt.bfloat16
ALU = mybir.AluOpType
ACT = mybir.ActivationFunctionType
AX_X = mybir.AxisListType.X

P = 128
D, SEQ, DEPTH = 1024, 512, 2
KD = D // P
NB = SEQ // P
H, HD = 4, 64
GW = H * HD
Q_LORA, KV_LORA, ROPE = 192, 128, 32
QK_W = HD + ROPE
TOPK = min(256, SEQ // 4)
CMP_LEN, CMP_STRIDE = 32, 16
N_CMP = (SEQ - CMP_LEN) // CMP_STRIDE + 1
NCP = 32
CMP_J = CMP_LEN // 2
EPS = 1e-6
MASKED = -1e30
TAKEN = -3e38
LOWEST = -2e38

F32R = mybir.dt.float32r

SPLIT = {"A1": (244, "t"), "A2": (160, "t"), "IQ": (128, "c"), "CM": (128, "c"), "FQ": (256, "c"), "FK": (256, "c"),
         "FV": (256, "t"), "GZ0": (256, "t"), "NQ": (256, "c"), "SW": (256, "cv"), "DQ": (256, "c"), "DK": (256, "c"),
         "DV": (256, "t"), "GZ1": (256, "t"), "GZ3": (256, "t"), "GZ2": (256, "t"),
         "O0": (256, "o"), "O1": (256, "o"), "O2": (256, "o"), "O3": (256, "o")}
SPLIT_NAMES = list(SPLIT)
NSP = len(SPLIT)
PIECES = 4
SLOT = KD * 256
RING = 3
N_GATE, N_SS = 4, 8
ADA_CHUNKS = 4
DVE_TILES = 6
UQ_W, UKV_W, CMPW_W = 2 * H * QK_W, 2 * GW, CMP_J * HD
assert NSP % 2 == 0


def steps_of(name):
    width, how = SPLIT[name]
    if how == "t":
        return [(name, i, "t") for i in range(NB)]
    if how == "cv":
        return [(name, 0, "c"), (name, 1, "c"), (name, 2, "v")]
    return [(name, i, "c") for i in range(width // P)]


STEPS = [s for n in SPLIT_NAMES if n[0] != "O" for s in steps_of(n)]
STEP_NO = {s: n for n, s in enumerate(STEPS)}

MIXERS = ["mla", "fox", "sel", "win", "dsa"]
UNITS = [(m, i, h) for m in MIXERS for i in range(NB) for h in range(H)]
NUN = len(UNITS)
OUT_COL = {"mla": 0, "fox": GW, "dsa": 2 * GW, "sel": 3 * GW, "win": 3 * GW}
FILLERS = SPLIT_NAMES[6:16]
PER_FILL = NUN // len(FILLERS)
CS_AT = 26
ADA_FROM = 44
CT_ORDER = [0, 1, 2, 3, 6, 7, 4, 5]


def main_items():
    items = []

    def split(c):
        return [("split", c, p) for p in range(PIECES)]

    def proj(name, part=None):
        st = steps_of(name)
        return [("proj", s, 0, KD) for s in (st if part is None else [st[part]])]

    items += [("norm",)] + split(1) + [("first",)] + split(2)
    items += proj("A2") + split(3) + [("latr",)]
    items += proj("IQ") + split(4) + [("lat",), ("foxT",)]
    items += proj("CM") + split(5) + [("blk",), ("uq",), ("ik",)]
    items += proj("FQ", 0) + [("ukv",), ("idx", 1)] + proj("FQ", 1) + split(6) + [("hid",)]
    items += proj("FK", 0) + [("idx", 2), ("mq",)] + proj("FK", 1) + [("mk",), ("idx", 3)] + split(7)
    ada_chunks = (N_GATE + N_SS) * ADA_CHUNKS
    done_chunks = 0
    turn_at = None
    top = [(r, i) for r in range(TOPK // 8) for i in range(1, NB)]
    for t in range(NUN):
        at_unit = len(items)
        items.append(("unit", t))
        name = FILLERS[t // PER_FILL]
        work = [(s, k) for s in steps_of(name) if s[2] != "v" for k in range(KD)]
        n = t % PER_FILL
        mine = work[len(work) * n // PER_FILL:len(work) * (n + 1) // PER_FILL]
        for s in dict.fromkeys(s for s, _ in mine):
            ks = [k for q, k in mine if q == s]
            items.append(("proj", s, ks[0], ks[-1] + 1))
        if name == "SW" and n == PER_FILL - 1:
            turn_at = t + 1
        if t == turn_at:
            items.insert(at_unit + 1, ("proj", ("SW", 2, "v"), 0, KD))
        c = SPLIT_NAMES.index(name) + 1
        if 1 <= n <= PIECES and t > PER_FILL:
            items.append(("split", c, n - 1))
        if t < len(top):
            items.append(("top",) + top[t])
        if t == len(top):
            items.append(("selm",))
        last = FILLERS[t // PER_FILL - 1]
        if t >= PER_FILL and last[:2] == "GZ" and n in (1, 3):
            items.append(("sig" if n == 1 else "silu", int(last[2])))
        for at, what in ((2, ("kc",)), (4, ("fb", 0)), (6, ("fb", 1)), (8, ("fb", 2)), (10, ("fb", 3)), (CS_AT, ("cs", 0)), (CS_AT + 1, ("cs", 1)), (CS_AT + 2, ("csoft",)), (CS_AT + 4, ("cturn",)),
                         (CS_AT + 6, ("cval", 0)), (CS_AT + 8, ("cval", 1)), (20, ("gss", 0)), (22, ("gn", 0)), (60, ("gss", 1)), (68, ("gn", 1)),
                         (70, ("gss", 3)), (76, ("gn", 3))):
            if t == at:
                items.append(what)
        if t >= ADA_FROM:
            upto = ada_chunks * (t - ADA_FROM + 1) // (NUN - ADA_FROM)
            for j in range(done_chunks, upto):
                items.append(("ada", j // ADA_CHUNKS, j % ADA_CHUNKS))
                if j % ADA_CHUNKS == 2 and j > ADA_CHUNKS:
                    items.append(("adasum", j // ADA_CHUNKS - 1))
            done_chunks = upto
    assert done_chunks == ada_chunks
    items += [("unit", NUN), ("sig", 2), ("adasum", N_GATE + N_SS - 1)] + [("yT", k) for k in CT_ORDER[:2]]
    items += [("unit", NUN + 1)] + [("yT", k) for k in CT_ORDER[2:4]] + [("unit", NUN + 2), ("silu", 2), ("gss", 2)]
    items += [("yT", k) for k in CT_ORDER[4:6]] + [("gn", 2), ("out", 0, 0, 6), ("out", 1, 0, 6)] + split(17)
    items += [("yT", k) for k in CT_ORDER[6:]]
    items += [("out", 0, 6, KD), ("out", 1, 6, KD), ("x", 0), ("x", 1)] + split(18)
    items += [("out", 2, 0, KD), ("x", 2), ("out", 3, 0, KD), ("x", 3)] + split(19)
    items += [("out", 4, 0, KD), ("x", 4), ("out", 5, 0, KD), ("x", 5)] + split(20)
    items += [("out", 6, 0, KD), ("x", 6), ("out", 7, 0, KD), ("x", 7), ("rms",)]
    return items


MAIN = main_items()


def ring_order():
    order = []
    for it in MAIN:
        if it[0] == "split" and it[2] == 0:
            order.append(("split", it[1]))
        elif it[0] in ("uq", "ukv"):
            order.append((it[0], 0))
        elif it[0] == "hid":
            order += [("cmpk", 0), ("cmpv", 0)]
        elif it[0] == "ada" and it[2] == 0:
            order.append(("ada", it[1]))
    return order


RING_UNITS = ring_order()
NR = len(RING_UNITS)
FIRST_UNITS = N_SS + 1
assert NR % RING == 0 and FIRST_UNITS % RING == 0
POS = {u: n for n, u in enumerate(RING_UNITS)}


def unit_width(u):
    kind, n = u
    if kind == "split":
        return KD * SPLIT[SPLIT_NAMES[n % NSP]][0]
    return {"uq": UQ_W, "ukv": UKV_W, "cmpk": CMPW_W, "cmpv": CMPW_W, "ada": SLOT}[kind]


WIDTHS = [unit_width(u) for u in RING_UNITS]
OFFSETS = [sum(WIDTHS[:n]) for n in range(NR + 1)]
A1_W, A2_W = SPLIT["A1"][0], SPLIT["A2"][0]
FIRST_W = N_SS * SLOT + KD * A1_W

C_QL, C_IK, C_IW, C_FF, C_NG, C_KVL, C_KR = 0, 192, 224, 228, 232, 244, 372
TM_W = A1_W + A2_W


def columns(widths):
    at, out = 0, {}
    for name, w in widths:
        out[name] = (at, at + w)
        at += w
    return out, at


PR, PR_W = columns([("b_gate", KD), ("b_next", 2 * KD), ("rms_next", KD), ("out_g", KD), ("q_g", 2), ("kv_g", 1),
                    ("b_f", H), ("pos", 2 * CMP_J), ("w2k", 2 * HD), ("w2v", HD)])
P0, P0_W = columns([("b_first", 2 * KD), ("rms_first", KD), ("fin_g", KD), ("c", KD), ("mean", P), ("one", 1),
                    ("eps", 1), ("late", 1)])
CO, CO_W = columns([("ident", P), ("alibi", H * SEQ), ("mask", SEQ), ("cmpb", NB * H * NCP), ("cos", NB * 16),
                    ("sin", NB * 16), ("selrow", H * P)])


def program(nc, x_t, first, w_first, w_all, par, const, y_t):
    xs = nc.dram_tensor("xs", (P, KD, SEQ), F32).ap()
    with ExitStack() as ctx:
        def sb(name, shape, dt=F32):
            return ctx.enter_context(nc.sbuf_tensor(name, shape, dt))

        def sem(name):
            return ctx.enter_context(nc.semaphore(name))

        h_hi, h_lo = sb("h_hi", [P, KD, SEQ], F32R), sb("h_lo", [P, KD, SEQ], F32R)
        ring = sb("ring", [P, RING, SLOT])
        w_hi, w_lo = sb("w_hi", [P, 2, SLOT], F32R), sb("w_lo", [P, 2, SLOT], F32R)
        o_sb = sb("o_sb", [P, NB, D])
        sz = sb("sz", [P, NB, D])
        tm = sb("tm", [P, NB, TM_W])
        fq, fk = sb("fq", [P, 2, SEQ]), sb("fk", [P, 2, SEQ])
        mq, mk = sb("mq", [P, H, SEQ]), sb("mk", [P, H, SEQ])
        v_tm = sb("v_tm", [P, NB, GW])
        fv = sb("fv", [P, NB, GW])
        nv = sb("nv", [P, NB, 2 * HD])
        fb = sb("fb", [P, H, SEQ])
        cst, prm, prf = sb("cst", [P, CO_W]), sb("prm", [P, PR_W]), sb("prf", [P, P0_W])
        sc, sct = sb("sc", [P, KD]), sb("sct", [P, KD])
        mod, gs = sb("mod", [P, 3 * KD]), sb("gs", [P, KD])
        acc = sb("acc", [P, 2, 256])
        rb = sb("rb", [P, SEQ])
        identb, maskb = sb("identb", [P, P], BF16), sb("maskb", [P, P], BF16)
        work = [None] + [sb(f"work{i}", [P, P * (i + 1)]) for i in range(1, NB)]
        selm = [None] + [sb(f"selm{i}", [P, P * (i + 1)], BF16) for i in range(1, NB)]
        top8 = sb("top8", [P, NB, 8])
        lss, llr = sb("lss", [P, 2, NB]), sb("llr", [P, 2, NB])
        fy, fa, fe, fl, fls = (sb(n, [P, NB, H]) for n in ("fy", "fa", "fe", "fl", "fls"))
        ge, gd, gsig = (sb(n, [P, NB, H, 3]) for n in ("ge", "gd", "gsig"))
        hide, hidr, hids = (sb(n, [HD, 2, NCP]) for n in ("hide", "hidr", "hids"))
        hidk, hidv = sb("hidk", [HD, NCP]), sb("hidv", [HD, H, NCP])
        kc2, vcd = sb("kc2", [P, NCP]), sb("vcd", [P, H, HD])
        pc = sb("pc", [P, NB, H, NCP])
        cmx, cden, crec, cfac = (sb(n, [P, NB, H]) for n in ("cmx", "cden", "crec", "cfac"))
        nmx, rsum = sb("nmx", [P, NUN]), sb("rsum", [P, NUN])
        rinv, rfac = sb("rinv", [P, NUN]), sb("rfac", [P, NUN])
        gss, gln, grs = (sb(n, [P, H, NB]) for n in ("gss", "gln", "grs"))
        iqr, ikr = ([sb(f"{n}{j}", [P, SEQ], F32R) for j in range(2)] for n in ("iqr", "ikr"))
        pr_ = [sb(f"pr{n}", [P, SEQ]) for n in range(3)]
        pt = [sb(f"pt{n}", [P, SEQ]) for n in range(2)]
        ps = ctx.enter_context(nc.psum_tensor("ps", [P, 8, 512], F32))
        MISC = 1

        flat_o = o_sb[:, :, :].rearrange("p i d -> p (i d)")
        flat_s = sz[:, :, :].rearrange("p i d -> p (i d)")
        xT = flat_s.rearrange("p (k t) -> p k t", k=KD)
        xg = flat_o.rearrange("p (k t) -> p k t", k=KD)
        q_tm = flat_o[:, 0:NB * H * QK_W].rearrange("p (i h e) -> p i h e", i=NB, h=H)
        k_tm = flat_o[:, NB * H * QK_W:2 * NB * H * QK_W].rearrange("p (i h e) -> p i h e", i=NB, h=H)
        rt = [flat_o[:, 3072 + 256 * n:3072 + 256 * n + 256].rearrange("p (i h e) -> p i h e", i=NB, h=H)
              for n in range(4)]
        qn = flat_s[:, 0:768].rearrange("p (i c) -> p i c", i=NB)
        kn = flat_s[:, 768:1280].rearrange("p (i c) -> p i c", i=NB)
        qlT = [flat_s[:, 1280:1792], flat_s[:, 1792:2304]]
        klT = flat_s[:, 2304:2816]
        ikd = flat_s[:, 2816:3328].rearrange("p (i g c) -> p i g c", i=NB, g=H)
        pct, otmp = tm[:, :, 0:P], tm[:, :, P:P + HD]
        squares, squares_l = tm[:, 0:2, C_KVL:C_KVL + P], pr_[2]
        fcum = flat_s[0:H, 3328:3840]
        cmp2 = mk[:, 0:2, :]
        blk = mq[:, :, :].rearrange("p h t -> p (h t)")[:, 0:2 * CMP_J * N_CMP].rearrange(
            "p (s j n) -> p s j n", s=2, j=CMP_J)
        nq, sw_k = mk[:, 0:2, :], [mk[:, 2, :], mk[:, 3, :]]
        nvT = flat_s[:, 1280:1792]
        dq, dk, dv = mq[:, 0:2, :], mq[:, 2:4, :], v_tm
        rl = fb
        flat_fb = fb[:, :, :].rearrange("p h t -> p (h t)")
        ez_a, ez_b = (flat_fb[:, n:n + NB * GW].rearrange("p (i c) -> p i c", i=NB) for n in (0, NB * GW))
        ez_of = {0: o_sb[:, :, 2 * GW:3 * GW], 1: ez_a, 3: ez_b, 2: ez_a}
        sqr = [pr_[0], pr_[1]]
        sqa = pr_[2]

        def con(name):
            return cst[:, CO[name][0]:CO[name][1]]

        def par_(name):
            return prm[:, PR[name][0]:PR[name][1]]

        def fst(name):
            return prf[:, P0[name][0]:P0[name][1]]

        ident = con("ident")
        alibi = con("alibi").rearrange("p (h t) -> p h t", h=H)
        cosv = con("cos").rearrange("p (i e) -> p i e", i=NB).unsqueeze(2)
        sinv = con("sin").rearrange("p (i e) -> p i e", i=NB).unsqueeze(2)
        selrow = con("selrow").rearrange("p (h c) -> p h c", h=H)
        late, eps, one = fst("late"), fst("eps"), fst("one")

        w_loaded = [sem(f"w_loaded{n}") for n in range(RING)]
        s_hi = sem("s_hi")
        s_lo = sem("s_lo")
        w_done = sem("w_done")
        w_direct = sem("w_direct")
        w_ada = sem("w_ada")
        par_loaded, first_loaded, const_loaded = sem("par_loaded"), sem("first_loaded"), sem("const_loaded")
        x_moved = sem("x_moved")
        go = sem("go")
        setup_act, setup_dve, setup_pe, setup_sq, setup_ms = (
            sem(n) for n in ("setup_act", "setup_dve", "setup_pe", "setup_sq", "setup_ms"))
        setup_fill, setup_sum, fin_out, y_stored = sem("setup_fill"), sem("setup_sum"), sem("fin_out"), sem("y_stored")

        layer_sems = []

        def lsem(name):
            layer_sems.append(sem(name))
            return layer_sems[-1]

        arrived = lsem("arrived")
        s_xg, s_hhi, s_h = lsem("s_xg"), lsem("s_hhi"), lsem("s_h")
        s_proj, s_evac = lsem("s_proj"), lsem("s_evac")
        s_ikd, s_ikp, s_ikh, s_ikT = lsem("s_ikd"), lsem("s_ikp"), lsem("s_ikh"), lsem("s_ikT")
        s_idx, s_relu, s_isc = lsem("s_idx"), lsem("s_relu"), lsem("s_isc")
        s_top, s_selm = lsem("s_top"), lsem("s_selm")
        s_lss, s_llr, s_lat, s_latp, s_latT = (lsem(n) for n in ("s_lss", "s_llr", "s_lat", "s_latp", "s_latT"))
        s_uq, s_uqe, s_ukv, s_ukve = lsem("s_uq"), lsem("s_uqe"), lsem("s_ukv"), lsem("s_ukve")
        s_rope = lsem("s_rope")
        s_mqp, s_mq, s_mkp, s_mk = lsem("s_mqp"), lsem("s_mq"), lsem("s_mkp"), lsem("s_mk")
        s_fa, s_fl, s_fls, s_flp, s_fcum = (lsem(n) for n in ("s_fa", "s_fl", "s_fls", "s_flp", "s_fcum"))
        s_fbp, s_fb = lsem("s_fbp"), lsem("s_fb")
        s_gd, s_ge, s_gsig = lsem("s_gd"), lsem("s_ge"), lsem("s_gsig")
        s_blk, s_hide, s_hid, s_kcp, s_kc = (lsem(n) for n in ("s_blk", "s_hide", "s_hid", "s_kcp", "s_kc"))
        s_cs, s_csub, s_cexp, s_pc = lsem("s_cs"), lsem("s_csub"), lsem("s_cexp"), lsem("s_pc")
        s_csum = lsem("s_csum")
        s_pctp, s_pct, s_cpv, s_co = lsem("s_pctp"), lsem("s_pct"), lsem("s_cpv"), lsem("s_co")
        s_sc, s_ttr, s_exp, s_tr = lsem("s_sc"), lsem("s_ttr"), lsem("s_exp"), lsem("s_tr")
        s_pta, s_ptd, s_pv, s_norm = lsem("s_pta"), lsem("s_ptd"), lsem("s_pv"), lsem("s_norm")
        s_sig, s_silu, s_grs, s_y = lsem("s_sig"), lsem("s_silu"), lsem("s_grs"), lsem("s_y")
        s_acc, s_adap, s_mod = lsem("s_acc"), lsem("s_adap"), lsem("s_mod")
        s_yp, s_oThi, s_oT = lsem("s_yp"), lsem("s_oThi"), lsem("s_oT")
        s_out, s_x, s_sq, s_sqa, s_ms, s_rb = (lsem(n) for n in ("s_out", "s_x", "s_sq", "s_sqa", "s_ms", "s_rb"))
        s_cast, s_swap = lsem("s_cast"), lsem("s_swap")
        d_link, a_link = lsem("d_link"), lsem("a_link")
        nums = [s.num for s in layer_sems]
        assert nums == list(range(nums[0], nums[0] + len(nums)))

        def linker(eng, s):
            count = [0]

            def link(ins):
                count[0] += 1
                ins.then_inc(s, 1)
                eng.wait_ge(s, count[0])
            return link

        PER_RING = 16 * (NR // RING)

        def raw(u):
            return ring[:, (FIRST_UNITS + POS[u]) % RING, 0:unit_width(u)]

        def wait_raw(eng, layer, u):
            n = FIRST_UNITS + POS[u]
            eng.wait_ge(w_loaded[n % RING], layer * PER_RING + 16 * (n // RING + 1))

        def wait_done(eng, layer, c):
            eng.wait_ge(w_done, layer * NSP + c + 1)

        def split_done(c):
            width = SPLIT[SPLIT_NAMES[c % NSP]][0]
            return [w[:, c % 2, 0:KD * width].rearrange("p (k c) -> p k c", k=KD) for w in (w_hi, w_lo)]

        def piece(c, p, view):
            n = KD * SPLIT[SPLIT_NAMES[c % NSP]][0] // PIECES
            return view[:, n * p:n * p + n]

        last_of = {n: steps_of(n)[-1] for n in SPLIT_NAMES}
        filler_steps = {s for n in FILLERS for s in steps_of(n)}
        BANK, before, user = {}, {}, {}
        for n, s in enumerate(STEPS):
            BANK[s] = 0 if s in filler_steps else n % 4
            before[s] = user.get(BANK[s])
            user[BANK[s]] = n
        N_PREP = sum(1 for s in STEPS if s not in filler_steps)

        def wait_step(eng, layer, s):
            if s == last_of[s[0]]:
                wait_done(eng, layer, SPLIT_NAMES.index(s[0]))
            else:
                eng.wait_ge(s_proj, sum(1 for q in STEPS[:STEP_NO[s] + 1] if q != last_of[q[0]]))

        SETUP_DVE = 1 + N_SS + 1
        block = ctx.enter_context(nc.Block())

        @block.sync
        def _(sp):
            sp.dma_start(prf[:], first).then_inc(first_loaded, 16)
            sp.dma_start(ring[:, 0, 0:KD * A1_W], w_first[:, N_SS * SLOT:FIRST_W]).then_inc(w_loaded[0], 16)
            for n in range(N_SS):
                if n + 1 == RING:
                    sp.dma_start(xT, x_t).then_inc(x_moved, 16)
                    sp.wait_ge(s_lo, PIECES)
                elif n + 1 > RING:
                    sp.wait_ge(setup_pe, n + 1 - RING)
                sp.dma_start(ring[:, (n + 1) % RING, :], w_first[:, n * SLOT:n * SLOT + SLOT])\
                    .then_inc(w_loaded[(n + 1) % RING], 16)
            sp.dma_start(prm[:], par[0]).then_inc(par_loaded, 16)
            sp.dma_start(cst[:], const).then_inc(const_loaded, 16)

            def used(layer, pos):
                if pos < 0:
                    if layer == 0:
                        sp.wait_ge(setup_pe, N_SS + pos + 1)
                        return
                    layer, pos = layer - 1, NR + pos
                kind, n = RING_UNITS[pos]
                if kind == "split":
                    sp.wait_ge(s_lo, PIECES * (layer * NSP + n + 1))
                elif kind == "ada":
                    sp.wait_ge(w_ada, N_SS + layer * (N_GATE + N_SS) + n + 1)
                else:
                    sp.wait_ge(w_direct, layer * 4 + ["uq", "ukv", "cmpk", "cmpv"].index(kind) + 1)

            def load(layer, pos):
                used(layer, pos - RING)
                n = (FIRST_UNITS + pos) % RING
                sp.dma_start(ring[:, n, 0:WIDTHS[pos]], w_all[layer, :, OFFSETS[pos]:OFFSETS[pos] + WIDTHS[pos]])\
                    .then_inc(w_loaded[n], 16)

            for layer in range(DEPTH):
                for pos in range(RING if layer else 0, NR - 2):
                    load(layer, pos)
                if layer:
                    sp.wait_ge(x_moved, layer * 16 * (KD + 1) + 16)
                sp.wait_ge(s_y, 4)
                sp.dma_start(xT, x_t if layer == 0 else xs).then_inc(x_moved, 16)
                for pos in range(NR - 2, NR):
                    load(layer, pos)
                if layer + 1 < DEPTH:
                    for pos in range(RING):
                        load(layer + 1, pos)
                    for k in range(KD):
                        sp.wait_ge(s_x, k + 1)
                        sp.dma_start(xs[:, k, :], xT[:, k, :]).then_inc(x_moved, 16)
                sp.sem_inc(arrived, 1)
                sp.wait_ge(go, layer + 1)
                if layer + 1 < DEPTH:
                    sp.dma_start(prm[:], par[layer + 1]).then_inc(par_loaded, 16)
            for k in range(KD):
                sp.wait_ge(fin_out, k + 1)
                sp.dma_start(y_t[:, k, :], xT[:, k, :]).then_inc(y_stored, 16)
            sp.wait_ge(y_stored, 16 * KD)

        @block.tensor
        def _(pe):
            mm, tp = nc.tensor.matmul, nc.tensor.transpose
            free = {}

            def take(banks, *by):
                for b in dict.fromkeys(free[b] for b in banks if b in free):
                    pe.wait_ge(*b)
                for b, f in zip(banks, by * len(banks) if len(by) == 1 else by):
                    free[b] = f

            def three(out, lhs, rhs, k, start, stop):
                mm(out, lhs[0][k], rhs[0][k], start=start, stop=False)
                mm(out, lhs[0][k], rhs[1][k], start=False, stop=False)
                return mm(out, lhs[1][k], rhs[0][k], start=False, stop=stop)

            def operands(s):
                name, i, how = s
                ws = split_done(SPLIT_NAMES.index(name))
                hs = (h_hi, h_lo)
                if how == "c":
                    return ([[w[:, k, P * i:P * i + P] for k in range(KD)] for w in ws],
                            [[h[:, k, :] for k in range(KD)] for h in hs])
                return ([[h[:, k, P * i:P * i + P] for k in range(KD)] for h in hs],
                        [[w[:, k, :] for k in range(KD)] for w in ws])

            def bank_out(s):
                n = SPLIT[s[0]][0] if s[2] == "t" else SEQ
                return ps[:, BANK[s], 0:n]

            def finish_step(last, s):
                last.then_inc(w_done if s == last_of[s[0]] else s_proj, 1)

            def proj(layer, s, k0, k1):
                name = s[0]
                if k0 == 0:
                    if s == steps_of(name)[0]:
                        pe.wait_ge(s_lo, layer * (PIECES * NSP) + PIECES * (SPLIT_NAMES.index(name) + 1))
                    if before[s] is not None:
                        pe.wait_ge(s_evac, before[s] + 1)
                        if STEPS[before[s]][0] == "IQ":
                            pe.wait_ge(s_ikT, 1)
                if s[2] == "v":
                    for i in range(NB):
                        last = tp(ps[:, BANK[s], P * i:P * i + P], nvT[:, P * i:P * i + P], ident)
                    return finish_step(last, s)
                lhs, rhs = operands(s)
                for k in range(k0, k1):
                    last = three(bank_out(s), lhs, rhs, k, k == 0, k == KD - 1)
                if k1 == KD:
                    finish_step(last, s)

            def first_unit(layer):
                pe.wait_ge(s_lo, layer * (PIECES * NSP) + PIECES)
                for k in range(KD):
                    pe.wait_ge(s_h, k + 1)
                    for s in steps_of("A1"):
                        lhs, rhs = operands(s)
                        last = three(bank_out(s), lhs, rhs, k, k == 0, k == KD - 1)
                        if k == KD - 1:
                            finish_step(last, s)

            def ik(layer):
                take([4], (s_ikT, 2))
                pe.wait_ge(s_ikd, 1)
                for i in range(NB):
                    last = tp(ps[:, 4, P * i:P * i + P], ikd[:, i].rearrange("p g c -> p (g c)"), ident)
                last.then_inc(s_ikp, 1)

            def idx(layer, i):
                if i == 1:
                    pe.wait_ge(s_ikT, 2)
                    pe.wait_ge(s_evac, STEP_NO[last_of["IQ"]] + 1)
                w = P * (i + 1)
                for h in range(H):
                    take([4 + h], (s_relu, H * (i - 1) + h + 1))
                    r = slice(32 * h, 32 * h + 32)
                    lhs = [[t[r, P * i:P * i + P]] for t in iqr]
                    rhs = [[t[r, 0:w]] for t in ikr]
                    three(ps[:, 4 + h, 0:w], lhs, rhs, 0, True, True).then_inc(s_idx, 1)

            def foxT(layer):
                take([7], (s_fcum, 1))
                pe.wait_ge(s_fls, 1)
                for i in range(NB):
                    last = tp(ps[0:H, 7, P * i:P * i + P], fls[:, i, :], ident)
                last.then_inc(s_flp, 1)

            def lat(layer):
                pe.wait_ge(par_loaded, layer * 16 + 16)
                pe.wait_ge(const_loaded, 16)
                take([4, 5, 6], (s_latT, 1), (s_latT, 2), (s_latT, 3))
                pe.wait_ge(s_lat, 1)
                for i in range(NB):
                    tp(ps[:, 4, P * i:P * i + P], qn[:, i, 0:P], ident)
                    tp(ps[0:Q_LORA - P, 5, P * i:P * i + P], qn[:, i, P:Q_LORA], ident)
                    last = tp(ps[:, 6, P * i:P * i + P], kn[:, i, :], ident)
                last.then_inc(s_latp, 1)

            def uq(layer):
                wait_raw(pe, layer, ("uq", 0))
                pe.wait_ge(s_latT, 2)
                w = raw(("uq", 0))
                for i in range(NB):
                    take([4 + i], (s_uqe, i + 1))
                    mm(ps[:, 4 + i, 0:H * QK_W], qlT[0][:, P * i:P * i + P], w[:, 0:H * QK_W], start=True, stop=False)
                    last = mm(ps[:, 4 + i, 0:H * QK_W], qlT[1][0:64, P * i:P * i + P], w[0:64, H * QK_W:2 * H * QK_W],
                              start=False, stop=True)
                    last.then_inc(s_uq if i < NB - 1 else w_direct, 1)

            def ukv(layer):
                wait_raw(pe, layer, ("ukv", 0))
                pe.wait_ge(s_latT, 3)
                for i in range(NB):
                    take([4 + i], (s_ukve, i + 1))
                    last = mm(ps[:, 4 + i, :], klT[:, P * i:P * i + P], raw(("ukv", 0)), start=True, stop=True)
                    last.then_inc(s_ukv if i < NB - 1 else w_direct, 1)

            def hid(layer):
                take([4], (s_hid, 2))
                pe.wait_ge(s_blk, 2)
                for s, u in enumerate((("cmpk", 0), ("cmpv", 0))):
                    wait_raw(pe, layer, u)
                    w = raw(u).rearrange("p (j c) -> p j c", j=CMP_J)
                    for j in range(CMP_J):
                        last = mm(ps[0:HD, 4, NCP * s:NCP * s + N_CMP], w[:, j, :], blk[:, s, j, :],
                                  start=j == 0, stop=j == CMP_J - 1)
                    last.then_inc(w_direct, 1)

            def kc(layer):
                pe.wait_ge(s_hid, 2)
                mm(ps[:, MISC, 0:N_CMP], par_("w2k")[0:HD, :], hidk[:, 0:N_CMP], start=True, stop=True)
                mm(ps[:, MISC, P:P + HD], hidv[:, :, :].rearrange("p g n -> p (g n)"), par_("w2v")[0:HD, :],
                   start=True, stop=True).then_inc(s_kcp, 1)

            def heads(src, made, done):
                for h in range(H):
                    take([4 + h], (done, h + 1))
                    for i in range(NB):
                        last = tp(ps[0:QK_W, 4 + h, P * i:P * i + P], src[:, i, h, :], ident)
                    last.then_inc(made, 1)

            def mqT(layer):
                pe.wait_ge(s_rope, 1)
                heads(q_tm, s_mqp, s_mq)

            def mkT(layer):
                pe.wait_ge(s_rope, 2)
                heads(k_tm, s_mkp, s_mk)

            def fbT(layer, h):
                pe.wait_ge(s_kc, 2) if h == 0 else pe.wait_ge(s_fb, h)
                mm(ps[:, MISC, :], selrow[0:H, h, :], fcum, start=True, stop=True).then_inc(s_fbp, 1)

            def cs(layer, odd):
                if odd:
                    pe.wait_ge(s_cs, 1)
                else:
                    pe.wait_ge(s_fb, H)
                    pe.wait_ge(s_evac, STEP_NO[last_of["NQ"]] + 1)
                for i in range(NB):
                    for h in (odd, odd + 2):
                        r = slice(64 * odd, 64 * odd + 64)
                        c = odd * 256 + (i * 2 + h // 2) * NCP
                        last = mm(ps[:, MISC, c:c + N_CMP], nq[r, h // 2, P * i:P * i + P], kc2[r, 0:N_CMP],
                                  start=True, stop=True)
                last.then_inc(s_cs, 1)

            def cmp_turn(layer):
                pe.wait_ge(s_csum, 1)
                pe.wait_ge(s_pc, 1)
                for i in range(NB):
                    last = tp(ps[:, MISC, P * i:P * i + P], pc[:, i].rearrange("p h n -> p (h n)"), ident)
                last.then_inc(s_pctp, 1)

            def cmp_values(layer, half):
                pe.wait_ge(s_pct, 1) if half == 0 else pe.wait_ge(s_co, 1)
                for i in (2 * half, 2 * half + 1):
                    c = (i % 2) * GW
                    last = mm(ps[:, MISC, c:c + GW], pct[:, i, :], vcd[:, :, :].rearrange("p h e -> p (h e)"),
                              start=True, stop=True)
                last.then_inc(s_cpv, 1)

            def scores(u):
                m, i, h = UNITS[u]
                n, w = 2 + u % 2, P * (i + 1)
                q = slice(P * i, P * i + P)
                r = slice(64 * (h % 2), 64 * (h % 2) + 64)
                lhs, rhs = {"mla": (mq[0:QK_W, h, q], mk[0:QK_W, h, 0:w]),
                            "fox": (fq[r, h // 2, q], fk[r, h // 2, 0:w]),
                            "dsa": (dq[r, h // 2, q], dk[r, h // 2, 0:w]),
                            "sel": (nq[r, h // 2, q], sw_k[h % 2][r, 0:w]),
                            "win": (nq[r, h // 2, q], sw_k[1 - h % 2][r, 0:w])}[m]
                if u >= 2:
                    pe.wait_ge(s_ttr, u - 1)
                if (i, h) == (0, 0):
                    if m == "mla":
                        pe.wait_ge(s_mk, H)
                        pe.wait_ge(s_evac, N_PREP)
                    elif m == "sel":
                        pe.wait_ge(s_swap, 1)
                    elif m != "win":
                        pe.wait_ge(s_evac, STEP_NO[last_of["FK" if m == "fox" else "DK"]] + 1)
                if m == "dsa" and i > 0:
                    pe.wait_ge(s_selm, i)
                if m == "fox" and (i, h) == (0, 0):
                    pe.wait_ge(s_cast, 1)
                masked = m == "fox" or (m == "dsa" and i > 0)
                last = mm(ps[:, n, 0:w], lhs, rhs, start=True, stop=not masked)
                if m == "fox":
                    last = mm(ps[:, n, w - P:w], identb[:, :], maskb[:, :], start=False, stop=True)
                elif masked:
                    last = mm(ps[:, n, 0:w], identb[:, :], selm[i][:, :], start=False, stop=True)
                last.then_inc(s_sc, 1)

            def turn(u):
                _, i, _ = UNITS[u]
                pe.wait_ge(s_exp, u + 1)
                if u == 0:
                    pe.wait_ge(s_relu, H * (NB - 1))
                if u >= 2:
                    pe.wait_ge(s_pta if u % 2 == 0 else s_ptd, u // 2)
                for j in range(i + 1):
                    last = tp(ps[:, 4 + u % 2, P * j:P * j + P], pr_[u % 3][:, P * j:P * j + P], ident)
                last.then_inc(s_tr, 1)

            def values(u):
                m, i, h = UNITS[u]
                g = u // H
                pe.wait_ge(s_pta if u % 2 == 0 else s_ptd, u // 2 + 1)
                if h == 0 and g >= 2:
                    pe.wait_ge(s_norm, g - 1)
                if (i, h) == (0, 0) and m in ("fox", "sel", "dsa"):
                    pe.wait_ge(s_evac, STEP_NO[last_of[{"fox": "FV", "sel": "SW", "dsa": "DV"}[m]]] + 1)
                for j in range(i + 1):
                    v = {"mla": v_tm[:, j, HD * h:HD * h + HD], "fox": fv[:, j, HD * h:HD * h + HD],
                         "dsa": dv[:, j, HD * h:HD * h + HD], "sel": nv[:, j, 0:HD], "win": nv[:, j, HD:2 * HD]}[m]
                    c = HD * h
                    last = mm(ps[:, 6 + g % 2, c:c + HD], pt[u % 2][:, P * j:P * j + P], v, start=j == 0, stop=j == i)
                last.then_inc(s_pv, 1)

            def unit(layer, t):
                if t < NUN:
                    scores(t)
                if 2 <= t < NUN + 2:
                    turn(t - 2)
                if t >= 3:
                    values(t - 3)

            def adasum(layer, n):
                pe.wait_ge(s_acc, n + 1)
                if n:
                    pe.wait_ge(s_mod, n)
                else:
                    pe.wait_ge(s_co, 2)
                for m in range(2):
                    last = mm(ps[:, MISC, m:m + 1], acc[:, n % 2, P * m:P * m + P], one, start=True, stop=True)
                last.then_inc(s_adap, 1)

            def yT(layer, k):
                j = CT_ORDER.index(k)
                pe.wait_ge(s_y, 3 if j < 6 else 4)
                if j < 2:
                    pe.wait_ge(s_ttr, NUN - 1 + j)
                else:
                    pe.wait_ge(s_oT, j - 1)
                for i in range(NB):
                    last = tp(ps[:, 2 + j % 2, P * i:P * i + P], o_sb[:, i, P * k:P * k + P], ident)
                last.then_inc(s_yp, 1)

            def out(layer, n, k0, k1):
                c = NSP - 4 + n // 2
                if k0 == 0 and n == 0:
                    pe.wait_ge(s_evac, len(STEPS))
                    pe.wait_ge(s_mod, N_GATE + N_SS)
                if k0 == 0 and n % 2 == 0:
                    pe.wait_ge(s_lo, layer * (PIECES * NSP) + PIECES * (c + 1))
                if n == 2:
                    pe.wait_ge(s_oT, KD)
                if k0 == 0 and n >= 4:
                    pe.wait_ge(s_x, n - 3)
                ws = split_done(c)
                for j in range(k0, k1):
                    k = CT_ORDER[j]
                    pe.wait_ge(s_oT, j + 1)
                    lhs = [[w[:, k, P * (n % 2):P * (n % 2) + P]] for w in ws]
                    rhs = [[h[:, k, :]] for h in (h_hi, h_lo)]
                    last = three(ps[:, n % 4, :], lhs, rhs, 0, j == 0, j == KD - 1)
                if k1 == KD:
                    last.then_inc(w_done if n % 2 else s_out, 1)

            def rms(layer):
                pe.wait_ge(s_sqa, KD - 2)
                mm(ps[:, 7, :], fst("mean"), sqa[:, :], start=True, stop=False)
                pe.wait_ge(s_sq, KD)
                mm(ps[:, 7, :], fst("mean"), sqr[(KD - 1) % 2][:, :], start=False, stop=True).then_inc(s_ms, 1)

            do = {"first": first_unit, "proj": proj, "ik": ik, "idx": idx, "foxT": foxT, "lat": lat, "uq": uq,
                  "ukv": ukv, "hid": hid, "kc": kc, "mq": mqT, "mk": mkT, "fb": fbT, "cs": cs, "cturn": cmp_turn,
                  "cval": cmp_values, "unit": unit, "adasum": adasum, "yT": yT, "out": out, "rms": rms}

            pe.wait_ge(first_loaded, 16)
            for n in range(N_SS):
                if n == N_SS - 1:
                    pe.wait_ge(setup_sq, KD - 1)
                    mm(ps[:, 6, :], fst("mean"), xg[:, 0, :], start=True, stop=True).then_inc(setup_ms, 1)
                pe.wait_ge(w_loaded[(n + 1) % RING], 16 * ((n + 1) // RING + 1))
                pe.wait_ge(setup_dve, 1 + n)
                w = ring[:, (n + 1) % RING, :].rearrange("p (k c) -> p k c", k=KD)
                for m in range(2):
                    for k in range(DVE_TILES, KD):
                        mm(ps[:, 7, m:m + 1], w[:, k, P * m:P * m + P], sc[:, k:k + 1], start=k == DVE_TILES, stop=False)
                    if m == 0:
                        pe.wait_ge(w_ada, n + 1)
                    last = mm(ps[:, 7, m:m + 1], acc[:, n % 2, P * m:P * m + P], one, start=False, stop=True)
                last.then_inc(setup_pe, 1)
            pe.wait_ge(setup_dve, SETUP_DVE)
            pe.wait_ge(setup_fill, 3)
            with pe.Fori(0, DEPTH) as layer:
                for kind, *args in MAIN:
                    if kind in do:
                        do[kind](layer, *args)
                pe.sem_inc(arrived, 1)
                pe.wait_ge(go, layer + 1)

        @block.scalar
        def _(act):
            a, cp = nc.scalar.activation, nc.scalar.copy
            lo, hi = slice(0, 64), slice(64, P)

            def split(layer, c, p, wait=True):
                if wait and p == 0:
                    wait_raw(act, layer, ("split", c))
                    if c >= 2:
                        wait_done(act, layer, c - 2)
                src = raw(("split", c)) if wait else ring[:, 0, :]
                cp(piece(c, p, w_hi[:, c % 2, :]), piece(c, p, src)).then_inc(s_hi, 1)

            def norm(layer):
                for k in range(KD):
                    act.wait_ge(s_xg, k + 1)
                    a(h_hi[:, k, :], xg[:, k, :], ACT.Identity, bias=mod[:, k:k + 1]).then_inc(s_hhi, 1)

            def evac(layer, s, k0, k1):
                if k1 < KD:
                    return
                name, i, how = s
                wait_step(act, layer, s)
                bank = ps[:, BANK[s], :]
                if name == "A1":
                    last = cp(tm[:, i, 0:A1_W], bank[:, 0:A1_W])
                elif name == "A2":
                    last = cp(tm[:, i, A1_W:TM_W], bank[:, 0:A2_W])
                elif name == "IQ":
                    last = cp(iqr[0][:, :], bank)
                elif name == "CM":
                    cp(cmp2[lo, 0, :], bank[lo, :])
                    cp(cmp2[hi, 0, 0:SEQ - 1], bank[lo, 1:SEQ])
                    cp(cmp2[lo, 1, :], bank[hi, :])
                    last = cp(cmp2[hi, 1, 0:SEQ - 1], bank[hi, 1:SEQ])
                elif name == "SW" and i == 0:
                    cp(sw_k[0], bank).then_inc(s_evac, 1)
                    act.wait_ge(s_evac, STEP_NO[s] + 1)
                    cp(sw_k[1][lo, :], sw_k[0][hi, :])
                    cp(sw_k[1][hi, :], sw_k[0][lo, :]).then_inc(s_swap, 1)
                    return
                elif name == "SW" and i == 1:
                    last = cp(nvT, bank)
                elif name == "SW":
                    last = cp(nv[:, :, :].rearrange("p i c -> p (i c)"), bank)
                elif how == "c":
                    last = cp({"FQ": fq, "FK": fk, "DQ": dq, "DK": dk, "NQ": nq}[name][:, i, :], bank)
                elif name == "FV":
                    last = cp(fv[:, i, :], bank[:, 0:GW])
                elif name == "DV":
                    last = cp(dv[:, i, :], bank[:, 0:GW])
                else:
                    g = int(name[2])
                    if i == 0 and g == 2:
                        act.wait_ge(s_silu, 2)
                    a(ez_of[g][:, i, :], bank[:, 0:GW], ACT.Exp, scale=-1.0)
                    last = cp(sz[:, i, GW * g:GW * g + GW], bank[:, 0:GW])
                last.then_inc(s_evac, 1)

            def first_unit(layer):
                for s in steps_of("A1"):
                    evac(layer, s, 0, KD)

            def latr(layer):
                act.wait_ge(s_fa, 1)
                link(a(fe[:, :, :], fa[:, :, :], ACT.Exp, scale=-1.0))
                a(fl[:, :, :], fe[:, :, :], ACT.Ln, bias=1.0).then_inc(s_fl, 1)
                act.wait_ge(s_gd, 1)
                a(ge[:, :, :, :], gd[:, :, :, :], ACT.Exp).then_inc(s_ge, 1)
                act.wait_ge(s_lss, 1)
                a(llr[:, 0, :], lss[:, 0, :], ACT.Ln, bias=eps, scale=1.0 / Q_LORA)
                link(a(llr[:, 1, :], lss[:, 1, :], ACT.Ln, bias=eps, scale=1.0 / KV_LORA))
                a(lss[:, :, :], llr[:, :, :], ACT.Exp, scale=-0.5).then_inc(s_llr, 1)

            def ik(layer):
                act.wait_ge(s_ikp, 1)
                cp(ikr[0][:, :], ps[:, 4, :]).then_inc(s_ikh, 1)

            def idx(layer, i):
                w = P * (i + 1)
                for h in range(H):
                    act.wait_ge(s_idx, H * (i - 1) + h + 1)
                    if i > 1:
                        act.wait_ge(s_isc, H * (i - 2) + h + 1)
                    a(rl[:, h, 0:w], ps[:, 4 + h, 0:w], ACT.Relu, scale=H ** -0.5).then_inc(s_relu, 1)

            def lat(layer):
                act.wait_ge(s_latp, 1)
                act.wait_ge(par_loaded, layer * 16 + 16)
                g = par_("q_g")
                a(qlT[0], ps[:, 4, :], ACT.Copy, scale=g[:, 0:1]).then_inc(s_latT, 1)
                a(qlT[1][0:64, :], ps[0:64, 5, :], ACT.Copy, scale=g[0:64, 1:2]).then_inc(s_latT, 1)
                a(klT, ps[:, 6, :], ACT.Copy, scale=par_("kv_g")).then_inc(s_latT, 1)

            def uq(layer):
                for i in range(NB):
                    if i < NB - 1:
                        act.wait_ge(s_uq, i + 1)
                    else:
                        act.wait_ge(w_direct, layer * 4 + 1)
                    cp(q_tm[:, i].rearrange("p h e -> p (h e)"), ps[:, 4 + i, 0:H * QK_W]).then_inc(s_uqe, 1)

            def ukv(layer):
                for i in range(NB):
                    if i < NB - 1:
                        act.wait_ge(s_ukv, i + 1)
                    else:
                        act.wait_ge(w_direct, layer * 4 + 2)
                    kv = ps[:, 4 + i, :].rearrange("p (h e) -> p h e", h=H)
                    cp(k_tm[:, i, :, 0:HD], kv[:, :, 0:HD])
                    cp(v_tm[:, i].rearrange("p (h e) -> p h e", h=H), kv[:, :, HD:2 * HD]).then_inc(s_ukve, 1)

            def hid(layer):
                act.wait_ge(w_direct, layer * 4 + 4)
                hp = ps[0:HD, 4, 0:2 * NCP].rearrange("p (s n) -> p s n", s=2)[:, :, 0:N_CMP]
                a(hide[:, :, 0:N_CMP], hp, ACT.Exp, scale=-1.0).then_inc(s_hide, 1)

            def kc(layer):
                act.wait_ge(s_kcp, 1)
                cp(kc2[:, 0:N_CMP], ps[:, MISC, 0:N_CMP]).then_inc(s_kc, 1)
                for h in range(H):
                    r = slice(NCP * h, NCP * h + NCP)
                    last = cp(vcd[r, h, :], ps[r, MISC, P:P + HD])
                last.then_inc(s_kc, 1)

            def heads(dst, made, done):
                for h in range(H):
                    act.wait_ge(made, h + 1)
                    cp(dst[0:QK_W, h, :], ps[0:QK_W, 4 + h, :]).then_inc(done, 1)

            def fbT(layer, h):
                act.wait_ge(s_isc, H * (NB - 1))
                act.wait_ge(s_fbp, h + 1)
                cp(fb[:, h, :], ps[:, MISC, :]).then_inc(s_fb, 1)

            def csoft(layer):
                act.wait_ge(s_csub, 1)
                a(pc[:, :, :, 0:N_CMP], pc[:, :, :, 0:N_CMP], ACT.Exp).then_inc(s_cexp, 1)

            def cmp_turn(layer):
                act.wait_ge(s_pctp, 1)
                cp(pct, ps[:, MISC, :].rearrange("p (i q) -> p i q", i=NB)).then_inc(s_pct, 1)

            def unit(layer, t):
                if t < NUN:
                    w = P * (UNITS[t][1] + 1)
                    buf = pr_[t % 3][:, 0:w]
                    act.wait_ge(s_ttr, t + 1)
                    a(buf, buf, ACT.Exp, bias=nmx[:, t:t + 1], scale=-1.0, accum_out=rsum[:, t:t + 1]).then_inc(s_exp, 1)
                u = t - 2
                if 0 <= u < NUN and u % 2 == 0:
                    w = P * (UNITS[u][1] + 1)
                    act.wait_ge(s_tr, u + 1)
                    if u >= 2:
                        act.wait_ge(s_pv, u - 1)
                    cp(pt[0][:, 0:w], ps[:, 4, 0:w]).then_inc(s_pta, 1)

            def sigmoid(layer, g):
                act.wait_ge(s_evac, STEP_NO[last_of[f"GZ{g}"]] + 1)
                link(a(ez_of[g], ez_of[g], ACT.Ln, bias=1.0))
                a(ez_of[g], ez_of[g], ACT.Exp, scale=-1.0).then_inc(s_sig, 1)

            gn_order = {0: 1, 1: 2, 3: 3, 2: 4}

            def group_norm(layer, m):
                act.wait_ge(s_norm, {0: 4, 1: 8, 3: 16, 2: 20}[m])
                for i in range(NB):
                    last = a(squares, o_sb[:, i, GW * m:GW * m + GW].rearrange("p (a b) -> p a b", a=2), ACT.Square, accum_out=gss[:, m, i:i + 1])
                    link(last)
                link(a(gln[:, m, :], gss[:, m, :], ACT.Ln, bias=eps, scale=1.0 / GW))
                a(grs[:, m, :], gln[:, m, :], ACT.Exp, scale=-0.5).then_inc(s_grs, 1)

            def yT(layer, k):
                act.wait_ge(s_yp, CT_ORDER.index(k) + 1)
                j = CT_ORDER.index(k)
                a(h_hi[:, k, :], ps[:, 2 + j % 2, :], ACT.Copy, scale=par_("out_g")[:, k:k + 1]).then_inc(s_oThi, 1)

            def x(layer, k):
                act.wait_ge(s_x, k + 1)
                if k >= 3:
                    act.wait_ge(s_sqa, k - 2)
                dst = sqa if k == 0 else sqr[k % 2]
                a(dst[:, :], xT[:, k, :], ACT.Square).then_inc(s_sq, 1)

            def rms(layer):
                act.wait_ge(s_ms, 1)
                link(a(rb[:, :], ps[:, 7, :], ACT.Ln, bias=eps))
                link(a(rb[:, :], rb[:, :], ACT.Exp, scale=-0.5))

            do = {"split": split, "norm": norm, "first": first_unit, "proj": evac, "latr": latr, "ik": ik, "idx": idx,
                  "lat": lat, "uq": uq, "ukv": ukv, "hid": hid, "kc": kc,
                  "mq": lambda layer: heads(mq, s_mqp, s_mq), "mk": lambda layer: heads(mk, s_mkp, s_mk),
                  "fb": fbT, "csoft": csoft, "cturn": cmp_turn, "unit": unit, "sig": sigmoid, "gss": group_norm, "yT": yT, "x": x, "rms": rms}

            nc.scalar.preload_act_table_set("natural_log_exp_and_others")
            act.wait_ge(first_loaded, 16)
            a(sct[:, :], fst("c"), ACT.Exp, scale=-1.0).then_inc(setup_act, 1)
            act.wait_ge(w_loaded[0], 16)
            for p in range(PIECES):
                split(0, 0, p, wait=False)
            act.wait_ge(x_moved, 16)
            for k in range(KD):
                a(xg[:, k, :], xT[:, k, :], ACT.Square).then_inc(setup_act, 1)
            act.wait_ge(setup_ms, 1)
            a(rb[:, :], ps[:, 6, :], ACT.Ln, bias=eps).then_inc(setup_act, 1)
            act.wait_ge(setup_act, KD + 2)
            a(rb[:, :], rb[:, :], ACT.Exp, scale=-0.5).then_inc(setup_act, 1)
            act.wait_ge(setup_dve, SETUP_DVE)
            act.wait_ge(setup_fill, 3)
            with act.Fori(0, DEPTH) as layer:
                link = linker(act, a_link)
                for kind, *args in MAIN:
                    if kind in do:
                        do[kind](layer, *args)
                act.sem_inc(arrived, 1)
                act.wait_ge(go, layer + 1)

        @block.vector
        def _(dve):
            v = nc.vector

            def heads_of(ap):
                return ap.rearrange("p (h e) -> p h e", h=H)

            def norm(layer):
                for k in range(KD + 1):
                    if k < KD:
                        v.scalar_tensor_tensor(out=xg[:, k, :], in0=xT[:, k, :], scalar=gs[:, k:k + 1], in1=rb[:, :],
                                               op0=ALU.mult, op1=ALU.mult).then_inc(s_xg, 1)
                    if k:
                        dve.wait_ge(s_hhi, k)
                        v.scalar_tensor_tensor(out=h_lo[:, k - 1, :], in0=xg[:, k - 1, :], scalar=mod[:, k - 1:k],
                                               in1=h_hi[:, k - 1, :].bitcast(F32), op0=ALU.add,
                                               op1=ALU.subtract).then_inc(s_h, 1)

            def casts(layer):
                dve.wait_ge(const_loaded, 16)
                v.tensor_copy(identb[:, :], ident)
                v.tensor_copy(maskb[:, :], con("mask")[:, SEQ - P:SEQ]).then_inc(s_cast, 1)

            def latr(layer):
                dve.wait_ge(par_loaded, layer * 16 + 16)
                dve.wait_ge(s_evac, STEP_NO[last_of["A1"]] + 1)
                bf = par_("b_f").unsqueeze(1).broadcast_to([P, NB, H])
                link(v.tensor_tensor(fy[:, :, :], tm[:, :, C_FF:C_FF + H], bf, ALU.add))
                v.scalar_tensor_tensor(out=fa[:, :, :], in0=fy[:, :, :], scalar=-1.0, in1=fy[:, :, :],
                                       op0=ALU.mult, op1=ALU.max).then_inc(s_fa, 1)
                v.tensor_scalar(gd[:, :, :, :].rearrange("p i h b -> p i (h b)"), tm[:, :, C_NG:C_NG + 3 * H],
                                -1.0, 80.0, ALU.mult, ALU.min).then_inc(s_gd, 1)
                for i in range(NB):
                    link(v.tensor_tensor_reduce(squares_l[:, 0:Q_LORA], tm[:, i, 0:Q_LORA], tm[:, i, 0:Q_LORA], 1.0, 0.0,
                                                ALU.mult, ALU.add, lss[:, 0, i:i + 1]))
                dve.wait_ge(s_evac, STEP_NO[last_of["A2"]] + 1)
                for i in range(NB):
                    kvl = tm[:, i, C_KVL:C_KVL + KV_LORA]
                    link(v.tensor_tensor_reduce(squares_l[:, 0:KV_LORA], kvl, kvl, 1.0, 0.0, ALU.mult, ALU.add,
                                                lss[:, 1, i:i + 1]))
                dve.sem_inc(s_lss, 1)
                dve.wait_ge(x_moved, layer * (16 * (KD + 1)) + 16)
                v.tensor_copy(ikd, tm[:, :, C_IK:C_IK + 32].unsqueeze(2).broadcast_to([P, NB, H, 32])).then_inc(s_ikd, 1)
                dve.wait_ge(s_fl, 1)
                v.scalar_tensor_tensor(out=fls[:, :, :], in0=fy[:, :, :], scalar=0.0, in1=fl[:, :, :],
                                       op0=ALU.min, op1=ALU.subtract).then_inc(s_fls, 1)
                dve.wait_ge(s_llr, 1)
                v.tensor_tensor(qn, tm[:, :, 0:Q_LORA], lss[:, 0, :].unsqueeze(2).broadcast_to([P, NB, Q_LORA]), ALU.mult)
                v.tensor_tensor(kn, tm[:, :, C_KVL:C_KVL + KV_LORA],
                                lss[:, 1, :].unsqueeze(2).broadcast_to([P, NB, KV_LORA]), ALU.mult).then_inc(s_lat, 1)
                dve.wait_ge(s_ge, 1)
                link(v.tensor_scalar(gd[:, :, :, :], ge[:, :, :, :], 1.0, None, ALU.add))
                v.reciprocal(gsig[:, :, :, :], gd[:, :, :, :]).then_inc(s_gsig, 1)

            def ik(layer):
                dve.wait_ge(s_ikh, 1)
                v.tensor_tensor(ikr[1][:, :], ps[:, 4, :], ikr[0][:, :].bitcast(F32), ALU.subtract).then_inc(s_ikT, 1)

            def evac(layer, s, k0, k1):
                if s[0] == "IQ" and k1 == KD:
                    dve.wait_ge(s_evac, STEP_NO[s] + 1)
                    v.tensor_tensor(iqr[1][:, :], ps[:, BANK[s], :], iqr[0][:, :].bitcast(F32), ALU.subtract)\
                        .then_inc(s_ikT, 1)

            def blocks(layer):
                dve.wait_ge(s_evac, STEP_NO[last_of["CM"]] + 1)
                pos = par_("pos").rearrange("p (s j) -> p s j", s=2)
                for s in range(2):
                    src = bass.AP(tensor=cmp2[:, s, :].tensor, offset=cmp2[:, s, :].offset,
                                  ap=[cmp2[:, s, :].ap[0], [2, CMP_J], [CMP_STRIDE, N_CMP]])
                    v.tensor_tensor(blk[:, s], src, pos[:, s, :].unsqueeze(2).broadcast_to([P, CMP_J, N_CMP]),
                                    ALU.add).then_inc(s_blk, 1)

            def rope(x1, x2, y1, y2):
                cb, sb_ = cosv.broadcast_to([P, NB, H, 16]), sinv.broadcast_to([P, NB, H, 16])
                v.tensor_tensor(rt[0], x1, cb, ALU.mult)
                v.tensor_tensor(rt[1], x2, sb_, ALU.mult)
                v.tensor_tensor(rt[2], x1, sb_, ALU.mult)
                link(v.tensor_tensor(rt[3], x2, cb, ALU.mult))
                v.tensor_tensor(y1, rt[0], rt[1], ALU.subtract)
                v.tensor_tensor(y2, rt[2], rt[3], ALU.add).then_inc(s_rope, 1)

            def uq(layer):
                dve.wait_ge(s_uqe, NB)
                x1, x2 = q_tm[:, :, :, HD:HD + 16], q_tm[:, :, :, HD + 16:HD + 32]
                rope(x1, x2, x1, x2)
                dve.wait_ge(s_rope, 1)

            def ukv(layer):
                k1 = tm[:, :, C_KR:C_KR + 16].unsqueeze(2).broadcast_to([P, NB, H, 16])
                k2 = tm[:, :, C_KR + 16:C_KR + 32].unsqueeze(2).broadcast_to([P, NB, H, 16])
                dve.wait_ge(s_ukve, NB)
                rope(k1, k2, k_tm[:, :, :, HD:HD + 16], k_tm[:, :, :, HD + 16:HD + 32])

            def foxT(layer):
                dve.wait_ge(s_flp, 1)
                v.tensor_tensor_scan(fcum, one[0:H, :].broadcast_to([H, SEQ]), ps[0:H, 7, :], 0.0, ALU.mult,
                                     ALU.add).then_inc(s_fcum, 1)

            def idx(layer, i):
                w = P * (i + 1)
                for h in range(H):
                    dve.wait_ge(s_relu, H * (i - 1) + h + 1)
                    before_ = con("mask")[:, SEQ - w:SEQ] if h == 0 else work[i][:, :]
                    v.scalar_tensor_tensor(out=work[i][:, :], in0=rl[:, h, 0:w],
                                           scalar=tm[:, i, C_IW + h:C_IW + h + 1], in1=before_,
                                           op0=ALU.mult, op1=ALU.add).then_inc(s_isc, 1)
                    dve.wait_ge(s_isc, H * (i - 1) + h + 1)

            def hid(layer):
                dve.wait_ge(s_hide, 1)
                hp = ps[0:HD, 4, 0:2 * NCP].rearrange("p (s n) -> p s n", s=2)[:, :, 0:N_CMP]
                link(v.tensor_scalar(hids[:, :, 0:N_CMP], hide[:, :, 0:N_CMP], 1.0, None, ALU.add))
                link(v.reciprocal(hidr[:, :, 0:N_CMP], hids[:, :, 0:N_CMP]))
                v.tensor_tensor(hidk[:, 0:N_CMP], hp[:, 0, :], hidr[:, 0, 0:N_CMP], ALU.mult).then_inc(s_hid, 1)
                v.tensor_tensor(hidv[:, :, 0:N_CMP], hp[:, 1:2, :].broadcast_to([HD, H, N_CMP]),
                                hidr[:, 1:2, 0:N_CMP].broadcast_to([HD, H, N_CMP]), ALU.mult).then_inc(s_hid, 1)

            tops = {}

            def top(layer, r, i):
                n = len(tops)
                tops[r, i] = n
                if r:
                    dve.wait_ge(s_top, 2 * tops[r - 1, i] + 2)
                v.max(top8[:, i, :], work[i][:, :]).then_inc(s_top, 1)
                dve.wait_ge(s_top, 2 * n + 1)
                v.match_replace(work[i][:, :], top8[:, i, :], work[i][:, :], TAKEN).then_inc(s_top, 1)

            def select(layer):
                dve.wait_ge(s_top, 2 * len(tops))
                for i in range(1, NB):
                    v.tensor_scalar(selm[i][:, :], work[i][:, :], LOWEST, MASKED, ALU.is_gt, ALU.mult).then_inc(s_selm, 1)

            def csoft(layer):
                cb = con("cmpb").rearrange("p (i h n) -> p i h n", i=NB, h=H)[:, :, :, 0:N_CMP]
                pcv = pc[:, :, :, 0:N_CMP]
                for b in range(2):
                    dve.wait_ge(s_cs, b + 1)
                    css = ps[:, MISC, 256 * b:256 * b + 256].rearrange("p (i h n) -> p i h n", i=NB, h=2)[:, :, :, 0:N_CMP]
                    last = v.tensor_tensor(pcv[:, :, b::2, :], css, cb[:, :, b::2, :], ALU.add)
                    if b == 0:
                        link(last)
                last.then_inc(s_csum, 1)
                dve.wait_ge(s_csum, 1)
                link(v.tensor_reduce(cmx[:, :, :], pcv, AX_X, ALU.max))
                link(v.tensor_tensor(pcv, pcv, cmx[:, :, :].unsqueeze(3).broadcast_to([P, NB, H, N_CMP]), ALU.subtract))
                v.tensor_scalar(pcv, pcv, HD ** -0.5, None, ALU.mult).then_inc(s_csub, 1)

            def cmp_turn(layer):
                dve.wait_ge(s_cexp, 1)
                link(v.tensor_reduce(cden[:, :, :], pc[:, :, :, 0:N_CMP], AX_X, ALU.add))
                link(v.reciprocal(crec[:, :, :], cden[:, :, :]))
                link(v.tensor_scalar(crec[:, 0, :], crec[:, 0, :], late, None, ALU.mult))
                v.tensor_tensor(cfac[:, :, :], crec[:, :, :], gsig[:, :, :, 0], ALU.mult).then_inc(s_pc, 1)
                dve.wait_ge(s_pc, 1)

            def cmp_out(layer, half):
                dve.wait_ge(s_cpv, half + 1)
                for i in (2 * half, 2 * half + 1):
                    o = heads_of(ps[:, MISC, (i % 2) * GW:(i % 2) * GW + GW])
                    fac = cfac[:, i].unsqueeze(2).broadcast_to([P, H, HD])
                    last = v.tensor_tensor(heads_of(o_sb[:, i, 3 * GW:4 * GW]), o, fac, ALU.mult)
                last.then_inc(s_co, 1)

            def normalise(g):
                m, i, _ = UNITS[H * g]
                c = slice(H * g, H * g + H)
                dve.wait_ge(s_pv, H * (g + 1))
                link(v.reciprocal(rinv[:, c], rsum[:, c]))
                fac = rinv[:, c]
                if m in ("sel", "win"):
                    link(v.tensor_tensor(rfac[:, c], rinv[:, c], gsig[:, i, :, 1 if m == "sel" else 2], ALU.mult))
                    fac = rfac[:, c]
                o = heads_of(ps[:, 6 + g % 2, 0:GW])
                dst = o_sb[:, i, OUT_COL[m]:OUT_COL[m] + GW]
                fac = fac.unsqueeze(2).broadcast_to([P, H, HD])
                if m in ("sel", "win"):
                    link(v.tensor_tensor(otmp, o, fac, ALU.mult))
                    v.tensor_tensor(heads_of(dst), heads_of(dst), otmp, ALU.add).then_inc(s_norm, 1)
                else:
                    v.tensor_tensor(heads_of(dst), o, fac, ALU.mult).then_inc(s_norm, 1)

            def unit(layer, t):
                if t < NUN:
                    m, i, h = UNITS[t]
                    w = P * (i + 1)
                    bias = {"mla": con("mask")[:, SEQ - w:SEQ], "fox": fb[:, h, 0:w]}.get(m, alibi[:, h, SEQ - w:SEQ])
                    dve.wait_ge(s_sc, t + 1)
                    if m == "fox" and i == 0:
                        dve.wait_ge(s_fb, h + 1)
                    if t >= 3:
                        dve.wait_ge(s_tr, t - 2)
                    scale = QK_W ** -0.5 if m == "mla" else HD ** -0.5
                    v.tensor_tensor_reduce(pr_[t % 3][:, 0:w], ps[:, 2 + t % 2, 0:w], bias, -scale, 3e38,
                                           ALU.add, ALU.min, nmx[:, t:t + 1]).then_inc(s_ttr, 1)
                u = t - 2
                if 0 <= u < NUN and u % 2 == 1:
                    w = P * (UNITS[u][1] + 1)
                    dve.wait_ge(s_tr, u + 1)
                    if u >= 2:
                        dve.wait_ge(s_pv, u - 1)
                    v.tensor_copy(pt[1][:, 0:w], ps[:, 5, 0:w]).then_inc(s_ptd, 1)
                if t >= 6 and (t - 2) % H == 0:
                    normalise((t - 2) // H - 1)

            silus = []

            def silu(layer, g):
                silus.append(g)
                dve.wait_ge(s_sig, len(silus))
                z = sz[:, :, GW * g:GW * g + GW]
                v.tensor_tensor(z, z, ez_of[g], ALU.mult).then_inc(s_silu, 1)

            grs_order = [0, 1, 3, 2]

            def gn(layer, m):
                dve.wait_ge(s_grs, grs_order.index(m) + 1)
                dve.wait_ge(s_silu, silus.index(m) + 1)
                for i in range(NB):
                    o = o_sb[:, i, GW * m:GW * m + GW]
                    last = v.scalar_tensor_tensor(out=o, in0=o, scalar=grs[:, m, i:i + 1],
                                                  in1=sz[:, i, GW * m:GW * m + GW], op0=ALU.mult, op1=ALU.mult)
                last.then_inc(s_y, 1)

            def ada_tiles(w, n, tiles, wait):
                dst = acc[:, n % 2, :]
                for k in tiles:
                    if k == 0:
                        last = v.tensor_scalar(dst, w[:, k, :], sc[:, k:k + 1], None, ALU.mult)
                    else:
                        last = v.scalar_tensor_tensor(out=dst, in0=w[:, k, :], scalar=sc[:, k:k + 1], in1=dst,
                                                      op0=ALU.mult, op1=ALU.add)
                    wait(last, k)

            def ada(layer, n, c):
                if c == 0:
                    wait_raw(dve, layer, ("ada", n))
                    if n >= 2:
                        dve.wait_ge(s_adap, n - 1)
                u = ("ada", n)

                def wait(last, k):
                    if k == KD - 1:
                        last.then_inc(w_ada, 1)
                        dve.wait_ge(w_ada, layer * (N_GATE + N_SS) + N_SS + n + 1)
                        dve.sem_inc(s_acc, 1)
                    else:
                        link(last)
                ada_tiles(raw(u).rearrange("p (k c) -> p k c", k=KD), n, (2 * c, 2 * c + 1), wait)

            def adasum(layer, n):
                dve.wait_ge(s_adap, n + 1)
                c = 2 * KD + 2 * n if n < N_GATE else 2 * (n - N_GATE)
                b = par_("b_gate")[:, 2 * n:2 * n + 2] if n < N_GATE else par_("b_next")[:, c:c + 2]
                v.tensor_tensor(mod[:, c:c + 2], ps[:, MISC, 0:2], b, ALU.add).then_inc(s_mod, 1)
                if n == N_GATE + N_SS - 1:
                    dve.wait_ge(s_mod, n + 1)
                    link(v.scalar_tensor_tensor(out=gs[:, :], in0=mod[:, KD:2 * KD], scalar=1.0, in1=par_("rms_next"),
                                                op0=ALU.add, op1=ALU.mult))

            def yT(layer, k):
                j = CT_ORDER.index(k)
                dve.wait_ge(s_oThi, j + 1)
                v.scalar_tensor_tensor(out=h_lo[:, k, :], in0=ps[:, 2 + j % 2, :], scalar=par_("out_g")[:, k:k + 1],
                                       in1=h_hi[:, k, :].bitcast(F32), op0=ALU.mult, op1=ALU.subtract).then_inc(s_oT, 1)

            def x(layer, k):
                if k % 2 == 0:
                    dve.wait_ge(s_out, k // 2 + 1)
                else:
                    wait_done(dve, layer, NSP - 4 + k // 2)
                if k == 0:
                    dve.wait_ge(x_moved, layer * (16 * (KD + 1)) + 32)
                v.scalar_tensor_tensor(out=xT[:, k, :], in0=ps[:, k % 4, :], scalar=mod[:, 2 * KD + k:2 * KD + k + 1],
                                       in1=xT[:, k, :], op0=ALU.mult, op1=ALU.add).then_inc(s_x, 1)

            do = {"norm": norm, "first": casts, "proj": evac, "latr": latr, "blk": blocks, "ik": ik, "uq": uq, "ukv": ukv, "foxT": foxT, "idx": idx,
                  "hid": hid, "top": top, "selm": select, "csoft": csoft, "cturn": cmp_turn, "cval": cmp_out,
                  "unit": unit, "silu": silu, "gn": gn, "ada": ada, "adasum": adasum, "yT": yT, "x": x}

            dve.wait_ge(first_loaded, 16)
            def first_mod(n):
                dve.wait_ge(setup_pe, n + 1)
                v.tensor_tensor(mod[:, 2 * n:2 * n + 2], ps[:, 7, 0:2], fst("b_first")[:, 2 * n:2 * n + 2],
                                ALU.add).then_inc(setup_dve, 1)

            for t in (hidv, pc, vcd):
                v.memset(t[...], 0.0).then_inc(setup_fill, 1)
            dve.wait_ge(setup_act, 1)
            v.tensor_scalar(sct[:, :], sct[:, :], 1.0, None, ALU.add).then_inc(setup_sum, 1)
            dve.wait_ge(setup_sum, 1)
            v.reciprocal(sct[:, :], sct[:, :]).then_inc(setup_sum, 1)
            dve.wait_ge(setup_sum, 2)
            v.tensor_tensor(sc[:, :], sct[:, :], fst("c"), ALU.mult).then_inc(setup_dve, 1)
            dve.wait_ge(setup_dve, 1)
            count = [2]
            for n in range(N_SS):
                dve.wait_ge(w_loaded[(n + 1) % RING], 16 * ((n + 1) // RING + 1))
                if n >= 2:
                    dve.wait_ge(setup_pe, n - 1)

                def wait(last, k):
                    if k == DVE_TILES - 1:
                        last.then_inc(w_ada, 1)
                    else:
                        count[0] += 1
                        last.then_inc(setup_sum, 1)
                        dve.wait_ge(setup_sum, count[0])
                ada_tiles(ring[:, (n + 1) % RING, :].rearrange("p (k c) -> p k c", k=KD), n, range(DVE_TILES), wait)
                if n:
                    first_mod(n - 1)
            first_mod(N_SS - 1)
            dve.wait_ge(setup_dve, 1 + N_SS)
            v.scalar_tensor_tensor(out=gs[:, :], in0=mod[:, KD:2 * KD], scalar=1.0, in1=fst("rms_first"),
                                   op0=ALU.add, op1=ALU.mult).then_inc(setup_dve, 1)
            dve.wait_ge(setup_dve, SETUP_DVE)
            dve.wait_ge(setup_fill, 3)
            dve.wait_ge(setup_act, KD + 3)
            with dve.Fori(0, DEPTH) as layer:
                link = linker(dve, d_link)
                for kind, *args in MAIN:
                    if kind in do:
                        do[kind](layer, *args)
                dve.wait_ge(s_x, KD)
                dve.sem_inc(arrived, 1)
                dve.wait_ge(go, layer + 1)
            for k in range(KD):
                v.scalar_tensor_tensor(out=xT[:, k, :], in0=xT[:, k, :], scalar=fst("fin_g")[:, k:k + 1], in1=rb[:, :],
                                       op0=ALU.mult, op1=ALU.mult).then_inc(fin_out, 1)

        @block.gpsimd
        def _(pool):
            g = nc.gpsimd

            def split(layer, c, p, src=None):
                pool.wait_ge(s_hi, layer * (PIECES * NSP) + PIECES * c + p + 1)
                src = raw(("split", c)) if src is None else src
                g.tensor_tensor(piece(c, p, w_lo[:, c % 2, :]), piece(c, p, src),
                                piece(c, p, w_hi[:, c % 2, :]).bitcast(F32), ALU.subtract).then_inc(s_lo, 1)

            def x(layer, k):
                if 1 <= k < KD - 1:
                    pool.wait_ge(s_sq, k + 1)
                    if k > 1:
                        pool.wait_ge(s_sqa, k - 1)
                    g.tensor_tensor(sqa[:, :], sqa[:, :], sqr[k % 2][:, :], ALU.add).then_inc(s_sqa, 1)

            for p in range(PIECES):
                split(0, 0, p, ring[:, 0, :])
            for k in range(1, KD):
                pool.wait_ge(setup_act, k + 2)
                if k > 1:
                    pool.wait_ge(setup_sq, k - 1)
                g.tensor_tensor(xg[:, 0, :], xg[:, 0, :], xg[:, k, :], ALU.add).then_inc(setup_sq, 1)
            with pool.Fori(0, DEPTH) as layer:
                for kind, *args in MAIN:
                    if kind == "split":
                        split(layer, *args)
                    elif kind == "x":
                        x(layer, *args)
                pool.wait_ge(arrived, 4)
                pool.sem_clear(range(nums[0], nums[0] + len(nums)))
                pool.sem_inc(go, 1)
def _constants():
    f = np.float32
    out = np.zeros((P, CO_W), f)

    def put(name, a):
        a = np.asarray(a, f)
        out[:a.shape[0], CO[name][0]:CO[name][1]] = a.reshape(a.shape[0], -1)

    p = np.arange(P)
    slopes = (2.0 ** (-8.0 * (np.arange(H) + 1) / H)).astype(f)
    c = np.arange(SEQ) - (SEQ - P)
    mask = np.where(c[None, :] <= p[:, None], 0.0, MASKED)
    put("ident", np.eye(P))
    put("mask", mask)
    put("alibi", slopes[None, :, None] * (HD ** 0.5 * c)[None, None, :] + mask[:, None, :])
    t = np.arange(SEQ).reshape(NB, P).T
    end = np.arange(NCP) * CMP_STRIDE + CMP_LEN - 1
    cmpb = slopes[None, None, :, None] * (HD ** 0.5 * end) + np.zeros((P, NB, 1, 1))
    put("cmpb", np.where(end <= t[:, :, None, None], cmpb, MASKED))
    inv = f(10000.0) ** (-np.arange(16, dtype=f) / f(16))
    ang = t[:, :, None].astype(f) * inv.astype(f)
    put("cos", np.cos(ang))
    put("sin", np.sin(ang))
    put("selrow", (np.eye(H) * -(HD ** 0.5))[:, :, None] * np.ones(P))
    return out


def _rows(w):
    return w.reshape(w.shape[0], -1, P, w.shape[-1]).transpose(0, 2, 1, 3)


def kernel(x, c, rms_g, w_ada, b_ada, w_in, mla_q_norm, mla_w_uq, mla_kv_norm, mla_w_ukv, fox_b_f,
           nsa_cmp_pos, nsa_cmp_w1, nsa_cmp_w2, out_norm_g, w_out, final_g):
    import concourse.bacc as bacc
    from concourse.bass_utils import run_bass_kernel_spmd

    (x, c, rms_g, w_ada, b_ada, w_in, mla_q_norm, mla_w_uq, mla_kv_norm, mla_w_ukv, fox_b_f, nsa_cmp_pos,
     nsa_cmp_w1, nsa_cmp_w2, out_norm_g, w_out, final_g) = (
        np.asarray(a) for a in (x, c, rms_g, w_ada, b_ada, w_in, mla_q_norm, mla_w_uq, mla_kv_norm, mla_w_ukv,
                                fox_b_f, nsa_cmp_pos, nsa_cmp_w1, nsa_cmp_w2, out_norm_g, w_out, final_g))
    widths = [("q_lat", 192), ("kv_lat", 128), ("k_rope", 32), ("fox_q", 256), ("fox_k", 256), ("fox_v", 256),
              ("fox_f", 4), ("dsa_q", 256), ("dsa_k", 256), ("dsa_v", 256), ("idx_q", 128), ("idx_k", 32),
              ("idx_w", 4), ("nsa_q", 256), ("k_cmp", 64), ("v_cmp", 64), ("k_sel", 64), ("v_sel", 64),
              ("k_win", 64), ("v_win", 64), ("nsa_gate", 12), ("gate_z", 1024)]
    rows, seg, at = _rows(w_in), {}, 0
    for name, w in widths:
        seg[name] = rows[..., at:at + w]
        at += w

    w_gate_z, ada, w_o = seg["gate_z"], _rows(w_ada), _rows(w_out)
    unit_segments = {"A1": ("q_lat", "idx_k", "idx_w", "fox_f", "nsa_gate"), "A2": ("kv_lat", "k_rope"),
                     "IQ": ("idx_q",), "CM": ("k_cmp", "v_cmp"), "FQ": ("fox_q",), "FK": ("fox_k",),
                     "FV": ("fox_v",), "NQ": ("nsa_q",), "SW": ("k_sel", "k_win", "v_sel", "v_win"),
                     "DQ": ("dsa_q",), "DK": ("dsa_k",), "DV": ("dsa_v",)}
    w_uq = np.zeros((DEPTH, 2 * P, H * QK_W), np.float32)
    w_uq[:, :Q_LORA] = mla_w_uq
    uq = _rows(w_uq)
    cmpw = nsa_cmp_w1.reshape(DEPTH, 2, CMP_J, P, HD).transpose(0, 3, 1, 2, 4)

    def split_unit(name, l):
        if name[0] == "G":
            g = int(name[2])
            return w_gate_z[l, ..., GW * g:GW * g + GW]
        if name[0] == "O":
            n = int(name[1])
            return w_o[l, ..., 256 * n:256 * n + 256]
        return np.concatenate([seg[n][l] for n in unit_segments[name]], axis=-1)

    def loaded_unit(kind, n, l):
        nxt = (l + 1) % DEPTH
        if kind == "split":
            return split_unit(SPLIT_NAMES[n % NSP], l if n < NSP else nxt)
        if kind == "ada":
            return ada[l, ..., 2 * D + 256 * n:][..., :256] if n < N_GATE else ada[nxt, ..., 256 * (n - N_GATE):][..., :256]
        return {"uq": uq[l], "ukv": mla_w_ukv[l], "cmpk": cmpw[l, :, 0], "cmpv": cmpw[l, :, 1]}[kind]

    w_all = np.stack([np.concatenate([loaded_unit(kind, n, l).reshape(P, -1) for kind, n in RING_UNITS], axis=-1)
                      for l in range(DEPTH)])
    w_first = np.concatenate([ada[0, ..., 256 * n:256 * n + 256].reshape(P, -1) for n in range(N_SS)]
                             + [split_unit("A1", 0).reshape(P, -1)], axis=-1)

    def cols(a):
        return np.swapaxes(a.reshape(*a.shape[:-1], -1, P), -1, -2)

    par = np.zeros((DEPTH, P, PR_W), np.float32)

    def put(name, a):
        par[:, :a.shape[1], PR[name][0]:PR[name][1]] = a

    b_cols, rms_cols = cols(b_ada), cols(rms_g)
    put("b_gate", b_cols[..., 2 * KD:])
    put("b_next", np.roll(b_cols[..., :2 * KD], -1, axis=0))
    put("rms_next", np.roll(rms_cols, -1, axis=0))
    put("out_g", cols(out_norm_g))
    qg = np.zeros((DEPTH, 2 * P), np.float32)
    qg[:, :Q_LORA] = mla_q_norm
    put("q_g", cols(qg))
    put("kv_g", mla_kv_norm[:, :, None])
    put("b_f", np.broadcast_to(fox_b_f[:, None, :], (DEPTH, P, H)))
    put("pos", nsa_cmp_pos.reshape(DEPTH, 2, CMP_J, P).transpose(0, 3, 1, 2).reshape(DEPTH, P, -1))
    put("w2k", np.concatenate([nsa_cmp_w2[:, 0]] * 2, axis=-1))
    put("w2v", nsa_cmp_w2[:, 1])

    first = np.zeros((P, P0_W), np.float32)
    late = np.arange(P)[:, None] >= CMP_LEN - 1
    for name, a in (("b_first", b_cols[0, :, :2 * KD]), ("rms_first", rms_cols[0]), ("fin_g", cols(final_g)),
                    ("c", cols(c[0])), ("mean", 1.0 / D), ("one", 1.0), ("eps", EPS), ("late", late)):
        first[:, P0[name][0]:P0[name][1]] = a

    arrays = {
        "x_t": x[0].T.reshape(KD, P, SEQ).transpose(1, 0, 2),
        "first": first, "w_first": w_first, "w_all": w_all, "par": par, "const": _constants(),
    }
    arrays = {k: np.ascontiguousarray(v) for k, v in arrays.items()}
    nc = bacc.Bacc("TRN2", target_bir_lowering=False, num_devices=1, dynamic_dma_scratch_size=1024)
    aps = [nc.dram_tensor(k, v.shape, mybir.dt.from_np(v.dtype), kind="ExternalInput").ap() for k, v in arrays.items()]
    y_t = nc.dram_tensor("y_t", (P, KD, SEQ), F32, kind="ExternalOutput").ap()
    program(nc, *aps, y_t)
    r = run_bass_kernel_spmd(nc, [arrays], core_ids=[0])
    y = np.asarray(r.results[0]["y_t"])
    return np.ascontiguousarray(y.transpose(1, 0, 2).reshape(D, SEQ).T)[None]
```

```python
from contextlib import ExitStack

import numpy as np
import concourse.bass as bass
from concourse import mybir

F32 = mybir.dt.float32
BF16 = mybir.dt.bfloat16
ALU = mybir.AluOpType
ACT = mybir.ActivationFunctionType
AX_X = mybir.AxisListType.X

P = 128
D, SEQ, DEPTH = 1024, 512, 2
KD = D // P
NB = SEQ // P
H, HD = 4, 64
GW = H * HD
Q_LORA, KV_LORA, ROPE = 192, 128, 32
QK_W = HD + ROPE
TOPK = min(256, SEQ // 4)
CMP_LEN, CMP_STRIDE = 32, 16
N_CMP = (SEQ - CMP_LEN) // CMP_STRIDE + 1
NCP = 32
CMP_J = CMP_LEN // 2
HALF = SEQ // 2
LO_ROW = 32
EPS = 1e-6
MASKED = -1e30
TAKEN = -3e38
LOWEST = -2e38

F32R = mybir.dt.float32r

SPLIT = {"A1": (276, "t"), "A2": (128, "c"), "IQ": (128, "c"), "CM": (128, "c"), "FQ": (256, "c"), "FK": (256, "c"),
         "FV": (256, "t"), "GZ0": (256, "t"), "NQ": (256, "c"), "SW": (256, "cv"), "DQ": (256, "c"), "DK": (256, "c"),
         "DV": (256, "t"), "GZ1": (256, "t"), "GZ3": (256, "t"), "GZ2": (256, "t"),
         "O0": (256, "o"), "O1": (256, "o"), "O2": (256, "o"), "O3": (256, "o")}
SPLIT_NAMES = list(SPLIT)
NSP = len(SPLIT)
PIECES = 4
SLOT = KD * 256
RING = 3
N_GATE, N_SS = 4, 8
ADA_CHUNKS = 4
DVE_TILES = 6
UQ_W, UKV_W, CMPW_W = 2 * H * QK_W, 2 * GW, CMP_J * HD
assert NSP % 2 == 0


def steps_of(name):
    width, how = SPLIT[name]
    if how == "t":
        return [(name, i, "t") for i in range(NB)]
    if how == "cv":
        return [(name, 0, "c"), (name, 1, "c"), (name, 2, "v")]
    return [(name, i, "c") for i in range(width // P)]


STEPS = [s for n in SPLIT_NAMES if n[0] != "O" for s in steps_of(n)]
STEP_NO = {s: n for n, s in enumerate(STEPS)}

MIXERS = ["mla", "fox", "sel", "win", "dsa"]
UNITS = [(m, i, h) for m in MIXERS for i in range(NB) for h in range(H)]
NUN = len(UNITS)
OUT_COL = {"mla": 0, "fox": GW, "dsa": 2 * GW, "sel": 3 * GW, "win": 3 * GW}
FILLERS = SPLIT_NAMES[6:16]
PER_FILL = NUN // len(FILLERS)
BESIDE = [(2, ("kc",)), (4, ("fsplit",)), (6, ("fb", 0)), (8, ("fb", 1)), (10, ("fb", 2)), (12, ("fb", 3)),
          (26, ("cs", 0)), (27, ("cs", 1)), (28, ("csoft",)), (31, ("cden",)), (33, ("cturn",)),
          (35, ("cval", 0)), (37, ("cval", 1)), (22, ("gn", 0)), (70, ("gn", 1)), (78, ("gn", 3))]
BESIDE += [(at + i, ("gss", m, i)) for at, m in ((18, 0), (57, 1), (69, 3)) for i in range(NB)]
ADA_FROM, ADA_TO = 48, 78
CT_ORDER = [0, 1, 2, 3, 6, 7, 4, 5]


def main_items():
    items = []

    def split(c):
        return [("split", c, p) for p in range(PIECES)]

    def proj(name, part=None):
        st = steps_of(name)
        return [("proj", s, 0, KD) for s in (st if part is None else [st[part]])]

    items += [("norm",)] + split(1) + [("first",)] + split(2)
    items += proj("A2") + split(3) + [("latr",)] + proj("IQ") + split(4) + [("kvs",), ("lat",), ("foxT",)]
    items += proj("CM") + split(5) + [("blk",), ("uq",), ("ik",)]
    items += proj("FQ", 0) + [("ukv",), ("idx", 1)] + proj("FQ", 1) + split(6) + [("hid",)]
    items += proj("FK", 0) + [("idx", 2), ("mq",)] + proj("FK", 1) + [("mk",), ("idx", 3)] + split(7)
    ada_chunks = (N_GATE + N_SS) * ADA_CHUNKS
    done_chunks = 0
    top = [(r, i) for r in range(TOPK // 8) for i in range(1, NB)]
    for t in range(NUN):
        items.append(("unit", t))
        if t == PER_FILL * (FILLERS.index("SW") + 1):
            items.append(("proj", ("SW", 2, "v"), 0, KD))
        name = FILLERS[t // PER_FILL]
        work = [(s, k) for s in steps_of(name) if s[2] != "v" for k in range(KD)]
        n = t % PER_FILL
        mine = work[len(work) * n // PER_FILL:len(work) * (n + 1) // PER_FILL]
        for s in dict.fromkeys(s for s, _ in mine):
            ks = [k for q, k in mine if q == s]
            items.append(("proj", s, ks[0], ks[-1] + 1))
        c = SPLIT_NAMES.index(name) + 1
        if 1 <= n <= PIECES and t > PER_FILL:
            items.append(("split", c, n - 1))
        if t < len(top):
            items.append(("top",) + top[t])
        if t == len(top):
            items.append(("selm",))
        last = FILLERS[t // PER_FILL - 1]
        if t >= PER_FILL and last[:2] == "GZ" and n in (1, 2, 4):
            items.append({1: ("sig", int(last[2]), 0), 2: ("sig", int(last[2]), 1), 4: ("silu", int(last[2]))}[n])
        items += [what for at, what in BESIDE if at == t]
        if ADA_FROM <= t < ADA_TO:
            upto = ada_chunks * (t - ADA_FROM + 1) // (ADA_TO - ADA_FROM)
            for j in range(done_chunks, upto):
                items.append(("ada", j // ADA_CHUNKS, j % ADA_CHUNKS))
                if j % ADA_CHUNKS == 2 and j > ADA_CHUNKS:
                    items.append(("adasum", j // ADA_CHUNKS - 1))
            done_chunks = upto
    assert done_chunks == ada_chunks
    items += [("unit", NUN), ("adasum", N_GATE + N_SS - 1)] + [("yT", k) for k in CT_ORDER[:2]] + [("sig", 2, 0)]
    items += [("unit", NUN + 1)] + [("yT", k) for k in CT_ORDER[2:4]] + [("sig", 2, 1), ("unit", NUN + 2)]
    items += [("silu", 2)] + [("gss", 2, i) for i in range(NB)]
    items += [("yT", k) for k in CT_ORDER[4:6]] + [("gn", 2), ("out", 0, 0, 4), ("out", 1, 0, 4), ("out", 0, 4, 6)]
    items += split(17) + [("yT", k) for k in CT_ORDER[6:]] + [("out", 1, 4, 6)]
    items += [("out", 0, 6, KD), ("out", 1, 6, KD), ("x", 0), ("x", 1)] + split(18)
    items += [("out", 2, 0, KD), ("x", 2), ("out", 3, 0, KD), ("x", 3)] + split(19)
    items += [("out", 4, 0, KD), ("x", 4), ("out", 5, 0, KD), ("x", 5)] + split(20)
    items += [("out", 6, 0, KD), ("x", 6), ("out", 7, 0, KD), ("x", 7), ("rms",)]
    return items


MAIN = main_items()


def ring_order():
    order = []
    for it in MAIN:
        if it[0] == "split" and it[2] == 0:
            order.append(("split", it[1]))
        elif it[0] in ("uq", "ukv"):
            order.append((it[0], 0))
        elif it[0] == "hid":
            order += [("cmpk", 0), ("cmpv", 0)]
        elif it[0] == "ada" and it[2] == 0:
            order.append(("ada", it[1]))
    return order


RING_UNITS = ring_order()
NR = len(RING_UNITS)
FIRST_UNITS = N_SS + 1
assert NR % RING == 0 and FIRST_UNITS % RING == 0
POS = {u: n for n, u in enumerate(RING_UNITS)}


def unit_width(u):
    kind, n = u
    if kind == "split":
        return KD * SPLIT[SPLIT_NAMES[n % NSP]][0]
    return {"uq": UQ_W, "ukv": UKV_W, "cmpk": CMPW_W, "cmpv": CMPW_W, "ada": SLOT}[kind]


WIDTHS = [unit_width(u) for u in RING_UNITS]
OFFSETS = [sum(WIDTHS[:n]) for n in range(NR + 1)]
A1_W = SPLIT["A1"][0]
FIRST_W = N_SS * SLOT + KD * A1_W

C_QL, C_IK, C_IW, C_FF, C_NG, C_KR = 0, 192, 224, 228, 232, 244


FIN_POOL = (3, 6)


def columns(widths):
    at, out = 0, {}
    for name, w in widths:
        out[name] = (at, at + w)
        at += w
    return out, at


PR, PR_W = columns([("b_gate", KD), ("b_next", 2 * KD), ("rms_next", KD), ("out_g", KD), ("q_g", 2), ("kv_g", 1),
                    ("b_f", H), ("pos", 2 * CMP_J), ("w2k", 2 * HD), ("w2v", HD)])
P0, P0_W = columns([("b_first", 2 * KD), ("rms_first", KD), ("fin_g", KD), ("c", KD), ("mean", P), ("one", 1),
                    ("eps", 1), ("late", 1)])
CO, CO_W = columns([("ident", P), ("alibi", H * SEQ), ("mask", SEQ), ("cmpb", NB * H * NCP), ("cos", NB * 16),
                    ("sin", NB * 16), ("selrow", H * P)])


def program(nc, x_t, first, w_first, w_all, par, const, y_t):
    xs = nc.dram_tensor("xs", (P, KD, SEQ), F32).ap()
    with ExitStack() as ctx:
        def sb(name, shape, dt=F32):
            return ctx.enter_context(nc.sbuf_tensor(name, shape, dt))

        def sem(name):
            return ctx.enter_context(nc.semaphore(name))

        h_hi, h_lo = sb("h_hi", [P, KD, SEQ], F32R), sb("h_lo", [P, KD, SEQ], F32R)
        ring = [sb(f"ring{n}", [P, w]) for n, w in enumerate((KD * A1_W, SLOT, KD * A1_W))]
        w_hi, w_lo = ([sb(f"{n}{j}", [P, w], F32R) for j, w in enumerate((KD * A1_W, SLOT))] for n in ("w_hi", "w_lo"))
        o_sb = sb("o_sb", [P, NB, D])
        sz = sb("sz", [P, NB, D])
        tm = sb("tm", [P, NB, A1_W])
        fq, fk = sb("fq", [P, 2, SEQ]), sb("fk", [P, 2, SEQ])
        mq, mk = sb("mq", [P, H, SEQ]), sb("mk", [P, H, SEQ])
        v_tm = sb("v_tm", [P, NB, GW])
        fv = sb("fv", [P, NB, GW])
        nv = sb("nv", [P, NB, 2 * HD])
        fb = sb("fb", [P, H, SEQ])
        cst, prm, prf = sb("cst", [P, CO_W]), sb("prm", [P, PR_W]), sb("prf", [P, P0_W])
        sc, sct = sb("sc", [P, KD]), sb("sct", [P, KD])
        mod, gs = sb("mod", [P, 3 * KD]), sb("gs", [P, KD])
        acc = sb("acc", [P, 2, 256])
        rb = sb("rb", [P, SEQ])
        identb, maskb = sb("identb", [P, P], BF16), sb("maskb", [P, P], BF16)
        work = [None] + [sb(f"work{i}", [P, P * (i + 1)]) for i in range(1, NB)]
        selm = [None] + [sb(f"selm{i}", [P, P * (i + 1)], BF16) for i in range(1, NB)]
        top8 = sb("top8", [P, NB, 8])
        lss, llr = sb("lss", [P, 2, NB]), sb("llr", [P, 2, NB])
        fy, fa, fe, fl, fls = (sb(n, [P, NB, H]) for n in ("fy", "fa", "fe", "fl", "fls"))
        ge, gd, gsig = (sb(n, [P, NB, H, 3]) for n in ("ge", "gd", "gsig"))
        hide, hidr, hids = (sb(n, [HD, 2, NCP]) for n in ("hide", "hidr", "hids"))
        hidk, hidv = sb("hidk", [HD, NCP]), sb("hidv", [HD, H, NCP])
        kc2, vcd = sb("kc2", [P, NCP]), sb("vcd", [P, H, HD])
        pc = sb("pc", [P, NB, H, NCP])
        cmx, cden, crec, cfac = (sb(n, [P, NB, H]) for n in ("cmx", "cden", "crec", "cfac"))
        nmx, rsum = sb("nmx", [P, NUN]), sb("rsum", [P, NUN])
        rinv, rfac = sb("rinv", [P, NUN]), sb("rfac", [P, NUN])
        gss, gln, grs = (sb(n, [P, H, NB]) for n in ("gss", "gln", "grs"))
        iqr, ikr = ([sb(f"{n}{j}", [P, SEQ], F32R) for j in range(2)] for n in ("iqr", "ikr"))
        pr_ = [sb(f"pr{n}", [P, SEQ]) for n in range(3)]
        pt = [sb(f"pt{n}", [P, SEQ]) for n in range(2)]
        ps = ctx.enter_context(nc.psum_tensor("ps", [P, 8, 512], F32))
        MISC = 1

        flat_o = o_sb[:, :, :].rearrange("p i d -> p (i d)")
        flat_s = sz[:, :, :].rearrange("p i d -> p (i d)")
        xT = flat_s.rearrange("p (k t) -> p k t", k=KD)
        xg = flat_o.rearrange("p (k t) -> p k t", k=KD)
        q_tm = flat_o[:, 0:NB * H * QK_W].rearrange("p (i h e) -> p i h e", i=NB, h=H)
        k_tm = flat_o[:, NB * H * QK_W:2 * NB * H * QK_W].rearrange("p (i h e) -> p i h e", i=NB, h=H)
        rt = [flat_o[:, 3072 + 256 * n:3072 + 256 * n + 256].rearrange("p (i h e) -> p i h e", i=NB, h=H)
              for n in range(4)]
        qn = flat_s[:, 0:768].rearrange("p (i c) -> p i c", i=NB)
        qlT = [flat_s[:, 1280:1792], flat_s[:, 1792:2304]]
        klT = flat_s[:, 2304:2816]
        ikd = flat_s[:, 2816:3328].rearrange("p (i g c) -> p i g c", i=NB, g=H)
        pct, otmp = tm[:, :, 0:P], tm[:, :, P:P + HD]
        squares, squares_l = tm[:, 0:2, 0:P], pr_[2]
        f_parts, sel_r = iqr
        kvsq = pr_[0]
        fcum = flat_s[0:H, 3328:3840]
        cmp2 = mk[:, 0:2, :]
        blk = mq[:, :, :].rearrange("p h t -> p (h t)")[:, 0:2 * CMP_J * N_CMP].rearrange(
            "p (s j n) -> p s j n", s=2, j=CMP_J)
        nq, sw_k = mk[:, 0:2, :], [mk[:, 2, :], mk[:, 3, :]]
        nvT = flat_s[:, 1280:1792]
        dq, dk, dv = mq[:, 0:2, :], mq[:, 2:4, :], v_tm
        rl = fb
        flat_fb = fb[:, :, :].rearrange("p h t -> p (h t)")
        ez_a, ez_b = (flat_fb[:, n:n + NB * GW].rearrange("p (i c) -> p i c", i=NB) for n in (0, NB * GW))
        ez_of = {0: o_sb[:, :, 2 * GW:3 * GW], 1: ez_a, 3: ez_b, 2: ez_a}
        sqr = [pr_[0], pr_[1]]
        sqa = pr_[2]

        def first_sums(n):
            return ps[:, 4 + 2 * (n % 2):6 + 2 * (n % 2), 0:1]

        def con(name):
            return cst[:, CO[name][0]:CO[name][1]]

        def par_(name):
            return prm[:, PR[name][0]:PR[name][1]]

        def fst(name):
            return prf[:, P0[name][0]:P0[name][1]]

        ident = con("ident")
        alibi = con("alibi").rearrange("p (h t) -> p h t", h=H)
        cosv = con("cos").rearrange("p (i e) -> p i e", i=NB).unsqueeze(2)
        sinv = con("sin").rearrange("p (i e) -> p i e", i=NB).unsqueeze(2)
        late, eps, one = fst("late"), fst("eps"), fst("one")

        w_loaded = [sem(f"w_loaded{n}") for n in range(RING)]
        s_hi = sem("s_hi")
        s_lo = sem("s_lo")
        w_done = sem("w_done")
        w_direct = sem("w_direct")
        w_ada = sem("w_ada")
        par_loaded, first_loaded, const_loaded = sem("par_loaded"), sem("first_loaded"), sem("const_loaded")
        x_moved = sem("x_moved")
        go = sem("go")
        setup_act, setup_dve, setup_pe, setup_sq, setup_ms = (
            sem(n) for n in ("setup_act", "setup_dve", "setup_pe", "setup_sq", "setup_ms"))
        setup_fill, setup_sum = sem("setup_fill"), sem("setup_sum")
        fin_out, fin_act, fin_pool, y_stored = (sem(n) for n in ("fin_out", "fin_act", "fin_pool", "y_stored"))

        layer_sems = []

        def lsem(name):
            layer_sems.append(sem(name))
            return layer_sems[-1]

        arrived = lsem("arrived")
        s_xg, s_hhi, s_h = lsem("s_xg"), lsem("s_hhi"), lsem("s_h")
        s_proj, s_evac = lsem("s_proj"), lsem("s_evac")
        s_ikd, s_ikp, s_ikh, s_ikT = lsem("s_ikd"), lsem("s_ikp"), lsem("s_ikh"), lsem("s_ikT")
        s_idx, s_relu, s_isc = lsem("s_idx"), lsem("s_relu"), lsem("s_isc")
        s_top, s_selm = lsem("s_top"), lsem("s_selm")
        s_lss, s_llr, s_lat, s_latp, s_latT = (lsem(n) for n in ("s_lss", "s_llr", "s_lat", "s_latp", "s_latT"))
        s_uq, s_uqe, s_ukv, s_ukve = lsem("s_uq"), lsem("s_uqe"), lsem("s_ukv"), lsem("s_ukve")
        s_rope = lsem("s_rope")
        s_mqp, s_mq, s_mkp, s_mk = lsem("s_mqp"), lsem("s_mq"), lsem("s_mkp"), lsem("s_mk")
        s_fa, s_fl, s_fls, s_flp, s_fcum = (lsem(n) for n in ("s_fa", "s_fl", "s_fls", "s_flp", "s_fcum"))
        s_fbp, s_fb = lsem("s_fbp"), lsem("s_fb")
        s_gd, s_ge, s_gsig = lsem("s_gd"), lsem("s_ge"), lsem("s_gsig")
        s_blk, s_hide, s_hid, s_kcp, s_kc = (lsem(n) for n in ("s_blk", "s_hide", "s_hid", "s_kcp", "s_kc"))
        s_cs, s_csub, s_cexp, s_pc = lsem("s_cs"), lsem("s_csub"), lsem("s_cexp"), lsem("s_pc")
        s_csum = lsem("s_csum")
        s_pctp, s_pct, s_cpv, s_co = lsem("s_pctp"), lsem("s_pct"), lsem("s_cpv"), lsem("s_co")
        s_sc, s_ttr, s_exp, s_tr = lsem("s_sc"), lsem("s_ttr"), lsem("s_exp"), lsem("s_tr")
        s_pta, s_ptd, s_pv, s_norm = lsem("s_pta"), lsem("s_ptd"), lsem("s_pv"), lsem("s_norm")
        s_sig, s_silu, s_grs, s_y = lsem("s_sig"), lsem("s_silu"), lsem("s_grs"), lsem("s_y")
        s_acc, s_adap, s_mod = lsem("s_acc"), lsem("s_adap"), lsem("s_mod")
        s_yp, s_oThi, s_oT = lsem("s_yp"), lsem("s_oThi"), lsem("s_oT")
        s_out, s_x, s_sq, s_sqa, s_ms, s_rb = (lsem(n) for n in ("s_out", "s_x", "s_sq", "s_sqa", "s_ms", "s_rb"))
        s_cast, s_swap, s_kvs, s_kvr, s_fpart, s_xh, s_sqh = (
            lsem(n) for n in ("s_cast", "s_swap", "s_kvs", "s_kvr", "s_fpart", "s_xh", "s_sqh"))
        d_link, a_link = lsem("d_link"), lsem("a_link")
        nums = [s.num for s in layer_sems]
        assert nums == list(range(nums[0], nums[0] + len(nums)))

        def linker(eng, s):
            count = [0]

            def link(ins):
                count[0] += 1
                ins.then_inc(s, 1)
                eng.wait_ge(s, count[0])
            return link

        PER_RING = 16 * (NR // RING)

        def raw(u):
            return ring[(FIRST_UNITS + POS[u]) % RING][:, 0:unit_width(u)]

        def wait_raw(eng, layer, u):
            n = FIRST_UNITS + POS[u]
            eng.wait_ge(w_loaded[n % RING], layer * PER_RING + 16 * (n // RING + 1))

        def wait_done(eng, layer, c):
            eng.wait_ge(w_done, layer * NSP + c + 1)

        def split_done(c):
            width = SPLIT[SPLIT_NAMES[c % NSP]][0]
            return [w[c % 2][:, 0:KD * width].rearrange("p (k c) -> p k c", k=KD) for w in (w_hi, w_lo)]

        def piece(c, p, view):
            n = KD * SPLIT[SPLIT_NAMES[c % NSP]][0] // PIECES
            return view[:, n * p:n * p + n]

        last_of = {n: steps_of(n)[-1] for n in SPLIT_NAMES}
        filler_steps = {s for n in FILLERS for s in steps_of(n)}
        BANK, before, user = {}, {}, {}
        for n, s in enumerate(STEPS):
            if s[2] == "v":
                BANK[s], before[s] = MISC, None
                continue
            BANK[s] = 0 if s in filler_steps else n % 4
            before[s] = user.get(BANK[s])
            user[BANK[s]] = n
        N_PREP = sum(1 for s in STEPS if s not in filler_steps)

        def wait_step(eng, layer, s):
            if s == last_of[s[0]]:
                wait_done(eng, layer, SPLIT_NAMES.index(s[0]))
            else:
                eng.wait_ge(s_proj, sum(1 for q in STEPS[:STEP_NO[s] + 1] if q != last_of[q[0]]))

        SETUP_DVE = 1 + N_SS + 1
        block = ctx.enter_context(nc.Block())

        @block.sync
        def _(sp):
            sp.dma_start(prf[:], first).then_inc(first_loaded, 16)
            sp.dma_start(ring[0][:, 0:KD * A1_W], w_first[:, N_SS * SLOT:FIRST_W]).then_inc(w_loaded[0], 16)
            for n in range(N_SS):
                if n + 1 == RING:
                    sp.dma_start(xT, x_t).then_inc(x_moved, 16)
                    sp.wait_ge(s_lo, PIECES)
                elif n + 1 > RING:
                    sp.wait_ge(setup_pe, n + 1 - RING)
                sp.dma_start(ring[(n + 1) % RING][:, 0:SLOT], w_first[:, n * SLOT:n * SLOT + SLOT])\
                    .then_inc(w_loaded[(n + 1) % RING], 16)
            sp.dma_start(prm[:], par[0]).then_inc(par_loaded, 16)
            sp.dma_start(cst[:], const).then_inc(const_loaded, 16)

            def used(layer, pos):
                if pos < 0:
                    if layer == 0:
                        sp.wait_ge(setup_pe, N_SS + pos + 1)
                        return
                    layer, pos = layer - 1, NR + pos
                kind, n = RING_UNITS[pos]
                if kind == "split":
                    sp.wait_ge(s_lo, PIECES * (layer * NSP + n + 1))
                elif kind == "ada":
                    sp.wait_ge(w_ada, N_SS + layer * (N_GATE + N_SS) + n + 1)
                else:
                    sp.wait_ge(w_direct, layer * 4 + ["uq", "ukv", "cmpk", "cmpv"].index(kind) + 1)

            def load(layer, pos):
                used(layer, pos - RING)
                n = (FIRST_UNITS + pos) % RING
                kind, number = RING_UNITS[pos]
                if layer == DEPTH - 1 and kind == "ada" and number >= N_GATE:
                    sp.sem_inc(w_loaded[n], 16)
                    return
                sp.dma_start(ring[n][:, 0:WIDTHS[pos]], w_all[layer, :, OFFSETS[pos]:OFFSETS[pos] + WIDTHS[pos]])\
                    .then_inc(w_loaded[n], 16)

            for layer in range(DEPTH):
                for pos in range(RING if layer else 0, NR - 2):
                    load(layer, pos)
                if layer:
                    sp.wait_ge(x_moved, layer * 16 * (KD + 1) + 16)
                sp.wait_ge(s_y, 4)
                sp.dma_start(xT, x_t if layer == 0 else xs).then_inc(x_moved, 16)
                for pos in range(NR - 2, NR):
                    load(layer, pos)
                if layer + 1 < DEPTH:
                    for pos in range(RING):
                        load(layer + 1, pos)
                    for k in range(KD):
                        sp.wait_ge(s_x, k + 1)
                        sp.dma_start(xs[:, k, :], xT[:, k, :]).then_inc(x_moved, 16)
                sp.sem_inc(arrived, 1)
                sp.wait_ge(go, layer + 1)
                if layer + 1 < DEPTH:
                    sp.dma_start(prm[:], par[layer + 1]).then_inc(par_loaded, 16)
            for k in range(KD):
                if k in FIN_POOL:
                    sp.wait_ge(fin_pool, FIN_POOL.index(k) + 1)
                else:
                    sp.wait_ge(fin_out, k + 1 - sum(j < k for j in FIN_POOL))
                sp.dma_start(y_t[:, k, :], xT[:, k, :]).then_inc(y_stored, 16)
            sp.wait_ge(y_stored, 16 * KD)

        @block.tensor
        def _(pe):
            mm, tp = nc.tensor.matmul, nc.tensor.transpose
            free = {}

            def take(banks, *by):
                for b in dict.fromkeys(free[b] for b in banks if b in free):
                    pe.wait_ge(*b)
                for b, f in zip(banks, by * len(banks) if len(by) == 1 else by):
                    free[b] = f

            def three(out, lhs, rhs, k, start, stop):
                mm(out, lhs[0][k], rhs[0][k], start=start, stop=False)
                mm(out, lhs[0][k], rhs[1][k], start=False, stop=False)
                return mm(out, lhs[1][k], rhs[0][k], start=False, stop=stop)

            def operands(s):
                name, i, how = s
                ws = split_done(SPLIT_NAMES.index(name))
                hs = (h_hi, h_lo)
                if how == "c":
                    return ([[w[:, k, P * i:P * i + P] for k in range(KD)] for w in ws],
                            [[h[:, k, :] for k in range(KD)] for h in hs])
                return ([[h[:, k, P * i:P * i + P] for k in range(KD)] for h in hs],
                        [[w[:, k, :] for k in range(KD)] for w in ws])

            def bank_out(s):
                n = SPLIT[s[0]][0] if s[2] == "t" else SEQ
                return ps[:, BANK[s], 0:n]

            def finish_step(last, s):
                last.then_inc(w_done if s == last_of[s[0]] else s_proj, 1)

            def proj(layer, s, k0, k1):
                name = s[0]
                if k0 == 0:
                    if s == steps_of(name)[0]:
                        pe.wait_ge(s_lo, layer * (PIECES * NSP) + PIECES * (SPLIT_NAMES.index(name) + 1))
                    if before[s] is not None:
                        pe.wait_ge(s_evac, before[s] + 1)
                        if STEPS[before[s]][0] == "IQ":
                            pe.wait_ge(s_ikT, 1)
                if s[2] == "v":
                    pe.wait_ge(s_evac, STEP_NO[s])
                    pe.wait_ge(s_csum, 1)
                    for i in range(NB):
                        last = tp(ps[:, BANK[s], P * i:P * i + P], nvT[:, P * i:P * i + P], ident)
                    return finish_step(last, s)
                lhs, rhs = operands(s)
                for k in range(k0, k1):
                    last = three(bank_out(s), lhs, rhs, k, k == 0, k == KD - 1)
                if k1 == KD:
                    finish_step(last, s)

            def first_unit(layer):
                pe.wait_ge(s_lo, layer * (PIECES * NSP) + PIECES)
                for k in range(KD):
                    pe.wait_ge(s_h, k + 1)
                    for s in steps_of("A1"):
                        lhs, rhs = operands(s)
                        last = three(bank_out(s), lhs, rhs, k, k == 0, k == KD - 1)
                        if k == KD - 1:
                            finish_step(last, s)

            def ik(layer):
                take([4], (s_ikT, 2))
                pe.wait_ge(s_ikd, 1)
                for i in range(NB):
                    last = tp(ps[:, 4, P * i:P * i + P], ikd[:, i].rearrange("p g c -> p (g c)"), ident)
                last.then_inc(s_ikp, 1)

            def idx(layer, i):
                if i == 1:
                    pe.wait_ge(s_ikT, 2)
                    pe.wait_ge(s_evac, STEP_NO[last_of["IQ"]] + 1)
                w = P * (i + 1)
                for n, (a, b) in enumerate(((0, 0), (0, 1), (1, 0))):
                    for h in range(H):
                        if n == 0:
                            take([4 + h], (s_relu, H * (i - 1) + h + 1))
                        r = slice(32 * h, 32 * h + 32)
                        last = mm(ps[:, 4 + h, 0:w], iqr[a][r, P * i:P * i + P], ikr[b][r, 0:w],
                                  start=n == 0, stop=n == 2)
                        if n == 2:
                            last.then_inc(s_idx, 1)

            def foxT(layer):
                take([7], (s_fcum, 1))
                pe.wait_ge(s_fls, 1)
                for i in range(NB):
                    last = tp(ps[0:H, 7, P * i:P * i + P], fls[:, i, :], ident)
                last.then_inc(s_flp, 1)

            def kvs(layer):
                take([6], (s_kvr, 1))
                pe.wait_ge(s_evac, STEP_NO[last_of["A2"]] + 1)
                for i in range(NB):
                    last = mm(ps[:, 6, i:i + 1], kvsq[:, P * i:P * i + P], one, start=True, stop=True)
                last.then_inc(s_kvs, 1)

            def lat(layer):
                pe.wait_ge(par_loaded, layer * 16 + 16)
                pe.wait_ge(const_loaded, 16)
                take([4, 5], (s_latT, 1), (s_latT, 2))
                pe.wait_ge(s_lat, 1)
                for i in range(NB):
                    tp(ps[:, 4, P * i:P * i + P], qn[:, i, 0:P], ident)
                    last = tp(ps[0:Q_LORA - P, 5, P * i:P * i + P], qn[:, i, P:Q_LORA], ident)
                last.then_inc(s_latp, 1)

            def uq(layer):
                wait_raw(pe, layer, ("uq", 0))
                pe.wait_ge(s_latT, 2)
                w = raw(("uq", 0))
                for i in range(NB):
                    take([4 + i], (s_uqe, i + 1))
                    mm(ps[:, 4 + i, 0:H * QK_W], qlT[0][:, P * i:P * i + P], w[:, 0:H * QK_W], start=True, stop=False)
                    last = mm(ps[:, 4 + i, 0:H * QK_W], qlT[1][0:64, P * i:P * i + P], w[0:64, H * QK_W:2 * H * QK_W],
                              start=False, stop=True)
                    last.then_inc(s_uq if i < NB - 1 else w_direct, 1)

            def ukv(layer):
                wait_raw(pe, layer, ("ukv", 0))
                for i in range(NB):
                    take([4 + i], (s_ukve, i + 1))
                    last = mm(ps[:, 4 + i, :], klT[:, P * i:P * i + P], raw(("ukv", 0)), start=True, stop=True)
                    last.then_inc(s_ukv if i < NB - 1 else w_direct, 1)

            def hid(layer):
                take([4], (s_hid, 2))
                pe.wait_ge(s_blk, 2)
                for s, u in enumerate((("cmpk", 0), ("cmpv", 0))):
                    wait_raw(pe, layer, u)
                    w = raw(u).rearrange("p (j c) -> p j c", j=CMP_J)
                    for j in range(CMP_J):
                        last = mm(ps[0:HD, 4, NCP * s:NCP * s + N_CMP], w[:, j, :], blk[:, s, j, :],
                                  start=j == 0, stop=j == CMP_J - 1)
                    last.then_inc(w_direct, 1)

            def kc(layer):
                pe.wait_ge(s_hid, 2)
                mm(ps[:, MISC, 0:N_CMP], par_("w2k")[0:HD, :], hidk[:, 0:N_CMP], start=True, stop=True)
                mm(ps[:, MISC, P:P + HD], hidv[:, :, :].rearrange("p g n -> p (g n)"), par_("w2v")[0:HD, :],
                   start=True, stop=True).then_inc(s_kcp, 1)

            def heads(src, made, done):
                for h in range(H):
                    take([4 + h], (done, h + 1))
                    for i in range(NB):
                        last = tp(ps[0:QK_W, 4 + h, P * i:P * i + P], src[:, i, h, :], ident)
                    last.then_inc(made, 1)

            def mqT(layer):
                pe.wait_ge(s_rope, 1)
                heads(q_tm, s_mqp, s_mq)

            def mkT(layer):
                pe.wait_ge(s_rope, 2)
                heads(k_tm, s_mkp, s_mk)

            def fbT(layer, h):
                if h == 0:
                    pe.wait_ge(s_fpart, 2)
                pe.wait_ge(s_kc, 2) if h == 0 else pe.wait_ge(s_fb, h)
                mm(ps[:, MISC, :], sel_r[0:LO_ROW + H, P * h:P * h + P], f_parts[0:LO_ROW + H, :], start=True,
                   stop=True).then_inc(s_fbp, 1)

            def cs(layer, odd):
                if odd:
                    pe.wait_ge(s_cs, 1)
                else:
                    pe.wait_ge(s_fb, H)
                    pe.wait_ge(s_evac, STEP_NO[last_of["NQ"]] + 1)
                for i in range(NB):
                    for h in (odd, odd + 2):
                        r = slice(64 * odd, 64 * odd + 64)
                        c = odd * 256 + (i * 2 + h // 2) * NCP
                        last = mm(ps[:, MISC, c:c + N_CMP], nq[r, h // 2, P * i:P * i + P], kc2[r, 0:N_CMP],
                                  start=True, stop=True)
                last.then_inc(s_cs, 1)

            def cmp_turn(layer):
                pe.wait_ge(s_evac, STEP_NO["SW", 2, "v"] + 1)
                pe.wait_ge(s_pc, 1)
                for i in range(NB):
                    last = tp(ps[:, MISC, P * i:P * i + P], pc[:, i].rearrange("p h n -> p (h n)"), ident)
                last.then_inc(s_pctp, 1)

            def cmp_values(layer, half):
                pe.wait_ge(s_pct, 1) if half == 0 else pe.wait_ge(s_co, 1)
                for i in (2 * half, 2 * half + 1):
                    c = (i % 2) * GW
                    last = mm(ps[:, MISC, c:c + GW], pct[:, i, :], vcd[:, :, :].rearrange("p h e -> p (h e)"),
                              start=True, stop=True)
                last.then_inc(s_cpv, 1)

            def scores(u):
                m, i, h = UNITS[u]
                w = P * (i + 1)
                if (i, h) == (0, 0):
                    if m == "mla":
                        pe.wait_ge(s_mk, H)
                        pe.wait_ge(s_evac, N_PREP)
                    elif m == "fox":
                        pe.wait_ge(s_cast, 1)
                        pe.wait_ge(s_evac, STEP_NO[last_of["FK"]] + 1)
                    elif m == "sel":
                        pe.wait_ge(s_swap, 1)
                    elif m == "dsa":
                        pe.wait_ge(s_evac, STEP_NO[last_of["DK"]] + 1)
                mask = {"fox": (maskb, w - P)}.get(m, None)
                if m == "dsa" and i > 0:
                    pe.wait_ge(s_selm, i)
                    mask = selm[i], 0
                q, last = slice(P * i, P * i + P), {}
                for v in (u, u + 1):
                    h, r = v % H, slice(64 * (v % 2), 64 * (v % 2) + 64)
                    lhs, rhs = {"mla": (mq[0:QK_W, h, q], mk[0:QK_W, h, 0:w]),
                                "fox": (fq[r, h // 2, q], fk[r, h // 2, 0:w]),
                                "dsa": (dq[r, h // 2, q], dk[r, h // 2, 0:w]),
                                "sel": (nq[r, h // 2, q], sw_k[h % 2][r, 0:w]),
                                "win": (nq[r, h // 2, q], sw_k[1 - h % 2][r, 0:w])}[m]
                    if v >= 2:
                        pe.wait_ge(s_ttr, v - 1)
                    last[v] = mm(ps[:, 2 + v % 2, 0:w], lhs, rhs, start=True, stop=mask is None)
                    if mask is None:
                        last[v].then_inc(s_sc, 1)
                if mask is not None:
                    for v in (u, u + 1):
                        mm(ps[:, 2 + v % 2, mask[1]:w], identb[:, :], mask[0][:, :], start=False,
                           stop=True).then_inc(s_sc, 1)

            def turn(u):
                _, i, _ = UNITS[u]
                pe.wait_ge(s_exp, u + 1)
                if u == 0:
                    pe.wait_ge(s_relu, H * (NB - 1))
                if u >= 2:
                    pe.wait_ge(s_pta if u % 2 == 0 else s_ptd, u // 2)
                for j in range(i + 1):
                    last = tp(ps[:, 4 + u % 2, P * j:P * j + P], pr_[u % 3][:, P * j:P * j + P], ident)
                last.then_inc(s_tr, 1)

            def values(u):
                m, i, h = UNITS[u]
                g = u // H
                pe.wait_ge(s_pta if u % 2 == 0 else s_ptd, u // 2 + 1)
                if h == 0 and g >= 2:
                    pe.wait_ge(s_norm, g - 1)
                if (i, h) == (0, 0) and m in ("fox", "sel", "dsa"):
                    pe.wait_ge(s_evac, STEP_NO[last_of[{"fox": "FV", "sel": "SW", "dsa": "DV"}[m]]] + 1)
                for j in range(i + 1):
                    v = {"mla": v_tm[:, j, HD * h:HD * h + HD], "fox": fv[:, j, HD * h:HD * h + HD],
                         "dsa": dv[:, j, HD * h:HD * h + HD], "sel": nv[:, j, 0:HD], "win": nv[:, j, HD:2 * HD]}[m]
                    c = HD * h
                    last = mm(ps[:, 6 + g % 2, c:c + HD], pt[u % 2][:, P * j:P * j + P], v, start=j == 0, stop=j == i)
                last.then_inc(s_pv, 1)

            def unit(layer, t):
                if t < NUN and t % 2 == 0:
                    scores(t)
                if 2 <= t < NUN + 2:
                    turn(t - 2)
                if t >= 3:
                    values(t - 3)

            def adasum(layer, n):
                pe.wait_ge(s_acc, n + 1)
                if n:
                    pe.wait_ge(s_mod, n)
                else:
                    pe.wait_ge(s_co, 2)
                for m in range(2):
                    last = mm(ps[:, MISC, m:m + 1], acc[:, n % 2, P * m:P * m + P], one, start=True, stop=True)
                last.then_inc(s_adap, 1)

            def yT(layer, k):
                j = CT_ORDER.index(k)
                pe.wait_ge(s_y, 3 if j < 6 else 4)
                if j < 2:
                    pe.wait_ge(s_ttr, NUN - 1 + j)
                else:
                    pe.wait_ge(s_oT, j - 1)
                for i in range(NB):
                    last = tp(ps[:, 2 + j % 2, P * i:P * i + P], o_sb[:, i, P * k:P * k + P], ident)
                last.then_inc(s_yp, 1)

            def out(layer, n, k0, k1):
                c = NSP - 4 + n // 2
                if k0 == 0 and n == 0:
                    pe.wait_ge(s_evac, len(STEPS))
                    pe.wait_ge(s_mod, N_GATE + N_SS)
                if k0 == 0 and n % 2 == 0:
                    pe.wait_ge(s_lo, layer * (PIECES * NSP) + PIECES * (c + 1))
                if n == 2:
                    pe.wait_ge(s_oT, KD)
                if k0 == 0 and n >= 4:
                    pe.wait_ge(s_x, n - 3)
                ws = split_done(c)
                for j in range(k0, k1):
                    k = CT_ORDER[j]
                    pe.wait_ge(s_oT, j + 1)
                    lhs = [[w[:, k, P * (n % 2):P * (n % 2) + P]] for w in ws]
                    rhs = [[h[:, k, :]] for h in (h_hi, h_lo)]
                    last = three(ps[:, n % 4, :], lhs, rhs, 0, j == 0, j == KD - 1)
                if k1 == KD:
                    last.then_inc(w_done if n % 2 else s_out, 1)

            def rms(layer):
                halves = [(ps[:, 6 + n, 0:HALF], slice(HALF * n, HALF * n + HALF)) for n in range(2)]
                pe.wait_ge(s_sqa, KD - 2)
                for out_, c in halves:
                    mm(out_, fst("mean"), sqa[:, c], start=True, stop=False)
                for (out_, c), (s, n) in zip(halves, ((s_sqh, 1), (s_sq, KD))):
                    pe.wait_ge(s, n)
                    mm(out_, fst("mean"), sqr[(KD - 1) % 2][:, c], start=False, stop=True).then_inc(s_ms, 1)

            do = {"first": first_unit, "proj": proj, "ik": ik, "idx": idx, "foxT": foxT, "lat": lat, "kvs": kvs,
                  "uq": uq,
                  "ukv": ukv, "hid": hid, "kc": kc, "mq": mqT, "mk": mkT, "fb": fbT, "cs": cs, "cturn": cmp_turn,
                  "cval": cmp_values, "unit": unit, "adasum": adasum, "yT": yT, "out": out, "rms": rms}

            pe.wait_ge(first_loaded, 16)
            for n in range(N_SS):
                if n == N_SS - 2:
                    pe.wait_ge(setup_sq, KD - 1)
                    mm(ps[:, 0, :], fst("mean"), xg[:, 0, :], start=True, stop=True).then_inc(setup_ms, 1)
                pe.wait_ge(w_loaded[(n + 1) % RING], 16 * ((n + 1) // RING + 1))
                pe.wait_ge(setup_dve, max(1, n))
                w = ring[(n + 1) % RING][:, 0:SLOT].rearrange("p (k c) -> p k c", k=KD)
                for m in range(2):
                    for k in range(DVE_TILES, KD):
                        mm(first_sums(n)[:, m, :], w[:, k, P * m:P * m + P], sc[:, k:k + 1], start=k == DVE_TILES,
                           stop=False)
                pe.wait_ge(w_ada, n + 1)
                for m in range(2):
                    last = mm(first_sums(n)[:, m, :], acc[:, n % 2, P * m:P * m + P], one, start=False, stop=True)
                last.then_inc(setup_pe, 1)
            pe.wait_ge(setup_dve, SETUP_DVE)
            pe.wait_ge(setup_fill, 3)
            with pe.Fori(0, DEPTH) as layer:
                for kind, *args in MAIN:
                    if kind in do:
                        do[kind](layer, *args)
                pe.sem_inc(arrived, 1)
                pe.wait_ge(go, layer + 1)

        @block.scalar
        def _(act):
            a, cp = nc.scalar.activation, nc.scalar.copy
            lo, hi = slice(0, 64), slice(64, P)

            def split(layer, c, p, wait=True):
                if wait and p == 0:
                    wait_raw(act, layer, ("split", c))
                    if c >= 2:
                        wait_done(act, layer, c - 2)
                src = raw(("split", c)) if wait else ring[0][:, :]
                cp(piece(c, p, w_hi[c % 2]), piece(c, p, src)).then_inc(s_hi, 1)

            def norm(layer):
                for k in range(KD):
                    act.wait_ge(s_xg, k + 1)
                    a(h_hi[:, k, :], xg[:, k, :], ACT.Identity, bias=mod[:, k:k + 1]).then_inc(s_hhi, 1)

            def evac(layer, s, k0, k1):
                if k1 < KD:
                    return
                name, i, how = s
                wait_step(act, layer, s)
                bank = ps[:, BANK[s], :]
                if name == "A1":
                    last = cp(tm[:, i, 0:A1_W], bank[:, 0:A1_W])
                elif name == "A2":
                    act.wait_ge(x_moved, layer * (16 * (KD + 1)) + 16)
                    act.wait_ge(par_loaded, layer * 16 + 16)
                    a(klT, bank, ACT.Copy, scale=par_("kv_g"))
                    last = a(kvsq[:, :], bank, ACT.Square)
                elif name == "IQ":
                    last = cp(iqr[0][:, :], bank)
                elif name == "CM":
                    cp(cmp2[lo, 0, :], bank[lo, :])
                    cp(cmp2[hi, 0, 0:SEQ - 1], bank[lo, 1:SEQ])
                    cp(cmp2[lo, 1, :], bank[hi, :])
                    last = cp(cmp2[hi, 1, 0:SEQ - 1], bank[hi, 1:SEQ])
                elif name == "SW" and i == 0:
                    cp(sw_k[0], bank).then_inc(s_evac, 1)
                    act.wait_ge(s_evac, STEP_NO[s] + 1)
                    cp(sw_k[1][lo, :], sw_k[0][hi, :])
                    cp(sw_k[1][hi, :], sw_k[0][lo, :]).then_inc(s_swap, 1)
                    return
                elif name == "SW" and i == 1:
                    last = cp(nvT, bank)
                elif name == "SW":
                    last = cp(nv[:, :, :].rearrange("p i c -> p (i c)"), bank)
                elif how == "c":
                    last = cp({"FQ": fq, "FK": fk, "DQ": dq, "DK": dk, "NQ": nq}[name][:, i, :], bank)
                elif name == "FV":
                    last = cp(fv[:, i, :], bank[:, 0:GW])
                elif name == "DV":
                    last = cp(dv[:, i, :], bank[:, 0:GW])
                else:
                    g = int(name[2])
                    if i == 0 and g == 2:
                        act.wait_ge(s_silu, 2)
                    a(ez_of[g][:, i, :], bank[:, 0:GW], ACT.Exp, scale=-1.0)
                    last = cp(sz[:, i, GW * g:GW * g + GW], bank[:, 0:GW])
                last.then_inc(s_evac, 1)

            def first_unit(layer):
                for s in steps_of("A1"):
                    evac(layer, s, 0, KD)

            def latr(layer):
                act.wait_ge(s_fa, 1)
                link(a(fe[:, :, :], fa[:, :, :], ACT.Exp, scale=-1.0))
                a(fl[:, :, :], fe[:, :, :], ACT.Ln, bias=1.0).then_inc(s_fl, 1)
                act.wait_ge(s_gd, 1)
                a(ge[:, :, :, :], gd[:, :, :, :], ACT.Exp).then_inc(s_ge, 1)
                act.wait_ge(s_lss, 1)
                link(a(llr[:, 0, :], lss[:, 0, :], ACT.Ln, bias=eps, scale=1.0 / Q_LORA))
                a(lss[:, 0, :], llr[:, 0, :], ACT.Exp, scale=-0.5).then_inc(s_llr, 1)

            def kvs(layer):
                act.wait_ge(s_kvs, 1)
                a(llr[:, 1, :], ps[:, 6, 0:NB], ACT.Ln, bias=eps, scale=1.0 / KV_LORA).then_inc(s_kvr, 1)
                act.wait_ge(s_kvr, 1)
                link(a(lss[:, 1, :], llr[:, 1, :], ACT.Exp, scale=-0.5))

            def ik(layer):
                act.wait_ge(s_ikp, 1)
                cp(ikr[0][:, :], ps[:, 4, :]).then_inc(s_ikh, 1)

            def idx(layer, i):
                w = P * (i + 1)
                for h in range(H):
                    act.wait_ge(s_idx, H * (i - 1) + h + 1)
                    if i > 1:
                        act.wait_ge(s_isc, H * (i - 2) + h + 1)
                    a(rl[:, h, 0:w], ps[:, 4 + h, 0:w], ACT.Relu, scale=H ** -0.5).then_inc(s_relu, 1)

            def lat(layer):
                act.wait_ge(s_latp, 1)
                g = par_("q_g")
                a(qlT[0], ps[:, 4, :], ACT.Copy, scale=g[:, 0:1]).then_inc(s_latT, 1)
                a(qlT[1][0:64, :], ps[0:64, 5, :], ACT.Copy, scale=g[0:64, 1:2]).then_inc(s_latT, 1)

            def uq(layer):
                for i in range(NB):
                    if i < NB - 1:
                        act.wait_ge(s_uq, i + 1)
                    else:
                        act.wait_ge(w_direct, layer * 4 + 1)
                    cp(q_tm[:, i].rearrange("p h e -> p (h e)"), ps[:, 4 + i, 0:H * QK_W]).then_inc(s_uqe, 1)

            def ukv(layer):
                for i in range(NB):
                    if i < NB - 1:
                        act.wait_ge(s_ukv, i + 1)
                    else:
                        act.wait_ge(w_direct, layer * 4 + 2)
                    kv = ps[:, 4 + i, :].rearrange("p (h e) -> p h e", h=H)
                    r = lss[:, 1, i:i + 1]
                    a(k_tm[:, i, :, 0:HD], kv[:, :, 0:HD], ACT.Copy, scale=r)
                    a(v_tm[:, i].rearrange("p (h e) -> p h e", h=H), kv[:, :, HD:2 * HD], ACT.Copy,
                      scale=r).then_inc(s_ukve, 1)

            def hid(layer):
                act.wait_ge(w_direct, layer * 4 + 4)
                hp = ps[0:HD, 4, 0:2 * NCP].rearrange("p (s n) -> p s n", s=2)[:, :, 0:N_CMP]
                a(hide[:, :, 0:N_CMP], hp, ACT.Exp, scale=-1.0).then_inc(s_hide, 1)

            def kc(layer):
                act.wait_ge(s_kcp, 1)
                cp(kc2[:, 0:N_CMP], ps[:, MISC, 0:N_CMP]).then_inc(s_kc, 1)
                for h in range(H):
                    r = slice(NCP * h, NCP * h + NCP)
                    last = cp(vcd[r, h, :], ps[r, MISC, P:P + HD])
                last.then_inc(s_kc, 1)

            def heads(dst, made, done):
                for h in range(H):
                    act.wait_ge(made, h + 1)
                    cp(dst[0:QK_W, h, :], ps[0:QK_W, 4 + h, :]).then_inc(done, 1)

            def fsplit(layer):
                cp(sel_r[:, :], con("selrow"))
                act.wait_ge(s_fcum, 1)
                cp(f_parts[0:H, :], fcum).then_inc(s_fpart, 1)

            def fbT(layer, h):
                act.wait_ge(s_isc, H * (NB - 1))
                act.wait_ge(s_fbp, h + 1)
                cp(fb[:, h, :], ps[:, MISC, :]).then_inc(s_fb, 1)

            def csoft(layer):
                act.wait_ge(s_csub, 1)
                a(pc[:, :, :, 0:N_CMP], pc[:, :, :, 0:N_CMP], ACT.Exp).then_inc(s_cexp, 1)

            def cmp_turn(layer):
                act.wait_ge(s_pctp, 1)
                cp(pct, ps[:, MISC, :].rearrange("p (i q) -> p i q", i=NB)).then_inc(s_pct, 1)

            def unit(layer, t):
                if t < NUN:
                    w = P * (UNITS[t][1] + 1)
                    buf = pr_[t % 3][:, 0:w]
                    act.wait_ge(s_ttr, t + 1)
                    a(buf, buf, ACT.Exp, bias=nmx[:, t:t + 1], scale=-1.0, accum_out=rsum[:, t:t + 1]).then_inc(s_exp, 1)
                u = t - 2
                if 0 <= u < NUN and u % 2 == 0:
                    w = P * (UNITS[u][1] + 1)
                    act.wait_ge(s_tr, u + 1)
                    if u >= 2:
                        act.wait_ge(s_pv, u - 1)
                    cp(pt[0][:, 0:w], ps[:, 4, 0:w]).then_inc(s_pta, 1)

            def sigmoid(layer, g, half):
                if half == 0:
                    act.wait_ge(s_evac, STEP_NO[last_of[f"GZ{g}"]] + 1)
                    link(a(ez_of[g], ez_of[g], ACT.Ln, bias=1.0))
                else:
                    a(ez_of[g], ez_of[g], ACT.Exp, scale=-1.0).then_inc(s_sig, 1)

            gn_order = {0: 1, 1: 2, 3: 3, 2: 4}

            def group_norm(layer, m, i):
                act.wait_ge(s_norm, {0: 4, 1: 8, 3: 16, 2: 20}[m])
                link(a(squares, o_sb[:, i, GW * m:GW * m + GW].rearrange("p (a b) -> p a b", a=2), ACT.Square,
                       accum_out=gss[:, m, i:i + 1]))
                if i == NB - 1:
                    link(a(gln[:, m, :], gss[:, m, :], ACT.Ln, bias=eps, scale=1.0 / GW))
                    a(grs[:, m, :], gln[:, m, :], ACT.Exp, scale=-0.5).then_inc(s_grs, 1)

            def yT(layer, k):
                act.wait_ge(s_yp, CT_ORDER.index(k) + 1)
                j = CT_ORDER.index(k)
                a(h_hi[:, k, :], ps[:, 2 + j % 2, :], ACT.Copy, scale=par_("out_g")[:, k:k + 1]).then_inc(s_oThi, 1)

            def x(layer, k):
                if k >= 3:
                    act.wait_ge(s_sqa, k - 2)
                if k == KD - 1:
                    act.wait_ge(s_xh, 1)
                    a(sqr[k % 2][:, 0:HALF], xT[:, k, 0:HALF], ACT.Square).then_inc(s_sqh, 1)
                    act.wait_ge(s_x, KD)
                    a(sqr[k % 2][:, HALF:], xT[:, k, HALF:], ACT.Square).then_inc(s_sq, 1)
                    return
                act.wait_ge(s_x, k + 1)
                dst = sqa if k == 0 else sqr[k % 2]
                a(dst[:, :], xT[:, k, :], ACT.Square).then_inc(s_sq, 1)

            def rms(layer):
                for n in range(2):
                    act.wait_ge(s_ms, n + 1)
                    c = slice(HALF * n, HALF * n + HALF)
                    link(a(rb[:, c], ps[:, 6 + n, 0:HALF], ACT.Ln, bias=eps))
                    last = a(rb[:, c], rb[:, c], ACT.Exp, scale=-0.5)
                link(last)

            do = {"split": split, "norm": norm, "first": first_unit, "proj": evac, "latr": latr, "ik": ik, "idx": idx,
                  "lat": lat, "kvs": kvs, "uq": uq, "ukv": ukv, "hid": hid, "kc": kc,
                  "mq": lambda layer: heads(mq, s_mqp, s_mq), "mk": lambda layer: heads(mk, s_mkp, s_mk),
                  "fsplit": fsplit, "fb": fbT, "csoft": csoft, "cturn": cmp_turn, "unit": unit,
                  "sig": sigmoid, "gss": group_norm, "yT": yT, "x": x, "rms": rms}

            nc.scalar.preload_act_table_set("natural_log_exp_and_others")
            act.wait_ge(first_loaded, 16)
            a(sct[:, :], fst("c"), ACT.Exp, scale=-1.0).then_inc(setup_act, 1)
            act.wait_ge(w_loaded[0], 16)
            for p in range(PIECES):
                split(0, 0, p, wait=False)
            act.wait_ge(x_moved, 16)
            for k in range(KD):
                a(xg[:, k, :], xT[:, k, :], ACT.Square).then_inc(setup_act, 1)
            act.wait_ge(setup_ms, 1)
            a(rb[:, :], ps[:, 0, :], ACT.Ln, bias=eps).then_inc(setup_act, 1)
            act.wait_ge(setup_act, KD + 2)
            a(rb[:, :], rb[:, :], ACT.Exp, scale=-0.5).then_inc(setup_act, 1)
            act.wait_ge(setup_dve, SETUP_DVE)
            act.wait_ge(setup_fill, 3)
            with act.Fori(0, DEPTH) as layer:
                link = linker(act, a_link)
                for kind, *args in MAIN:
                    if kind in do:
                        do[kind](layer, *args)
                act.sem_inc(arrived, 1)
                act.wait_ge(go, layer + 1)
            for k in FIN_POOL:
                a(xT[:, k, :], xT[:, k, :], ACT.Copy, scale=fst("fin_g")[:, k:k + 1]).then_inc(fin_act, 1)

        @block.vector
        def _(dve):
            v = nc.vector

            def heads_of(ap):
                return ap.rearrange("p (h e) -> p h e", h=H)

            def norm(layer):
                for k in range(KD + 1):
                    if k < KD:
                        v.scalar_tensor_tensor(out=xg[:, k, :], in0=xT[:, k, :], scalar=gs[:, k:k + 1], in1=rb[:, :],
                                               op0=ALU.mult, op1=ALU.mult).then_inc(s_xg, 1)
                    if k:
                        dve.wait_ge(s_hhi, k)
                        v.scalar_tensor_tensor(out=h_lo[:, k - 1, :], in0=xg[:, k - 1, :], scalar=mod[:, k - 1:k],
                                               in1=h_hi[:, k - 1, :].bitcast(F32), op0=ALU.add,
                                               op1=ALU.subtract).then_inc(s_h, 1)

            def casts(layer):
                dve.wait_ge(const_loaded, 16)
                v.tensor_copy(identb[:, :], ident)
                v.tensor_copy(maskb[:, :], con("mask")[:, SEQ - P:SEQ]).then_inc(s_cast, 1)

            def latr(layer):
                dve.wait_ge(par_loaded, layer * 16 + 16)
                dve.wait_ge(s_evac, STEP_NO[last_of["A1"]] + 1)
                bf = par_("b_f").unsqueeze(1).broadcast_to([P, NB, H])
                link(v.tensor_tensor(fy[:, :, :], tm[:, :, C_FF:C_FF + H], bf, ALU.add))
                v.scalar_tensor_tensor(out=fa[:, :, :], in0=fy[:, :, :], scalar=-1.0, in1=fy[:, :, :],
                                       op0=ALU.mult, op1=ALU.max).then_inc(s_fa, 1)
                v.tensor_scalar(gd[:, :, :, :].rearrange("p i h b -> p i (h b)"), tm[:, :, C_NG:C_NG + 3 * H],
                                -1.0, 80.0, ALU.mult, ALU.min).then_inc(s_gd, 1)
                for i in range(NB):
                    link(v.tensor_tensor_reduce(squares_l[:, 0:Q_LORA], tm[:, i, 0:Q_LORA], tm[:, i, 0:Q_LORA], 1.0, 0.0,
                                                ALU.mult, ALU.add, lss[:, 0, i:i + 1]))
                dve.sem_inc(s_lss, 1)
                dve.wait_ge(x_moved, layer * (16 * (KD + 1)) + 16)
                v.tensor_copy(ikd, tm[:, :, C_IK:C_IK + 32].unsqueeze(2).broadcast_to([P, NB, H, 32])).then_inc(s_ikd, 1)
                dve.wait_ge(s_fl, 1)
                v.scalar_tensor_tensor(out=fls[:, :, :], in0=fy[:, :, :], scalar=0.0, in1=fl[:, :, :],
                                       op0=ALU.min, op1=ALU.subtract).then_inc(s_fls, 1)
                dve.wait_ge(s_llr, 1)
                v.tensor_tensor(qn, tm[:, :, 0:Q_LORA], lss[:, 0, :].unsqueeze(2).broadcast_to([P, NB, Q_LORA]),
                                ALU.mult).then_inc(s_lat, 1)
                dve.wait_ge(s_ge, 1)
                link(v.tensor_scalar(gd[:, :, :, :], ge[:, :, :, :], 1.0, None, ALU.add))
                v.reciprocal(gsig[:, :, :, :], gd[:, :, :, :]).then_inc(s_gsig, 1)

            def ik(layer):
                dve.wait_ge(s_ikh, 1)
                v.tensor_tensor(ikr[1][:, :], ps[:, 4, :], ikr[0][:, :].bitcast(F32), ALU.subtract).then_inc(s_ikT, 1)

            def evac(layer, s, k0, k1):
                if s[0] == "IQ" and k1 == KD:
                    dve.wait_ge(s_evac, STEP_NO[s] + 1)
                    v.tensor_tensor(iqr[1][:, :], ps[:, BANK[s], :], iqr[0][:, :].bitcast(F32), ALU.subtract)\
                        .then_inc(s_ikT, 1)

            def blocks(layer):
                dve.wait_ge(s_evac, STEP_NO[last_of["CM"]] + 1)
                pos = par_("pos").rearrange("p (s j) -> p s j", s=2)
                for s in range(2):
                    src = bass.AP(tensor=cmp2[:, s, :].tensor, offset=cmp2[:, s, :].offset,
                                  ap=[cmp2[:, s, :].ap[0], [2, CMP_J], [CMP_STRIDE, N_CMP]])
                    v.tensor_tensor(blk[:, s], src, pos[:, s, :].unsqueeze(2).broadcast_to([P, CMP_J, N_CMP]),
                                    ALU.add).then_inc(s_blk, 1)

            def rope(x1, x2, y1, y2):
                cb, sb_ = cosv.broadcast_to([P, NB, H, 16]), sinv.broadcast_to([P, NB, H, 16])
                v.tensor_tensor(rt[0], x1, cb, ALU.mult)
                v.tensor_tensor(rt[1], x2, sb_, ALU.mult)
                v.tensor_tensor(rt[2], x1, sb_, ALU.mult)
                link(v.tensor_tensor(rt[3], x2, cb, ALU.mult))
                v.tensor_tensor(y1, rt[0], rt[1], ALU.subtract)
                v.tensor_tensor(y2, rt[2], rt[3], ALU.add).then_inc(s_rope, 1)

            def uq(layer):
                dve.wait_ge(s_uqe, NB)
                x1, x2 = q_tm[:, :, :, HD:HD + 16], q_tm[:, :, :, HD + 16:HD + 32]
                rope(x1, x2, x1, x2)
                dve.wait_ge(s_rope, 1)

            def ukv(layer):
                k1 = tm[:, :, C_KR:C_KR + 16].unsqueeze(2).broadcast_to([P, NB, H, 16])
                k2 = tm[:, :, C_KR + 16:C_KR + 32].unsqueeze(2).broadcast_to([P, NB, H, 16])
                dve.wait_ge(s_ukve, NB)
                rope(k1, k2, k_tm[:, :, :, HD:HD + 16], k_tm[:, :, :, HD + 16:HD + 32])

            def foxT(layer):
                dve.wait_ge(s_flp, 1)
                v.tensor_tensor_scan(fcum, one[0:H, :].broadcast_to([H, SEQ]), ps[0:H, 7, :], 0.0, ALU.mult,
                                     ALU.add).then_inc(s_fcum, 1)

            def fsplit(layer):
                dve.wait_ge(s_fpart, 1)
                v.tensor_tensor(f_parts[LO_ROW:LO_ROW + H, :], fcum, f_parts[0:H, :].bitcast(F32),
                                ALU.subtract).then_inc(s_fpart, 1)

            def idx(layer, i):
                w = P * (i + 1)
                for h in range(H):
                    dve.wait_ge(s_relu, H * (i - 1) + h + 1)
                    before_ = con("mask")[:, SEQ - w:SEQ] if h == 0 else work[i][:, :]
                    v.scalar_tensor_tensor(out=work[i][:, :], in0=rl[:, h, 0:w],
                                           scalar=tm[:, i, C_IW + h:C_IW + h + 1], in1=before_,
                                           op0=ALU.mult, op1=ALU.add).then_inc(s_isc, 1)
                    dve.wait_ge(s_isc, H * (i - 1) + h + 1)

            def hid(layer):
                dve.wait_ge(s_hide, 1)
                hp = ps[0:HD, 4, 0:2 * NCP].rearrange("p (s n) -> p s n", s=2)[:, :, 0:N_CMP]
                link(v.tensor_scalar(hids[:, :, 0:N_CMP], hide[:, :, 0:N_CMP], 1.0, None, ALU.add))
                link(v.reciprocal(hidr[:, :, 0:N_CMP], hids[:, :, 0:N_CMP]))
                v.tensor_tensor(hidk[:, 0:N_CMP], hp[:, 0, :], hidr[:, 0, 0:N_CMP], ALU.mult).then_inc(s_hid, 1)
                v.tensor_tensor(hidv[:, :, 0:N_CMP], hp[:, 1:2, :].broadcast_to([HD, H, N_CMP]),
                                hidr[:, 1:2, 0:N_CMP].broadcast_to([HD, H, N_CMP]), ALU.mult).then_inc(s_hid, 1)

            tops = {}

            def top(layer, r, i):
                n = len(tops)
                tops[r, i] = n
                if r:
                    dve.wait_ge(s_top, 2 * tops[r - 1, i] + 2)
                v.max(top8[:, i, :], work[i][:, :]).then_inc(s_top, 1)
                dve.wait_ge(s_top, 2 * n + 1)
                v.match_replace(work[i][:, :], top8[:, i, :], work[i][:, :], TAKEN).then_inc(s_top, 1)

            def select(layer):
                dve.wait_ge(s_top, 2 * len(tops))
                for i in range(1, NB):
                    v.tensor_scalar(selm[i][:, :], work[i][:, :], LOWEST, MASKED, ALU.is_gt,
                                    ALU.mult).then_inc(s_selm, 1)

            def csoft(layer):
                cb = con("cmpb").rearrange("p (i h n) -> p i h n", i=NB, h=H)[:, :, :, 0:N_CMP]
                pcv = pc[:, :, :, 0:N_CMP]
                for b in range(2):
                    dve.wait_ge(s_cs, b + 1)
                    css = ps[:, MISC, 256 * b:256 * b + 256].rearrange("p (i h n) -> p i h n", i=NB, h=2)
                    css = css[:, :, :, 0:N_CMP]
                    last = v.tensor_tensor(pcv[:, :, b::2, :], css, cb[:, :, b::2, :], ALU.add)
                    if b == 0:
                        link(last)
                last.then_inc(s_csum, 1)
                dve.wait_ge(s_csum, 1)
                link(v.tensor_reduce(cmx[:, :, :], pcv, AX_X, ALU.max))
                link(v.tensor_tensor(pcv, pcv, cmx[:, :, :].unsqueeze(3).broadcast_to([P, NB, H, N_CMP]), ALU.subtract))
                v.tensor_scalar(pcv, pcv, HD ** -0.5, None, ALU.mult).then_inc(s_csub, 1)

            def cmp_sums(layer):
                dve.wait_ge(s_cexp, 1)
                link(v.tensor_reduce(cden[:, :, :], pc[:, :, :, 0:N_CMP], AX_X, ALU.add))
                link(v.reciprocal(crec[:, :, :], cden[:, :, :]))
                link(v.tensor_scalar(crec[:, 0, :], crec[:, 0, :], late, None, ALU.mult))
                v.tensor_tensor(cfac[:, :, :], crec[:, :, :], gsig[:, :, :, 0], ALU.mult).then_inc(s_pc, 1)
                dve.wait_ge(s_pc, 1)

            def cmp_out(layer, half):
                dve.wait_ge(s_cpv, half + 1)
                for i in (2 * half, 2 * half + 1):
                    o = heads_of(ps[:, MISC, (i % 2) * GW:(i % 2) * GW + GW])
                    fac = cfac[:, i].unsqueeze(2).broadcast_to([P, H, HD])
                    last = v.tensor_tensor(heads_of(o_sb[:, i, 3 * GW:4 * GW]), o, fac, ALU.mult)
                last.then_inc(s_co, 1)

            def normalise(g):
                m, i, _ = UNITS[H * g]
                c = slice(H * g, H * g + H)
                dve.wait_ge(s_pv, H * (g + 1))
                link(v.reciprocal(rinv[:, c], rsum[:, c]))
                fac = rinv[:, c]
                if m in ("sel", "win"):
                    link(v.tensor_tensor(rfac[:, c], rinv[:, c], gsig[:, i, :, 1 if m == "sel" else 2], ALU.mult))
                    fac = rfac[:, c]
                o = heads_of(ps[:, 6 + g % 2, 0:GW])
                dst = o_sb[:, i, OUT_COL[m]:OUT_COL[m] + GW]
                fac = fac.unsqueeze(2).broadcast_to([P, H, HD])
                if m in ("sel", "win"):
                    link(v.tensor_tensor(otmp, o, fac, ALU.mult))
                    v.tensor_tensor(heads_of(dst), heads_of(dst), otmp, ALU.add).then_inc(s_norm, 1)
                else:
                    v.tensor_tensor(heads_of(dst), o, fac, ALU.mult).then_inc(s_norm, 1)

            def unit(layer, t):
                if t < NUN:
                    m, i, h = UNITS[t]
                    w = P * (i + 1)
                    bias = {"mla": con("mask")[:, SEQ - w:SEQ], "fox": fb[:, h, 0:w]}.get(m, alibi[:, h, SEQ - w:SEQ])
                    dve.wait_ge(s_sc, t + 1)
                    if m == "fox" and i == 0:
                        dve.wait_ge(s_fb, h + 1)
                    if t >= 3:
                        dve.wait_ge(s_tr, t - 2)
                    scale = QK_W ** -0.5 if m == "mla" else HD ** -0.5
                    v.tensor_tensor_reduce(pr_[t % 3][:, 0:w], ps[:, 2 + t % 2, 0:w], bias, -scale, 3e38,
                                           ALU.add, ALU.min, nmx[:, t:t + 1]).then_inc(s_ttr, 1)
                u = t - 2
                if 0 <= u < NUN and u % 2 == 1:
                    w = P * (UNITS[u][1] + 1)
                    dve.wait_ge(s_tr, u + 1)
                    if u >= 2:
                        dve.wait_ge(s_pv, u - 1)
                    v.tensor_copy(pt[1][:, 0:w], ps[:, 5, 0:w]).then_inc(s_ptd, 1)
                if t >= 6 and (t - 2) % H == 0:
                    normalise((t - 2) // H - 1)

            silus = []

            def silu(layer, g):
                silus.append(g)
                dve.wait_ge(s_sig, len(silus))
                z = sz[:, :, GW * g:GW * g + GW]
                v.tensor_tensor(z, z, ez_of[g], ALU.mult).then_inc(s_silu, 1)

            grs_order = [0, 1, 3, 2]

            def gn(layer, m):
                dve.wait_ge(s_grs, grs_order.index(m) + 1)
                dve.wait_ge(s_silu, silus.index(m) + 1)
                for i in range(NB):
                    o = o_sb[:, i, GW * m:GW * m + GW]
                    last = v.scalar_tensor_tensor(out=o, in0=o, scalar=grs[:, m, i:i + 1],
                                                  in1=sz[:, i, GW * m:GW * m + GW], op0=ALU.mult, op1=ALU.mult)
                last.then_inc(s_y, 1)

            def ada_tiles(w, n, tiles, wait):
                dst = acc[:, n % 2, :]
                for k in tiles:
                    if k == 0:
                        last = v.tensor_scalar(dst, w[:, k, :], sc[:, k:k + 1], None, ALU.mult)
                    else:
                        last = v.scalar_tensor_tensor(out=dst, in0=w[:, k, :], scalar=sc[:, k:k + 1], in1=dst,
                                                      op0=ALU.mult, op1=ALU.add)
                    wait(last, k)

            def ada(layer, n, c):
                if c == 0:
                    wait_raw(dve, layer, ("ada", n))
                    if n >= 2:
                        dve.wait_ge(s_adap, n - 1)
                u = ("ada", n)

                def wait(last, k):
                    if k == KD - 1:
                        last.then_inc(w_ada, 1)
                        dve.wait_ge(w_ada, layer * (N_GATE + N_SS) + N_SS + n + 1)
                        dve.sem_inc(s_acc, 1)
                    else:
                        link(last)
                ada_tiles(raw(u).rearrange("p (k c) -> p k c", k=KD), n, (2 * c, 2 * c + 1), wait)

            def adasum(layer, n):
                dve.wait_ge(s_adap, n + 1)
                c = 2 * KD + 2 * n if n < N_GATE else 2 * (n - N_GATE)
                b = par_("b_gate")[:, 2 * n:2 * n + 2] if n < N_GATE else par_("b_next")[:, c:c + 2]
                v.tensor_tensor(mod[:, c:c + 2], ps[:, MISC, 0:2], b, ALU.add).then_inc(s_mod, 1)
                if n == N_GATE + N_SS - 1:
                    dve.wait_ge(s_mod, n + 1)
                    link(v.scalar_tensor_tensor(out=gs[:, :], in0=mod[:, KD:2 * KD], scalar=1.0, in1=par_("rms_next"),
                                                op0=ALU.add, op1=ALU.mult))

            def yT(layer, k):
                j = CT_ORDER.index(k)
                dve.wait_ge(s_oThi, j + 1)
                v.scalar_tensor_tensor(out=h_lo[:, k, :], in0=ps[:, 2 + j % 2, :], scalar=par_("out_g")[:, k:k + 1],
                                       in1=h_hi[:, k, :].bitcast(F32), op0=ALU.mult, op1=ALU.subtract).then_inc(s_oT, 1)

            def x(layer, k):
                if k % 2 == 0:
                    dve.wait_ge(s_out, k // 2 + 1)
                else:
                    wait_done(dve, layer, NSP - 4 + k // 2)
                if k == KD - 1:
                    for n, s in enumerate((s_xh, s_x)):
                        c = slice(HALF * n, HALF * n + HALF)
                        v.scalar_tensor_tensor(out=xT[:, k, c], in0=ps[:, k % 4, c],
                                               scalar=mod[:, 2 * KD + k:2 * KD + k + 1], in1=xT[:, k, c],
                                               op0=ALU.mult, op1=ALU.add).then_inc(s, 1)
                    return
                if k == 0:
                    dve.wait_ge(x_moved, layer * (16 * (KD + 1)) + 32)
                v.scalar_tensor_tensor(out=xT[:, k, :], in0=ps[:, k % 4, :], scalar=mod[:, 2 * KD + k:2 * KD + k + 1],
                                       in1=xT[:, k, :], op0=ALU.mult, op1=ALU.add).then_inc(s_x, 1)

            do = {"norm": norm, "first": casts, "proj": evac, "latr": latr, "blk": blocks, "ik": ik,
                  "uq": uq, "ukv": ukv, "foxT": foxT, "fsplit": fsplit, "idx": idx,
                  "hid": hid, "top": top, "selm": select, "csoft": csoft, "cden": cmp_sums, "cval": cmp_out,
                  "unit": unit, "silu": silu, "gn": gn, "ada": ada, "adasum": adasum, "yT": yT, "x": x}

            dve.wait_ge(first_loaded, 16)
            def first_mod(n):
                dve.wait_ge(setup_pe, n + 1)
                v.tensor_tensor(mod[:, 2 * n:2 * n + 2].unsqueeze(2), first_sums(n),
                                fst("b_first")[:, 2 * n:2 * n + 2].unsqueeze(2), ALU.add).then_inc(setup_dve, 1)

            for t in (hidv, pc, vcd):
                v.memset(t[...], 0.0).then_inc(setup_fill, 1)
            dve.wait_ge(setup_act, 1)
            v.tensor_scalar(sct[:, :], sct[:, :], 1.0, None, ALU.add).then_inc(setup_sum, 1)
            dve.wait_ge(setup_sum, 1)
            v.reciprocal(sct[:, :], sct[:, :]).then_inc(setup_sum, 1)
            dve.wait_ge(setup_sum, 2)
            v.tensor_tensor(sc[:, :], sct[:, :], fst("c"), ALU.mult).then_inc(setup_dve, 1)
            dve.wait_ge(setup_dve, 1)
            count = [2]
            for n in range(N_SS):
                dve.wait_ge(w_loaded[(n + 1) % RING], 16 * ((n + 1) // RING + 1))
                if n >= 2:
                    dve.wait_ge(setup_pe, n - 1)

                def wait(last, k):
                    if k == DVE_TILES - 1:
                        last.then_inc(w_ada, 1)
                    else:
                        count[0] += 1
                        last.then_inc(setup_sum, 1)
                        dve.wait_ge(setup_sum, count[0])
                ada_tiles(ring[(n + 1) % RING][:, 0:SLOT].rearrange("p (k c) -> p k c", k=KD), n, range(DVE_TILES), wait)
                if n:
                    first_mod(n - 1)
            first_mod(N_SS - 1)
            dve.wait_ge(setup_dve, 1 + N_SS)
            v.scalar_tensor_tensor(out=gs[:, :], in0=mod[:, KD:2 * KD], scalar=1.0, in1=fst("rms_first"),
                                   op0=ALU.add, op1=ALU.mult).then_inc(setup_dve, 1)
            dve.wait_ge(setup_dve, SETUP_DVE)
            dve.wait_ge(setup_fill, 3)
            dve.wait_ge(setup_act, KD + 3)
            with dve.Fori(0, DEPTH) as layer:
                link = linker(dve, d_link)
                for kind, *args in MAIN:
                    if kind in do:
                        do[kind](layer, *args)
                dve.wait_ge(s_x, KD)
                dve.sem_inc(arrived, 1)
                dve.wait_ge(go, layer + 1)
            for k in range(KD):
                if k in FIN_POOL:
                    continue
                v.scalar_tensor_tensor(out=xT[:, k, :], in0=xT[:, k, :], scalar=fst("fin_g")[:, k:k + 1], in1=rb[:, :],
                                       op0=ALU.mult, op1=ALU.mult).then_inc(fin_out, 1)

        @block.gpsimd
        def _(pool):
            g = nc.gpsimd

            def split(layer, c, p, src=None):
                pool.wait_ge(s_hi, layer * (PIECES * NSP) + PIECES * c + p + 1)
                src = raw(("split", c)) if src is None else src
                g.tensor_tensor(piece(c, p, w_lo[c % 2]), piece(c, p, src),
                                piece(c, p, w_hi[c % 2]).bitcast(F32), ALU.subtract).then_inc(s_lo, 1)

            def x(layer, k):
                if 1 <= k < KD - 1:
                    pool.wait_ge(s_sq, k + 1)
                    if k > 1:
                        pool.wait_ge(s_sqa, k - 1)
                    g.tensor_tensor(sqa[:, :], sqa[:, :], sqr[k % 2][:, :], ALU.add).then_inc(s_sqa, 1)

            for p in range(PIECES):
                split(0, 0, p, ring[0][:, :])
            for k in range(1, KD):
                pool.wait_ge(setup_act, k + 2)
                if k > 1:
                    pool.wait_ge(setup_sq, k - 1)
                g.tensor_tensor(xg[:, 0, :], xg[:, 0, :], xg[:, k, :], ALU.add).then_inc(setup_sq, 1)
            with pool.Fori(0, DEPTH) as layer:
                for kind, *args in MAIN:
                    if kind == "split":
                        split(layer, *args)
                    elif kind == "x":
                        x(layer, *args)
                pool.wait_ge(arrived, 4)
                pool.sem_clear(range(nums[0], nums[0] + len(nums)))
                pool.sem_inc(go, 1)
            for n, k in enumerate(FIN_POOL):
                pool.wait_ge(fin_act, n + 1)
                g.tensor_tensor(xT[:, k, :], xT[:, k, :], rb[:, :], ALU.mult).then_inc(fin_pool, 1)
def _constants():
    f = np.float32
    out = np.zeros((P, CO_W), f)

    def put(name, a):
        a = np.asarray(a, f)
        out[:a.shape[0], CO[name][0]:CO[name][1]] = a.reshape(a.shape[0], -1)

    p = np.arange(P)
    slopes = (2.0 ** (-8.0 * (np.arange(H) + 1) / H)).astype(f)
    c = np.arange(SEQ) - (SEQ - P)
    mask = np.where(c[None, :] <= p[:, None], 0.0, MASKED)
    put("ident", np.eye(P))
    put("mask", mask)
    put("alibi", slopes[None, :, None] * (HD ** 0.5 * c)[None, None, :] + mask[:, None, :])
    t = np.arange(SEQ).reshape(NB, P).T
    end = np.arange(NCP) * CMP_STRIDE + CMP_LEN - 1
    cmpb = slopes[None, None, :, None] * (HD ** 0.5 * end) + np.zeros((P, NB, 1, 1))
    put("cmpb", np.where(end <= t[:, :, None, None], cmpb, MASKED))
    inv = f(10000.0) ** (-np.arange(16, dtype=f) / f(16))
    ang = t[:, :, None].astype(f) * inv.astype(f)
    put("cos", np.cos(ang))
    put("sin", np.sin(ang))
    sel = np.zeros((LO_ROW + H, H, P))
    sel[:H] = sel[LO_ROW:] = (np.eye(H) * -(HD ** 0.5))[:, :, None]
    put("selrow", sel)
    return out


def _rows(w):
    return w.reshape(w.shape[0], -1, P, w.shape[-1]).transpose(0, 2, 1, 3)


def kernel(x, c, rms_g, w_ada, b_ada, w_in, mla_q_norm, mla_w_uq, mla_kv_norm, mla_w_ukv, fox_b_f,
           nsa_cmp_pos, nsa_cmp_w1, nsa_cmp_w2, out_norm_g, w_out, final_g):
    import concourse.bacc as bacc
    from concourse.bass_utils import run_bass_kernel_spmd

    (x, c, rms_g, w_ada, b_ada, w_in, mla_q_norm, mla_w_uq, mla_kv_norm, mla_w_ukv, fox_b_f, nsa_cmp_pos,
     nsa_cmp_w1, nsa_cmp_w2, out_norm_g, w_out, final_g) = (
        np.asarray(a) for a in (x, c, rms_g, w_ada, b_ada, w_in, mla_q_norm, mla_w_uq, mla_kv_norm, mla_w_ukv,
                                fox_b_f, nsa_cmp_pos, nsa_cmp_w1, nsa_cmp_w2, out_norm_g, w_out, final_g))
    widths = [("q_lat", 192), ("kv_lat", 128), ("k_rope", 32), ("fox_q", 256), ("fox_k", 256), ("fox_v", 256),
              ("fox_f", 4), ("dsa_q", 256), ("dsa_k", 256), ("dsa_v", 256), ("idx_q", 128), ("idx_k", 32),
              ("idx_w", 4), ("nsa_q", 256), ("k_cmp", 64), ("v_cmp", 64), ("k_sel", 64), ("v_sel", 64),
              ("k_win", 64), ("v_win", 64), ("nsa_gate", 12), ("gate_z", 1024)]
    rows, seg, at = _rows(w_in), {}, 0
    for name, w in widths:
        seg[name] = rows[..., at:at + w]
        at += w

    w_gate_z, ada, w_o = seg["gate_z"], _rows(w_ada), _rows(w_out)
    unit_segments = {"A1": ("q_lat", "idx_k", "idx_w", "fox_f", "nsa_gate", "k_rope"), "A2": ("kv_lat",),
                     "IQ": ("idx_q",), "CM": ("k_cmp", "v_cmp"), "FQ": ("fox_q",), "FK": ("fox_k",),
                     "FV": ("fox_v",), "NQ": ("nsa_q",), "SW": ("k_sel", "k_win", "v_sel", "v_win"),
                     "DQ": ("dsa_q",), "DK": ("dsa_k",), "DV": ("dsa_v",)}
    w_uq = np.zeros((DEPTH, 2 * P, H * QK_W), np.float32)
    w_uq[:, :Q_LORA] = mla_w_uq
    uq = _rows(w_uq)
    cmpw = nsa_cmp_w1.reshape(DEPTH, 2, CMP_J, P, HD).transpose(0, 3, 1, 2, 4)

    def split_unit(name, l):
        if name[0] == "G":
            g = int(name[2])
            return w_gate_z[l, ..., GW * g:GW * g + GW]
        if name[0] == "O":
            n = int(name[1])
            return w_o[l, ..., 256 * n:256 * n + 256]
        return np.concatenate([seg[n][l] for n in unit_segments[name]], axis=-1)

    def loaded_unit(kind, n, l):
        nxt = (l + 1) % DEPTH
        if kind == "split":
            return split_unit(SPLIT_NAMES[n % NSP], l if n < NSP else nxt)
        if kind == "ada":
            of, at = (l, 2 * D + 256 * n) if n < N_GATE else (nxt, 256 * (n - N_GATE))
            return ada[of, ..., at:at + 256]
        return {"uq": uq[l], "ukv": mla_w_ukv[l], "cmpk": cmpw[l, :, 0], "cmpv": cmpw[l, :, 1]}[kind]

    w_all = np.stack([np.concatenate([loaded_unit(kind, n, l).reshape(P, -1) for kind, n in RING_UNITS], axis=-1)
                      for l in range(DEPTH)])
    w_first = np.concatenate([ada[0, ..., 256 * n:256 * n + 256].reshape(P, -1) for n in range(N_SS)]
                             + [split_unit("A1", 0).reshape(P, -1)], axis=-1)

    def cols(a):
        return np.swapaxes(a.reshape(*a.shape[:-1], -1, P), -1, -2)

    par = np.zeros((DEPTH, P, PR_W), np.float32)

    def put(name, a):
        par[:, :a.shape[1], PR[name][0]:PR[name][1]] = a

    b_cols, rms_cols = cols(b_ada), cols(rms_g)
    put("b_gate", b_cols[..., 2 * KD:])
    put("b_next", np.roll(b_cols[..., :2 * KD], -1, axis=0))
    put("rms_next", np.roll(rms_cols, -1, axis=0))
    put("out_g", cols(out_norm_g))
    qg = np.zeros((DEPTH, 2 * P), np.float32)
    qg[:, :Q_LORA] = mla_q_norm
    put("q_g", cols(qg))
    put("kv_g", mla_kv_norm[:, :, None])
    put("b_f", np.broadcast_to(fox_b_f[:, None, :], (DEPTH, P, H)))
    put("pos", nsa_cmp_pos.reshape(DEPTH, 2, CMP_J, P).transpose(0, 3, 1, 2).reshape(DEPTH, P, -1))
    put("w2k", np.concatenate([nsa_cmp_w2[:, 0]] * 2, axis=-1))
    put("w2v", nsa_cmp_w2[:, 1])

    first = np.zeros((P, P0_W), np.float32)
    late = np.arange(P)[:, None] >= CMP_LEN - 1
    for name, a in (("b_first", b_cols[0, :, :2 * KD]), ("rms_first", rms_cols[0]), ("fin_g", cols(final_g)),
                    ("c", cols(c[0])), ("mean", 1.0 / D), ("one", 1.0), ("eps", EPS), ("late", late)):
        first[:, P0[name][0]:P0[name][1]] = a

    arrays = {
        "x_t": x[0].T.reshape(KD, P, SEQ).transpose(1, 0, 2),
        "first": first, "w_first": w_first, "w_all": w_all, "par": par, "const": _constants(),
    }
    arrays = {k: np.ascontiguousarray(v) for k, v in arrays.items()}
    nc = bacc.Bacc("TRN2", target_bir_lowering=False, num_devices=1, dynamic_dma_scratch_size=1024)
    aps = [nc.dram_tensor(k, v.shape, mybir.dt.from_np(v.dtype), kind="ExternalInput").ap() for k, v in arrays.items()]
    y_t = nc.dram_tensor("y_t", (P, KD, SEQ), F32, kind="ExternalOutput").ap()
    program(nc, *aps, y_t)
    r = run_bass_kernel_spmd(nc, [arrays], core_ids=[0])
    y = np.asarray(r.results[0]["y_t"])
    return np.ascontiguousarray(y.transpose(1, 0, 2).reshape(D, SEQ).T)[None]
```
